# Optimizing a Trainium2 kernel written in Bass

```python
import jax, jax.numpy as jnp
from jax import lax
import numpy as np

D_MODEL = 1024
BATCH = 1
SEQ = 512
DEPTH = 2

GRID_W = 64
CTX_LEN = 256
HEAD_DIM = 64
A_HEADS = 8
A_KV_HEADS = 2
B_HEADS = 8
Q_BLOCK = 128
NA_ROWS_MAX = 8
NA_COLS = 16
ROPE_THETA = 10000.0
GLA_HEADS = 4
GLA_DK = D_MODEL // 2
GLA_DV = D_MODEL
GLA_GATE_RANK = 16
GLA_GATE_NORM = 16.0
GLA_CHUNK = 64
N_EXPERTS = 16
EC_CAPACITY = 2
EXPERT_FF = 1024
N_EVEN = (DEPTH + 1) // 2
N_ODD = DEPTH // 2
ATTN_SIZES = (A_HEADS * HEAD_DIM, A_KV_HEADS * HEAD_DIM, A_KV_HEADS * HEAD_DIM, B_HEADS * HEAD_DIM, B_HEADS * HEAD_DIM, B_HEADS * HEAD_DIM)
ATTN_HEADS = (A_HEADS, A_KV_HEADS, A_KV_HEADS, B_HEADS, B_HEADS, B_HEADS)
ATTN_IN = A_HEADS * HEAD_DIM + 2 * A_KV_HEADS * HEAD_DIM + 3 * B_HEADS * HEAD_DIM
ATTN_MIX = (A_HEADS + B_HEADS) * HEAD_DIM
GLA_SIZES = (GLA_DK, GLA_DK, GLA_DV, GLA_DV, GLA_GATE_RANK, GLA_GATE_RANK)
GLA_IN = 2 * GLA_DK + 2 * GLA_DV + 2 * GLA_GATE_RANK
EPS = 1e-6

kernel_name = 'hybrid_gqa_natten_gla_ecmoe_prefix'

def rms_norm(x, g):
    xf = x.astype(jnp.float32)
    y = xf * lax.rsqrt(jnp.mean(xf * xf, axis=-1, keepdims=True) + EPS)
    return (y * g.astype(jnp.float32)).astype(x.dtype)

def split_cols(p, sizes):
    out, start = [], 0
    for s in sizes:
        out.append(p[..., start:start + s])
        start += s
    return out

def to_heads(a, n):
    return a.reshape(a.shape[:-1] + (n, a.shape[-1] // n))

def axial_rope_tables(n):
    half = HEAD_DIM // 2
    t = jnp.arange(n, dtype=jnp.int32)
    inv = ROPE_THETA ** (-jnp.arange(0, half, 2, dtype=jnp.float32) / half)
    def tab(pos):
        ang = pos.astype(jnp.float32)[:, None] * inv[None, :]
        ang = jnp.concatenate([ang, ang], axis=-1)
        return jnp.cos(ang)[:, None, :], jnp.sin(ang)[:, None, :]
    cos_r, sin_r = tab(t // GRID_W)
    cos_c, sin_c = tab(t % GRID_W)
    return cos_r, sin_r, cos_c, sin_c

def apply_axial_rope(x, tables):
    cos_r, sin_r, cos_c, sin_c = tables
    half = x.shape[-1] // 2
    def rot(u, cos, sin):
        u1, u2 = jnp.split(u, 2, axis=-1)
        return u * cos + jnp.concatenate([-u2, u1], axis=-1) * sin
    xf = x.astype(jnp.float32)
    y = jnp.concatenate([rot(xf[..., :half], cos_r, sin_r), rot(xf[..., half:], cos_c, sin_c)], axis=-1)
    return y.astype(x.dtype)

def gqa_softmax(q, k, v):
    b, t, hq, dh = q.shape
    hk = k.shape[2]
    qg = q.reshape(b, t, hk, hq // hk, dh)
    s = jnp.einsum('btkgd,bskd->bkgts', qg, k).astype(jnp.float32) * (dh ** -0.5)
    p = jax.nn.softmax(s, axis=-1).astype(v.dtype)
    o = jnp.einsum('bkgts,bskd->btkgd', p, v)
    return o.reshape(b, t, hq, dh)

def neighbourhood_attention(q, k, v, k_ctx, v_ctx, rpb):
    b, n, h, dh = q.shape
    rows = n // GRID_W
    wr = min(NA_ROWS_MAX, rows)
    wc = NA_COLS
    qg = q.reshape(b, rows, GRID_W, h, dh)
    kg = k.reshape(b, rows, GRID_W, h, dh)
    vg = v.reshape(b, rows, GRID_W, h, dh)
    col = np.arange(GRID_W)
    col_idx = np.clip(col - wc // 2, 0, GRID_W - wc)[:, None] + np.arange(wc)[None, :]
    dc_idx = col_idx - col[:, None] + (NA_COLS - 1)
    scale = dh ** -0.5
    def row_block(args):
        r, q_r = args
        rs = jnp.clip(r - wr // 2, 0, rows - wr)
        k_win = lax.dynamic_slice_in_dim(kg, rs, wr, axis=1)[:, :, col_idx]
        v_win = lax.dynamic_slice_in_dim(vg, rs, wr, axis=1)[:, :, col_idx]
        dr_idx = rs + jnp.arange(wr) - r + (NA_ROWS_MAX - 1)
        bias = rpb[:, dr_idx[:, None, None], dc_idx[None, :, :]].transpose(0, 2, 1, 3)
        s_win = jnp.einsum('bwhd,biwjhd->bhwij', q_r, k_win).astype(jnp.float32) * scale + bias.astype(jnp.float32)
        s_ctx = jnp.einsum('bwhd,blhd->bhwl', q_r, k_ctx).astype(jnp.float32) * scale
        s = jnp.concatenate([s_win.reshape(b, h, GRID_W, wr * wc), s_ctx], axis=-1)
        p = jax.nn.softmax(s, axis=-1).astype(v.dtype)
        p_win = p[..., :wr * wc].reshape(b, h, GRID_W, wr, wc)
        p_ctx = p[..., wr * wc:]
        return jnp.einsum('bhwij,biwjhd->bwhd', p_win, v_win) + jnp.einsum('bhwl,blhd->bwhd', p_ctx, v_ctx)
    out = lax.map(row_block, (jnp.arange(rows, dtype=jnp.int32), qg.transpose(1, 0, 2, 3, 4)))
    return out.transpose(1, 0, 2, 3, 4).reshape(b, n, h, dh)

def attn_mixer(u, uc, w_in, w_out, qa_g, ka_g, qb_g, kb_g, rpb, rope, need_ctx_out):
    def project(hh):
        qa, ka, va, qb, kb, vb = [to_heads(p, nh) for p, nh in zip(split_cols(hh @ w_in, ATTN_SIZES), ATTN_HEADS)]
        return rms_norm(qa, qa_g), rms_norm(ka, ka_g), va, rms_norm(qb, qb_g), rms_norm(kb, kb_g), vb
    qa, ka, va, qb, kb, vb = project(u)
    cqa, cka, cva, cqb, ckb, cvb = project(uc)
    qa = apply_axial_rope(qa, rope)
    ka = apply_axial_rope(ka, rope)
    b, n = u.shape[0], u.shape[1]
    k_all = jnp.concatenate([ka, cka], axis=1)
    v_all = jnp.concatenate([va, cva], axis=1)
    q_blocks = qa.reshape(b, n // Q_BLOCK, Q_BLOCK, A_HEADS, HEAD_DIM).transpose(1, 0, 2, 3, 4)
    oa = lax.map(lambda qi: gqa_softmax(qi, k_all, v_all), q_blocks)
    oa = oa.transpose(1, 0, 2, 3, 4).reshape(b, n, A_HEADS * HEAD_DIM)
    ob = neighbourhood_attention(qb, kb, vb, ckb, cvb, rpb).reshape(b, n, B_HEADS * HEAD_DIM)
    y = jnp.concatenate([oa, ob], axis=-1) @ w_out
    yc = None
    if need_ctx_out:
        l = uc.shape[1]
        coa = gqa_softmax(cqa, cka, cva).reshape(b, l, A_HEADS * HEAD_DIM)
        cob = gqa_softmax(cqb, ckb, cvb).reshape(b, l, B_HEADS * HEAD_DIM)
        yc = jnp.concatenate([coa, cob], axis=-1) @ w_out
    return y, yc

def gla_chunked(q, k, v, g, s0):
    b, t, h, dk = q.shape
    dv = v.shape[-1]
    n = t // GLA_CHUNK
    def chunks(a):
        return a.astype(jnp.float32).reshape(b, n, GLA_CHUNK, h, a.shape[-1]).transpose(1, 0, 3, 2, 4)
    qc = chunks(q) * (dk ** -0.5)
    kc, vc, gc = chunks(k), chunks(v), chunks(g)
    cum = jnp.cumsum(gc, axis=3)
    cum_last = cum[:, :, :, -1:, :]
    q_dec = qc * jnp.exp(cum)
    k_inv = kc * jnp.exp(-cum)
    k_state = kc * jnp.exp(cum_last - cum)
    mask = jnp.tril(jnp.ones((GLA_CHUNK, GLA_CHUNK), dtype=bool))
    a_intra = jnp.where(mask, jnp.einsum('nbhid,nbhjd->nbhij', q_dec, k_inv), 0.0)
    o_intra = jnp.einsum('nbhij,nbhje->nbhie', a_intra, vc)
    def step(s, xs):
        q_d, k_s, v_c, c_last = xs
        o_inter = jnp.einsum('bhid,bhde->bhie', q_d, s)
        s = s * jnp.swapaxes(jnp.exp(c_last), -1, -2) + jnp.einsum('bhjd,bhje->bhde', k_s, v_c)
        return s, o_inter
    s_fin, o_inter = lax.scan(step, s0, (q_dec, k_state, vc, cum_last))
    o = (o_intra + o_inter).transpose(1, 0, 3, 2, 4).reshape(b, t, h, dv)
    return o.astype(v.dtype), s_fin

def gla_final_state(k, v, g):
    cum = jnp.cumsum(g.astype(jnp.float32), axis=1)
    kd = k.astype(jnp.float32) * jnp.exp(cum[:, -1:] - cum)
    return jnp.einsum('bthd,bthe->bhde', kd, v.astype(jnp.float32))

def gla_mixer(u, uc, w_in, gk_w_f, gk_b_f, gk_w_b, gk_b_b, onorm_g, w_out, need_ctx_out):
    def project(hh):
        q, k, v, og, zf, zb = split_cols(hh @ w_in, GLA_SIZES)
        gf = jax.nn.log_sigmoid((zf @ gk_w_f + gk_b_f).astype(jnp.float32)) / GLA_GATE_NORM
        gb = jax.nn.log_sigmoid((zb @ gk_w_b + gk_b_b).astype(jnp.float32)) / GLA_GATE_NORM
        return (to_heads(q, GLA_HEADS), to_heads(k, GLA_HEADS), to_heads(v, GLA_HEADS), og,
                to_heads(gf, GLA_HEADS), to_heads(gb, GLA_HEADS))
    def merge(o_f, o_b, og):
        o = rms_norm(o_f + o_b, onorm_g)
        o = o.reshape(o.shape[:2] + (GLA_DV,)) * jax.nn.silu(og)
        return o @ w_out
    flip = lambda a: a[:, ::-1]
    cq, ck, cv, cog, cgf, cgb = project(uc)
    q, k, v, og, gf, gb = project(u)
    b = u.shape[0]
    yc = None
    if need_ctx_out:
        s0 = jnp.zeros((b, GLA_HEADS, GLA_DK // GLA_HEADS, GLA_DV // GLA_HEADS), jnp.float32)
        co_f, s_f = gla_chunked(cq, ck, cv, cgf, s0)
        co_b, s_b = gla_chunked(flip(cq), flip(ck), flip(cv), flip(cgb), s0)
        yc = merge(co_f, flip(co_b), cog)
    else:
        s_f = gla_final_state(ck, cv, cgf)
        s_b = gla_final_state(flip(ck), flip(cv), flip(cgb))
    o_f, _ = gla_chunked(q, k, v, gf, s_f)
    o_b, _ = gla_chunked(flip(q), flip(k), flip(v), flip(gb), s_b)
    return merge(o_f, flip(o_b), og), yc

def expert_choice_ffn(hh, w_router, w_gate, w_up, w_down):
    b, n, d = hh.shape
    cap = EC_CAPACITY * n // N_EXPERTS
    aff = jax.nn.softmax((hh @ w_router).astype(jnp.float32), axis=-1)
    gate, idx = lax.top_k(aff.transpose(0, 2, 1), cap)
    xg = jax.vmap(lambda hb, ib: hb[ib])(hh, idx)
    a = jnp.einsum('becd,edf->becf', xg, w_gate)
    up = jnp.einsum('becd,edf->becf', xg, w_up)
    y = jnp.einsum('becf,efd->becd', jax.nn.silu(a) * up, w_down) * gate[..., None].astype(hh.dtype)
    return jax.vmap(lambda yb, ib: jnp.zeros((n, d), hh.dtype).at[ib.reshape(-1)].add(yb.reshape(-1, d)))(y, idx)

def setup_inputs(seed: int = 0):
    key = jax.random.key(seed)
    ks = jax.random.split(key, 26)
    f32 = jnp.float32
    def w(k, shape, fan_in, g=1.0):
        return jax.random.normal(k, shape, f32) * (g * fan_in ** -0.5)
    def gain(k, shape):
        return 1.0 + 0.02 * jax.random.normal(k, shape, f32)
    def small(k, shape, s):
        return s * jax.random.normal(k, shape, f32)
    return {
        'x': jax.random.normal(ks[0], (BATCH, SEQ, D_MODEL), f32),
        'c': jax.random.normal(ks[1], (BATCH, D_MODEL), f32),
        'ctx': jax.random.normal(ks[2], (BATCH, CTX_LEN, D_MODEL), f32),
        'c_ctx': jax.random.normal(ks[3], (D_MODEL,), f32),
        'ada_w': w(ks[4], (DEPTH, D_MODEL, 6 * D_MODEL), D_MODEL, 0.5),
        'ada_b': small(ks[5], (DEPTH, 6 * D_MODEL), 0.02),
        'norm1_g': gain(ks[6], (DEPTH, D_MODEL)),
        'norm2_g': gain(ks[7], (DEPTH, D_MODEL)),
        'attn_w_in': w(ks[8], (N_EVEN, D_MODEL, ATTN_IN), D_MODEL),
        'attn_w_out': w(ks[9], (N_EVEN, ATTN_MIX, D_MODEL), ATTN_MIX),
        'a_q_norm': gain(ks[10], (N_EVEN, HEAD_DIM)),
        'a_k_norm': gain(ks[11], (N_EVEN, HEAD_DIM)),
        'b_q_norm': gain(ks[12], (N_EVEN, HEAD_DIM)),
        'b_k_norm': gain(ks[13], (N_EVEN, HEAD_DIM)),
        'na_rpb': small(ks[14], (N_EVEN, B_HEADS, 2 * NA_ROWS_MAX - 1, 2 * NA_COLS - 1), 0.1),
        'gla_w_in': w(ks[15], (N_ODD, D_MODEL, GLA_IN), D_MODEL),
        'gla_gk_w_f': w(ks[16], (N_ODD, GLA_GATE_RANK, GLA_DK), GLA_GATE_RANK),
        'gla_gk_b_f': small(ks[17], (N_ODD, GLA_DK), 0.1),
        'gla_gk_w_b': w(ks[18], (N_ODD, GLA_GATE_RANK, GLA_DK), GLA_GATE_RANK),
        'gla_gk_b_b': small(ks[19], (N_ODD, GLA_DK), 0.1),
        'gla_o_norm': gain(ks[20], (N_ODD, GLA_DV // GLA_HEADS)),
        'gla_w_out': w(ks[21], (N_ODD, GLA_DV, D_MODEL), GLA_DV),
        'moe_router': w(ks[22], (DEPTH, D_MODEL, N_EXPERTS), D_MODEL),
        'moe_w_gate': w(ks[23], (DEPTH, N_EXPERTS, D_MODEL, EXPERT_FF), D_MODEL),
        'moe_w_up': w(ks[24], (DEPTH, N_EXPERTS, D_MODEL, EXPERT_FF), D_MODEL),
        'moe_w_down': w(ks[25], (DEPTH, N_EXPERTS, EXPERT_FF, D_MODEL), EXPERT_FF),
    }

def reference(x, c, ctx, c_ctx, ada_w, ada_b, norm1_g, norm2_g, attn_w_in, attn_w_out,
              a_q_norm, a_k_norm, b_q_norm, b_k_norm, na_rpb, gla_w_in, gla_gk_w_f, gla_gk_b_f,
              gla_gk_w_b, gla_gk_b_b, gla_o_norm, gla_w_out, moe_router, moe_w_gate, moe_w_up, moe_w_down):
    n = x.shape[1]
    rope = axial_rope_tables(n)
    s_lat = jax.nn.silu(c)
    s_ctx = jax.nn.silu(c_ctx)[None, :]
    h, hc = x, ctx
    for layer in range(DEPTH):
        last = layer == DEPTH - 1
        i = layer // 2
        m = jnp.split((s_lat @ ada_w[layer] + ada_b[layer])[:, None, :], 6, axis=-1)
        mc = jnp.split((s_ctx @ ada_w[layer] + ada_b[layer])[:, None, :], 6, axis=-1)
        u = rms_norm(h, norm1_g[layer]) * (1 + m[1]) + m[0]
        uc = rms_norm(hc, norm1_g[layer]) * (1 + mc[1]) + mc[0]
        if layer % 2 == 0:
            y, yc = attn_mixer(u, uc, attn_w_in[i], attn_w_out[i], a_q_norm[i], a_k_norm[i],
                               b_q_norm[i], b_k_norm[i], na_rpb[i], rope, not last)
        else:
            y, yc = gla_mixer(u, uc, gla_w_in[i], gla_gk_w_f[i], gla_gk_b_f[i], gla_gk_w_b[i],
                              gla_gk_b_b[i], gla_o_norm[i], gla_w_out[i], not last)
        h = h + m[2] * y
        u = rms_norm(h, norm2_g[layer]) * (1 + m[4]) + m[3]
        h = h + m[5] * expert_choice_ffn(u, moe_router[layer], moe_w_gate[layer], moe_w_up[layer], moe_w_down[layer])
        if not last:
            hc = hc + mc[2] * yc
            uc = rms_norm(hc, norm2_g[layer]) * (1 + mc[4]) + mc[3]
            hc = hc + mc[5] * expert_choice_ffn(uc, moe_router[layer], moe_w_gate[layer], moe_w_up[layer], moe_w_down[layer])
    return h


_drawn_inputs = setup_inputs


def setup_inputs(seed=0):
    import zlib

    import numpy as np

    out = dict(_drawn_inputs(seed))
    spreads = {}
    factors = {'norm1_g': 7.001,
     'norm2_g': 6.017,
     'a_q_norm': 8.0,
     'a_k_norm': 8.0,
     'b_q_norm': 8.0,
     'b_k_norm': 8.0,
     'na_rpb': 8.0,
     'gla_gk_b_f': 8.0,
     'gla_gk_b_b': 8.0,
     'gla_o_norm': 8.0}
    for name, (base, spread) in spreads.items():
        noise = np.random.default_rng([zlib.crc32(name.encode()), seed]).standard_normal(out[name].shape)
        drawn = base * np.exp(spread * noise) if base else spread * noise
        out[name] = __import__('jax').numpy.asarray(drawn.astype(out[name].dtype))
    for name, factor in factors.items():
        out[name] = (out[name] * factor).astype(out[name].dtype)
    return out
```

```python
from collections import namedtuple
from contextlib import ExitStack

import numpy as np
import concourse.bass as bass
from concourse import mybir

F32 = mybir.dt.float32
U32 = mybir.dt.uint32
I32 = mybir.dt.int32
ALU = mybir.AluOpType
ACT = mybir.ActivationFunctionType
X_AXIS = mybir.AxisListType.X


def named(**things):
    return namedtuple("Named", list(things))(**things)


P = 128
D = 1024
KD = D // P
LAT, CTX = 512, 256
TOK = LAT + CTX
LT, CT = LAT // P, CTX // P
TT = LT + CT
HD = 64
A_H, A_KV, B_H = 8, 2, 8
ATTN_IN = A_H * HD + 2 * A_KV * HD + 3 * B_H * HD
GRID_W, ROWS, NA_COLS = 64, LAT // 64, 16
DR, DC = 15, 31
E = 16
FF = 1024
CAP_L, CAP_C = 2 * LAT // E, 2 * CTX // E
G_H, G_DK, G_DV, CHUNK = 4, 128, 256, 64
EPS = 1e-6
MASKED = -1e30
BW = 512
SLOTS = 6
SLOT = 4096
NSH = DR - 1

C_ID, C_ROPE, C_MASKF, C_MASKB, C_RESET = 0, 128, 128 + LT * 128, 256 + LT * 128, 384 + LT * 128
C_FLIP = C_RESET + LAT
C_ALL = C_FLIP + P


def shape_constants():
    t = np.arange(LAT)
    half = HD // 2
    inv = (np.float32(10000.0) ** (-np.arange(0, half, 2, dtype=np.float32) / np.float32(half))).astype(np.float32)
    out = np.zeros((P, C_ALL), np.float32)
    out[:, C_ID:C_ID + P] = np.eye(P)
    tabs = []
    for pos in (t // GRID_W, t % GRID_W):
        ang = pos.astype(np.float32)[:, None] * inv[None, :]
        tabs.append((np.cos(ang), np.sin(ang)))
    cos = np.concatenate([tabs[0][0], tabs[0][0], tabs[1][0], tabs[1][0]], 1)
    sin = np.concatenate([-tabs[0][1], tabs[0][1], -tabs[1][1], tabs[1][1]], 1)
    rope = np.concatenate([cos, sin], 1).reshape(LT, P, 2 * HD).transpose(1, 0, 2)
    out[:, C_ROPE:C_ROPE + LT * P] = rope.reshape(P, LT * P)
    j, i = np.arange(P)[:, None], np.arange(P)[None, :]
    same = j // CHUNK == i // CHUNK
    out[:, C_MASKF:C_MASKF + P] = same & (i >= j)
    out[:, C_MASKB:C_MASKB + P] = same & (i <= j)
    out[:, C_RESET:C_RESET + LAT] = (t % CHUNK != 0)[None, :]
    out[:, C_FLIP:] = np.kron(np.eye(2), np.eye(GRID_W)[::-1])
    return out


def build(nc, A, out, stop=None):
    ctx = ExitStack()
    with ctx:
        def sb(name, shape, dt=F32):
            return ctx.enter_context(nc.sbuf_tensor(name, shape, dt))

        def sem(name):
            return ctx.enter_context(nc.semaphore(name))

        H = sb("H", [P, TT, D])
        UT = sb("UT", [P, KD, TOK])
        RING = sb("RING", [P, SLOTS, SLOT])
        CONST = sb("CONST", [P, C_ALL])
        VROWS = sb("VROWS", [88, 2, P])
        VCOL = sb("VCOL", [P, 2, 88])
        SC = sb("SC", [P, KD, 2])
        SCT = sb("SCT", [P, 2, KD, 2])
        MCOL = sb("MCOL", [P, 48, 2])
        ACOL = sb("ACOL", [P, 2, KD, 2])
        MROW = sb("MROW", [P, 2, D])
        GA = sb("GA", [P, 2, HD])
        GB = sb("GB", [P, 2])
        RW = sb("RW", [P, 2, KD, E])
        ONORM = sb("ONORM", [P, G_DV])
        GKW = sb("GKW", [48, G_H * G_DK])
        WZ = sb("WZ", [P, KD, 48])
        STAT = sb("STAT", [P, 320])
        XR = sb("XR", [P, 9984])
        PS = ctx.enter_context(nc.psum_tensor("PS", [P, 8 * BW], F32))

        def bank(b, n=1):
            return PS[:, b * BW:(b + n) * BW]

        def xr(at, *shape):
            n = int(np.prod(shape))
            assert at + n <= 9984
            v = XR[:, at:at + n]
            return v if len(shape) == 1 else v.rearrange(
                "p (a b) -> p a b" if len(shape) == 2 else "p (a b c) -> p a b c",
                **dict(zip("abc", shape)))

        ident = CONST[:, C_ID:C_ID + P]

        RPB = nc.dram_tensor("rpb_scratch", (96 + B_H * DR * DC + 96,), F32, kind="Internal").ap()
        XH = [nc.dram_tensor(f"xhat_{l}", ((TOK, LAT)[l], D), F32, kind="Internal").ap() for l in range(2)]
        ACC = [nc.dram_tensor(f"moe_sum_{l}", ((TOK, LAT)[l], D), F32, kind="Internal").ap() for l in range(2)]

        CONST_LOADS = 16 * 26

        passed = sem("passed")

        plan = [(("ada", 0, c), c % SLOTS) for c in range(12)]
        plan += [(("win", c), s) for c, s in enumerate((0, 1, 5, 0, 1))]
        plan += [(("wout", 0, h), h) for h in range(2)]
        plan += [(("moe", 0, e, s), s) for e in range(E) for s in range(SLOTS)]
        plan += [(("ada", 1, c), c % SLOTS) for c in range(12)]
        plan += [(("gla", c), 3 + c % 3) for c in range(6)]
        plan += [(("wout", 1, h), s) for h, s in enumerate((5, 3))]
        plan += [(("moe", 1, e, s), s) for e in range(E) for s in range(SLOTS)]
        place, filled = {}, [0] * SLOTS
        for name, s in plan:
            place[name] = (s, filled[s])
            filled[s] += 1

        slot_full = [sem(f"slot_full{s}") for s in range(SLOTS)]
        slot_free = [sem(f"slot_free{s}") for s in range(SLOTS)]
        consts_loaded = sem("consts_loaded")
        engine_done = {k: sem(f"phase_done_{k}") for k in ("pe", "dve", "act", "pool")}

        def slot(name, k=KD):
            return RING[:, place[name][0], :].rearrange("p (k n) -> p k n", k=k)

        def wait_full(eng, name):
            s, n = place[name]
            eng.wait_ge(slot_full[s], 16 * (n + 1))

        GATE, UP, DOWN = 1, 3, 5

        def wait_product(eng, l, matrix, e):
            eng.wait_ge(slot_free[matrix], e + (place[("moe", l, 0, matrix)][1] + 1))

        def apart(eng):
            eng.sem_inc(passed, 1)

        def free(name):
            return slot_free[place[name][0]]

        def begin(eng, me, n):
            for k, s in engine_done.items():
                if k != me:
                    eng.wait_ge(s, n)

        def end(eng, me):
            eng.drain().then_inc(engine_done[me], 1)

        h_loaded = sem("h_loaded")
        bias_copied = sem("bias_copied")
        bias_loaded = sem("bias_loaded")
        bias_masked = sem("bias_masked")
        bias_flipped, bias_evac_dve, bias_evac_act = sem("bias_flipped"), sem("bias_evac_dve"), sem("bias_evac_act")
        out_stored = sem("out_stored")
        dve_step, act_step, pool_step = sem("dve_step"), sem("act_step"), sem("pool_step")
        vec_turned, vec_cols = sem("vec_turned"), sem("vec_cols")
        cond_ready, cond_exp = sem("cond_ready"), sem("cond_exp")
        steps = {"dve": 0, "act": 0, "pool": 0}

        def dve_after(ins):
            steps["dve"] += 1
            ins.then_inc(dve_step, 1)
            nc.vector.wait_ge(dve_step, steps["dve"])

        def act_after(ins):
            steps["act"] += 1
            ins.then_inc(act_step, 1)
            nc.scalar.wait_ge(act_step, steps["act"])

        def pool_after(ins):
            steps["pool"] += 1
            ins.then_inc(pool_step, 1)
            nc.gpsimd.wait_ge(pool_step, steps["pool"])

        def group(tag, *names):
            return named(**{n: sem(f"{n}_{tag}") for n in names})

        def uses(sems, counts):
            sems = sems._asdict()
            out, before = [], {k: 0 for k in sems}
            for c in counts:
                out.append(named(**sems, n=named(**before)))
                before = {k: before[k] + c[k] for k in before}
            return out

        ada_s = uses(group("ada", "products"), [dict(products=1)] * 2)
        norm_s = dict(zip(((0, 0), (0, 1), (1, 0), (1, 1)), uses(
            group("norm", "sumsq", "inverse", "rstd", "xhat", "turned", "evac_act", "evac_dve", "stored0", "stored1"),
            [dict(sumsq=t, inverse=1, rstd=1, xhat=t, turned=t, evac_act=t, evac_dve=t, stored0=8 * t * w,
                  stored1=8 * t * w) for t, w in ((TT, 0), (TT, 1), (TT, 0), (LT, 1))])))
        prj = group("prj", "product", "squares", "inverse", "rstd", "v_out", "scaled", "stage",
                    "turned", "evac")
        att = group("att", "scores", "biased", "negmax", "probs", "normal", "turned", "evac_act",
                    "evac_dve", "mixed", "evac_mix")
        outp = uses(group("out", "gate_turned", "gate_act", "product", "added"),
                    [dict(gate_turned=1, gate_act=1, product=t, added=t) for t in (TT, LT)])
        routing = ("logits", "shifted", "exps", "aff", "turned", "packed", "routed", "gate_turned", "gate_act", "gate_dve")
        rt = uses(group("route", *routing), [dict.fromkeys(routing, 1)] * 2)
        once = ("silu", "hidden", "h_turned", "routes", "idx_next")
        ahead = ("x_turned", "xt_act", "xt_dve", "ht_act", "ht_dve", "y_act", "y_dve")
        moe = uses(group("moe", "zeroed", "gathered", "scattered", "readback0", "readback1", "added", *once, *ahead),
                   [dict(zeroed=1, gathered=16 * (E + 1), scattered=16 * (E + 1), readback0=8 * t, readback1=8 * t,
                         added=t, **dict.fromkeys(once, E), **dict.fromkeys(ahead, E + 1)) for t in (TT, LT)])
        gp = group("gp", "product", "evac_act", "z_out", "gate_x", "gate_abs", "gate_exp", "gate_ln", "cum", "raw")
        gs = group("gs", "e_pos", "e_neg", "diff", "e_diff", "qdec", "kinv", "kst", "kturned", "kst_out",
                   "s0", "s0_out", "a_done", "a_out", "upd", "state", "o_done", "o_out")
        mg = group("mg", "squares", "inverse", "rstd", "scaled", "turned", "evac")

        block = ctx.enter_context(nc.Block())

        wout_a2 = sem("wout_a2")
        wz_loaded = sem("wz_loaded")
        acc_cleared = [sem(f"moe_sum_cleared{l}") for l in range(2)]
        IDXT, GATET = sb("IDXT", [96, E + 1], I32), sb("GATET", [96, E])
        IDXG, IDXS, GCUR = sb("IDXG", [96, 1], I32), sb("IDXS", [96, 1], I32), sb("GCUR", [96, 1])

        NSLOT = [CAP_L + CAP_C, CAP_L]

        V = xr(0, TT, (A_KV + B_H) * HD)
        QK = RING[:, 2:5, :].rearrange("p s n -> p (s n)")[:, 0:13 * TOK].rearrange("p (j t) -> p j t", j=13)
        BIAS = RING[:, 0:2, :].rearrange("p s n -> p (s n)")[:, 0:B_H * NSH * GRID_W]
        BIAS_N = B_H * NSH * GRID_W // BW
        PROB = xr(3840, 3, TOK)
        PROBT = xr(3840 + 3 * TOK, 2, TOK)
        SQ = xr(3840, 2, BW)
        STAGE = xr(3840 + 1024, 2, BW)
        ROT = xr(3840 + 2048, BW)
        STAGE2 = xr(3840 + 2560, 2, BW)
        heads = [named(head=h, t=t, base=HD * (h % 2), q=5 + h // 2, k=9 + h // 2, v=P + (h // 2) * P, mix=4 + h // 2,
                       biased=t < LT) for h in range(B_H) for t in range(TT)]
        heads += [named(head=h, t=t, base=HD * (h // 4), q=h % 4, k=4, v=0, mix=h % 4, biased=False)
                  for h in range(A_H) for t in range(TT)]
        ring012 = RING[:, 0:3, :].rearrange("p s n -> p (s n)")
        GV = ring012[:, 0:TT * D].rearrange("p (t n) -> p t n", t=TT)
        OG = ring012[:, TT * D:(TT + LT) * D].rearrange("p (t n) -> p t n", t=LT)
        GQ = ring012[:, (TT + LT) * D:].rearrange("p (j n) -> p j n", j=G_H)
        GK = xr(0, G_H, TOK)
        CUM = [xr(3072, G_H, TOK), xr(6144, G_H, TOK)]
        GLN, ZT = MROW[:, 0, 0:TOK], MROW[0:48, 1, 0:TOK]
        GO = UT[:, :, :].rearrange("p k t -> p (k t)")[:, 0:LT * D].rearrange("p (t n) -> p t n", t=LT)
        OT = RING[:, 4, :].rearrange("p (k t) -> p k t", k=KD)
        gates = [(d, j) for d in range(2) for j in range(G_H)]

        def lane(d):
            r = RING[:, 3 + d, :]
            return named(QZ=r[:, 0:1024], TMP=r[:, 1024:1792], KI=r[:, 1792:2304], KS=r[:, 2304:3072],
                         AT=r[:, 3072:3584], S=r[:, 3584:4096].rearrange("p (b e) -> p b e", b=2),
                         DEC=STAT[:, 80 + 8 * d:88 + 8 * d],
                         qz=lambda t, eo: r[:, (2 * t + eo) * P:(2 * t + eo + 1) * P],
                         qview=lambda t: r[:, 2 * t * P:2 * t * P + 384].rearrange("p (e x) -> p e x", e=2)[:, :, 0:CHUNK])

        lanes = [lane(0), lane(1)]

        def lane_o(h, d, pair):
            return 2 * LT * h + 2 * pair + d + 1

        def lane_state(h, d, i):
            return 2 * (2 * LT - 1) * h + 2 * i + d + 1

        MSR = STAT[:, 0:16]
        PH = STAT[:, 16:64]
        SM = STAT[:, 64:80]
        xhat = xr(0, 2, D)
        sq_junk = xr(2048, D)

        @block.sync
        def _(sp):
            sp.dma_start(CONST[:, :], A["shape_constants"]).then_inc(consts_loaded, 16)
            for l in range(2):
                for at, src in ((0, A["ada_b"][l]), (48, A["norm1_g"][l]), (56, A["norm2_g"][l]),
                                (64, A["c"][0]), (72, A["c_ctx"])):
                    n = int(np.prod(src.shape)) // P
                    sp.dma_start(VROWS[at:at + n, l, :], src.rearrange("(a p) -> a p", p=P)).then_inc(consts_loaded, 16)
                for at, src in ((80, A["gla_gk_b_f"][0]), (84, A["gla_gk_b_b"][0])):
                    sp.dma_start(VROWS[at:at + 4, l, :], src.rearrange("(a p) -> a p", p=P)).then_inc(consts_loaded, 16)
                sp.dma_start(RW[:, l], A["moe_router"][l].rearrange("(k p) e -> p k e", p=P)).then_inc(consts_loaded, 16)
            sp.dma_start(H[:, 0:LT, :], A["x"][0].rearrange("(t p) d -> p t d", p=P)).then_inc(h_loaded, 16)
            sp.dma_start(H[:, LT:TT, :], A["ctx"][0].rearrange("(t p) d -> p t d", p=P)).then_inc(h_loaded, 16)
            for i, g in enumerate(("a_q_norm", "a_k_norm")):
                sp.dma_start(GA[:, i, :], A[g][0:1, :].to_broadcast([P, HD])).then_inc(consts_loaded, 16)
            for i, g in enumerate(("b_q_norm", "b_k_norm")):
                for half in range(2):
                    sp.dma_start(GB[half * HD:(half + 1) * HD, i:i + 1],
                                 A[g].rearrange("a d -> d a")).then_inc(consts_loaded, 16)
            sp.dma_start(ONORM[:, :], A["gla_o_norm"][0:1, :].to_broadcast([P, G_DV])).then_inc(consts_loaded, 16)
            sp.dma_start(GKW[0:16, :], A["gla_gk_w_f"][0]).then_inc(consts_loaded, 16)
            sp.dma_start(GKW[32:48, :], A["gla_gk_w_b"][0]).then_inc(consts_loaded, 16)

            def load(name, src, dst=None):
                s, n = place[name]
                if n:
                    sp.wait_ge(slot_free[s], n)
                sp.dma_start(slot(name) if dst is None else dst, src).then_inc(slot_full[s], 16)

            def load_ada(l):
                for c in range(12):
                    load(("ada", l, c), A["ada_w"][l].rearrange("(k p) n -> p k n", p=P)[:, :, c * BW:(c + 1) * BW])

            def after_phase(n):
                for done in engine_done.values():
                    sp.wait_ge(done, n)

            def load_experts(l):
                w3 = [A[w][l].rearrange("e (k p) n -> p e k n", p=P)
                      for w in ("moe_w_gate", "moe_w_up", "moe_w_down")]
                with sp.Fori(0, E) as e:
                    for s in range(SLOTS):
                        w, half = w3[s // 2], s % 2
                        first = place[("moe", l, 0, s)][1]
                        sp.wait_ge(slot_free[s], e + first)
                        sp.dma_start(RING[:, s, :].rearrange("p (k n) -> p k n", k=4),
                                     w[:, bass.ds(e, 1), 4 * half:4 * half + 4, :].rearrange("p e k n -> p (e k) n")
                                     ).then_inc(slot_full[s], 16)

            load_ada(0)
            n = B_H * DR * DC
            flat = A["na_rpb"][0].rearrange("h a b -> (h a b)")
            sp.dma_start(RPB[96:96 + n], flat).then_inc(bias_copied, 16)
            sp.dma_start(RPB[0:96], flat[0:96]).then_inc(bias_copied, 16)
            sp.dma_start(RPB[96 + n:192 + n], flat[0:96]).then_inc(bias_copied, 16)
            w = A["attn_w_in"][0].rearrange("(k p) n -> p k n", p=P)
            for c in range(5):
                lo, hi = c * BW, min((c + 1) * BW, ATTN_IN)
                load(("win", c), w[:, :, lo:hi], slot(("win", c))[:, :, 0:hi - lo])
            after_phase(3)
            sp.wait_ge(bias_copied, 48)
            for half in range(2):
                for h in range(B_H):
                    src = bass.AP(RPB.tensor, 96 + h * DR * DC + (1 - half) * DC + NA_COLS - GRID_W,
                                  [[1, GRID_W], [DC, NSH], [1, GRID_W]])
                    sp.dma_start(BIAS[half * GRID_W:(half + 1) * GRID_W, h * NSH * GRID_W:(h + 1) * NSH * GRID_W]
                                 .rearrange("p (s c) -> p s c", s=NSH), src).then_inc(bias_loaded, 16)
            sp.wait_ge(att.biased, B_H * LT)
            for h in range(2):
                s, n = place[("wout", 0, h)]
                sp.wait_ge(slot_free[s], n)
                dst = RING[:, s, :].rearrange("p (k n) -> p k n", k=4)
                if h == 0:
                    for a, arrived in enumerate((slot_full[s], wout_a2)):
                        sp.dma_start(dst[a * HD:(a + 1) * HD],
                                     A["attn_w_out"][0][a * 256:(a + 1) * 256, :].rearrange("(j p) n -> p j n", p=HD)
                                     ).then_inc(arrived, 16)
                else:
                    sp.dma_start(dst, A["attn_w_out"][0][512:1024, :].rearrange("(k p) n -> p k n", p=P)
                                 ).then_inc(slot_full[s], 16)
            after_phase(4)
            load_experts(0)
            load_ada(1)
            w = A["gla_w_in"][0].rearrange("(k p) n -> p k n", p=P)
            for c in range(6):
                load(("gla", c), w[:, :, c * BW:(c + 1) * BW])
            after_phase(11)
            for h in range(2):
                s, n = place[("wout", 1, h)]
                sp.wait_ge(slot_free[s], n)
                sp.dma_start(RING[:, s, :].rearrange("p (k n) -> p k n", k=4),
                             A["gla_w_out"][0][h * 512:(h + 1) * 512, :].rearrange("(k p) n -> p k n", p=P)
                             ).then_inc(slot_full[s], 16)
            after_phase(13)
            load_experts(1)
            after_phase(15)
            sp.dma_start(out.rearrange("(t p) d -> p t d", p=P), H[:, 0:LT, :]).then_inc(out_stored, 16)
            sp.wait_ge(out_stored, 16)

        @block.tensor
        def _(pe):
            mm = nc.tensor.matmul

            def ada(l):
                for c in range(12):
                    wait_full(pe, ("ada", l, c))
                    w = slot(("ada", l, c))
                    for sub in range(4):
                        at = (c * 4 + sub) * 2
                        for k in range(KD):
                            last = mm(bank(0)[:, at:at + 2], w[:, k, sub * P:(sub + 1) * P], SC[:, k, :],
                                      start=(k == 0), stop=(k == KD - 1))
                    last.then_inc(free(("ada", l, c)), 1)
                pe.drain().then_inc(ada_s[l].products, 1)

            def norm_turn(l, w, tiles):
                s = norm_s[(l, w)]
                for t in range(tiles):
                    pe.wait_ge(s.xhat, s.n.xhat + t + 1)
                    if t >= 2:
                        pe.wait_ge(s.evac_act, s.n.evac_act + t - 1)
                        pe.wait_ge(s.evac_dve, s.n.evac_dve + t - 1)
                    for k in range(KD):
                        last = nc.tensor.transpose(bank(2 * (t % 2) + k // 4)[:, (k % 4) * P:(k % 4 + 1) * P],
                                                   xhat[:, t % 2, k * P:(k + 1) * P], ident)
                    last.then_inc(s.turned, 1)

            def gate_rows(s, vec, b0):
                for w in range(2):
                    for k in range(KD):
                        last = mm(bank(b0 + 2 * w + k // 4)[:, (k % 4) * P:(k % 4 + 1) * P],
                                  MCOL[:, vec * KD + k, w:w + 1].to_broadcast([P, P]), ident, start=True, stop=True)
                last.then_inc(s.gate_turned, 1)

            def out_projection(l, tiles, MIXT):
                s = outp[l]
                gate_rows(s, 2, 4)
                wait_full(pe, ("wout", l, 0))
                if l == 0:
                    pe.wait_ge(wout_a2, 16)
                wait_full(pe, ("wout", l, 1))
                for t in range(tiles):
                    if t >= 2:
                        pe.wait_ge(s.added, s.n.added + t - 1)
                    for n in range(2):
                        for k in range(KD):
                            wv = RING[:, place[("wout", l, k // 4)][0], :].rearrange("p (k n) -> p k n", k=4)
                            last = mm(bank(2 * (t % 2) + n), MIXT[:, k, t * P:(t + 1) * P],
                                      wv[:, k % 4, n * BW:(n + 1) * BW], start=(k == 0), stop=(k == KD - 1))
                    last.then_inc(s.product, 1)
                pe.drain().then_inc(free(("wout", l, 0)), 1)
                pe.drain().then_inc(free(("wout", l, 1)), 1)

            def route(l, tiles):
                n, s = norm_s[(l, 1)], rt[l]
                pe.wait_ge(n.evac_act, n.n.evac_act + tiles)
                pe.wait_ge(n.evac_dve, n.n.evac_dve + tiles)
                for t in range(tiles):
                    for k in range(KD):
                        last = mm(bank(4)[:, t * E:(t + 1) * E], UT[:, k, t * P:(t + 1) * P], RW[:, l, k, :],
                                  start=(k == 0), stop=(k == KD - 1))
                last.then_inc(s.logits, 1)
                pe.wait_ge(s.aff, s.n.aff + 1)
                for t in range(tiles):
                    last = nc.tensor.transpose(bank(5 + t // 4)[0:48, (t % 4) * P:(t % 4 + 1) * P],
                                               xr(3100, TT, 48)[:, t, :], ident)
                last.then_inc(s.turned, 1)
                pe.wait_ge(s.packed, s.n.packed + 1)
                n = NSLOT[l]
                for i in range(2):
                    last = nc.tensor.transpose(bank(4)[0:n, 128 + i * E:128 + (i + 1) * E],
                                               STAT[0:E, 96 + i * 96:96 + i * 96 + n], ident[0:E, 0:E])
                last.then_inc(s.routed, 1)
                gate_rows(s, 5, 0)

            def experts(l):
                s, n = moe[l], NSLOT[l]
                XG, XT, HID, HT = xr(0, D), xr(1024, KD, 96), xr(1792, D), xr(2816, KD, 96)

                def turn_rows(src, done):
                    for k in range(KD):
                        last = nc.tensor.transpose(bank(6 + k // 4)[:, (k % 4) * P:(k % 4) * P + n],
                                                   src[0:n, k * P:(k + 1) * P], ident[0:n, 0:n])
                    last.then_inc(done, 1)

                pe.wait_ge(s.gathered, s.n.gathered + 16)
                turn_rows(XG, s.x_turned)
                with pe.Fori(0, E) as e:
                    pe.wait_ge(s.xt_act, s.n.xt_act + e + 1)
                    pe.wait_ge(s.xt_dve, s.n.xt_dve + e + 1)
                    for sl in range(4):
                        pe.wait_ge(slot_full[sl], e * 16 + 16 * (place[("moe", l, 0, sl)][1] + 1))
                        w = RING[:, sl, :].rearrange("p (k n) -> p k n", k=4)
                        for k in range(4):
                            for nn in range(2):
                                last = mm(bank(2 * (sl // 2) + nn)[0:n, :], XT[:, (sl % 2) * 4 + k, 0:n],
                                          w[:, k, nn * BW:(nn + 1) * BW], start=(sl % 2 == 0 and k == 0),
                                          stop=(sl % 2 == 1 and k == 3))
                        last.then_inc(slot_free[sl], 1)
                    pe.wait_ge(s.gathered, s.n.gathered + e * 16 + 32)
                    pe.wait_ge(s.ht_act, s.n.ht_act + e + 1)
                    pe.wait_ge(s.ht_dve, s.n.ht_dve + e + 1)
                    apart(pe)
                    turn_rows(XG, s.x_turned)
                    pe.wait_ge(s.hidden, s.n.hidden + e + 1)
                    pe.wait_ge(s.xt_act, s.n.xt_act + e + 2)
                    pe.wait_ge(s.xt_dve, s.n.xt_dve + e + 2)
                    apart(pe)
                    turn_rows(HID, s.h_turned)
                    pe.wait_ge(s.ht_act, s.n.ht_act + e + 2)
                    pe.wait_ge(s.ht_dve, s.n.ht_dve + e + 2)
                    pe.wait_ge(s.y_act, s.n.y_act + e + 1)
                    pe.wait_ge(s.y_dve, s.n.y_dve + e + 1)
                    for sl in range(4, 6):
                        pe.wait_ge(slot_full[sl], e * 16 + 16 * (place[("moe", l, 0, sl)][1] + 1))
                        w = RING[:, sl, :].rearrange("p (k n) -> p k n", k=4)
                        for k in range(4):
                            for nn in range(2):
                                last = mm(bank(4 + nn)[0:n, :], HT[:, (sl - 4) * 4 + k, 0:n],
                                          w[:, k, nn * BW:(nn + 1) * BW], start=(sl == 4 and k == 0),
                                          stop=(sl == 5 and k == 3))
                        last.then_inc(slot_free[sl], 1)

            pe.wait_ge(consts_loaded, CONST_LOADS)
            for l in range(2):
                last = nc.tensor.transpose(bank(1)[:, l * 88:(l + 1) * 88], VROWS[:, l, :], ident[0:88, 0:88])
            last.then_inc(vec_turned, 1)
            pe.wait_ge(cond_ready, 1)
            ada(0)
            end(pe, "pe")
            begin(pe, "pe", 1)
            norm_turn(0, 0, TT)
            end(pe, "pe")
            begin(pe, "pe", 2)
            units = [(c, t) for c in range(5) for t in range(TT)]

            def turn_heads(u):
                c, t = units[u]
                if c == 4:
                    return
                pe.wait_ge(prj.stage, u + 1)
                if u >= 2:
                    pe.wait_ge(prj.evac, u - 1)
                src = STAGE2[:, u % 2, :] if c < 2 else STAGE[:, u % 2, :]
                for cols in ((0, 1, 2, 3), (0, 2, 3), (0, 1, 2, 3), (0, 1))[c]:
                    last = nc.tensor.transpose(bank(4 + u % 2)[:, cols * P:(cols + 1) * P],
                                               src[:, cols * P:(cols + 1) * P], ident)
                last.then_inc(prj.turned, 1)

            for u, (c, t) in enumerate(units):
                w = min(BW, ATTN_IN - c * BW)
                if t == 0:
                    wait_full(pe, ("win", c))
                if u >= 4:
                    pe.wait_ge(prj.scaled, u - 3)
                    pe.wait_ge(prj.v_out, u - 3)
                for k in range(KD):
                    last = mm(bank(u % 4)[:, 0:w], UT[:, k, t * P:(t + 1) * P], slot(("win", c))[:, k, 0:w],
                              start=(k == 0), stop=(k == KD - 1))
                last.then_inc(prj.product, 1)
                if t == TT - 1:
                    pe.drain().then_inc(free(("win", c)), 1)
                if u:
                    turn_heads(u - 1)
            end(pe, "pe")
            begin(pe, "pe", 3)
            pe.wait_ge(bias_masked, 1)
            for i in range(BIAS_N):
                if i >= 4:
                    pe.wait_ge((bias_evac_dve, bias_evac_act)[i % 2], i // 2 - 1)
                mm(bank(i % 4), CONST[:, C_FLIP:C_FLIP + P], BIAS[:, i * BW:(i + 1) * BW], start=True, stop=True
                   ).then_inc(bias_flipped, 1)
            pe.wait_ge(bias_evac_dve, BIAS_N // 2)
            pe.wait_ge(bias_evac_act, BIAS_N // 2)
            N = len(heads)
            for i in range(N + 3):
                if i < N:
                    u = heads[i]
                    if i >= 2:
                        pe.wait_ge(att.probs, i - 1)
                    q = QK[u.base:u.base + HD, u.q, u.t * P:(u.t + 1) * P]
                    b0 = 2 * (i % 2)
                    if u.t < LT:
                        mm(bank(b0), q, QK[u.base:u.base + HD, u.k, 0:LAT], start=True, stop=True)
                    mm(bank(b0 + 1)[:, 0:CTX], q, QK[u.base:u.base + HD, u.k, LAT:TOK], start=True,
                       stop=True).then_inc(att.scores, 1)
                j = i - 2
                if 0 <= j < N:
                    u = heads[j]
                    pe.wait_ge(att.normal, j + 1)
                    if j >= 1:
                        pe.wait_ge(att.evac_act, j)
                        pe.wait_ge(att.evac_dve, j)
                    for kt in range(0 if u.t < LT else LT, TT):
                        last = nc.tensor.transpose(bank(4 + kt // 4)[:, (kt % 4) * P:(kt % 4 + 1) * P],
                                                   PROB[:, j % 3, kt * P:(kt + 1) * P], ident)
                    last.then_inc(att.turned, 1)
                j = i - 3
                if 0 <= j < N:
                    u = heads[j]
                    pe.wait_ge(att.evac_act, j + 1)
                    pe.wait_ge(att.evac_dve, j + 1)
                    if j >= 2:
                        pe.wait_ge(att.evac_mix, j - 1)
                    kts = range(0 if u.t < LT else LT, TT)
                    for kt in kts:
                        last = mm(bank(6 + j % 2)[:, 0:P], V[:, kt, u.v:u.v + P],
                                  PROBT[:, j % 2, kt * P:(kt + 1) * P], start=(kt == kts[0]), stop=(kt == TT - 1))
                    last.then_inc(att.mixed, 1)
            end(pe, "pe")
            begin(pe, "pe", 4)
            out_projection(0, TT, UT)
            end(pe, "pe")
            begin(pe, "pe", 5)
            norm_turn(0, 1, TT)
            route(0, TT)
            end(pe, "pe")
            begin(pe, "pe", 6)
            experts(0)
            end(pe, "pe")
            begin(pe, "pe", 7)
            ada(1)
            end(pe, "pe")
            begin(pe, "pe", 8)
            norm_turn(1, 0, TT)
            end(pe, "pe")
            begin(pe, "pe", 9)
            n_out = [0]

            def next_bank():
                i = n_out[0]
                if i >= 4:
                    pe.wait_ge(gp.evac_act, i - 3)
                n_out[0] += 1
                return bank(i % 4)

            for c in range(2):
                wait_full(pe, ("gla", c))
                for j in range(G_H):
                    for lo, hi in ((0, LAT), (LAT, TOK))[:1 + c]:
                        b = next_bank()
                        for k in range(KD):
                            last = mm(b[:, 0:hi - lo], slot(("gla", c))[:, k, j * P:(j + 1) * P], UT[:, k, lo:hi],
                                      start=(k == 0), stop=(k == KD - 1))
                        last.then_inc(gp.product, 1)
                pe.drain().then_inc(free(("gla", c)), 1)
            for lo, hi in ((0, LAT), (LAT, TOK)):
                b = next_bank()
                for k in range(KD):
                    last = mm(b[0:48, 0:hi - lo], WZ[:, k, :], UT[:, k, lo:hi], start=(k == 0), stop=(k == KD - 1))
                last.then_inc(gp.product, 1)
            for c in range(2, 6):
                wait_full(pe, ("gla", c))
                for t in range(TT if c < 4 else LT):
                    b = next_bank()
                    for k in range(KD):
                        last = mm(b, UT[:, k, t * P:(t + 1) * P], slot(("gla", c))[:, k, :],
                                  start=(k == 0), stop=(k == KD - 1))
                    last.then_inc(gp.product, 1)
                pe.drain().then_inc(free(("gla", c)), 1)
            pe.wait_ge(gp.evac_act, n_out[0])
            for i, (d, j) in enumerate(gates):
                b0 = 4 + 2 * (i % 2)
                if i >= 2:
                    pe.wait_ge(gp.gate_x, i - 1)
                    pe.wait_ge(gp.gate_abs, i - 1)
                for lo, hi in ((0, LAT), (LAT, TOK)):
                    last = mm(bank(b0, 2)[:, lo:hi], GKW[32 * d:32 * d + 16, j * P:(j + 1) * P],
                              ZT[32 * d:32 * d + 16, lo:hi], start=True, stop=True)
                last.then_inc(gp.raw, 1)
            end(pe, "pe")
            begin(pe, "pe", 10)
            for h in range(G_H):
                for d in range(2):
                    L = lanes[d]
                    n = 2 * h + d
                    b0 = 4 * d
                    pe.wait_ge(gs.kst, n + 1)
                    if h:
                        pe.wait_ge(gs.o_out, lane_o(h - 1, d, LT - 1))
                    for t in range(TT):
                        last = nc.tensor.transpose(bank(b0 + t // 4)[:, (t % 4) * P:(t % 4 + 1) * P],
                                                   L.KS[:, t * P:(t + 1) * P], ident)
                    last.then_inc(gs.kturned, 1)
                for d in range(2):
                    L = lanes[d]
                    n = 2 * h + d
                    b0 = 4 * d
                    pe.wait_ge(gs.kst_out, n + 1)
                    for i in range(CT):
                        last = mm(bank(b0 + 2)[:, 0:G_DV], L.KS[:, (LT + i) * P:(LT + i + 1) * P],
                                  GV[:, LT + i, h * G_DV:(h + 1) * G_DV], start=(i == 0), stop=(i == CT - 1))
                    last.then_inc(gs.s0, 1)
                    pe.wait_ge(gs.qdec, n + 1)
                    pe.wait_ge(gs.kinv, n + 1)
                    for t in range(LT):
                        last = mm(bank(b0)[:, t * P:(t + 1) * P], L.KI[:, t * P:(t + 1) * P], L.qview(t),
                                  start=True, stop=True)
                    last.then_inc(gs.a_done, 1)
                for d in range(2):
                    n = 2 * h + d
                    pe.wait_ge(gs.a_out, n + 1)
                    pe.wait_ge(gs.s0_out, n + 1)
                for i in range(2 * LT):
                    for d in range(2):
                        L = lanes[d]
                        b0 = 4 * d
                        c = i if d == 0 else 2 * LT - 1 - i
                        t, eo = c // 2, c % 2
                        ob = bank(b0 + 1 + 2 * ((i // 2) % 2))[:, 0:G_DV]
                        v = GV[:, t, h * G_DV:(h + 1) * G_DV]
                        if i % 2 == 0:
                            if i >= 4:
                                pe.wait_ge(gs.o_out, lane_o(h, d, i // 2 - 2))
                            mm(ob, L.AT[:, t * P:(t + 1) * P], v, start=True, stop=False)
                        if i:
                            pe.wait_ge(gs.state, lane_state(h, d, i - 1))
                        last = mm(ob, L.qz(t, eo), L.S[:, i % 2, :], start=False, stop=(i % 2 == 1))
                        if i % 2:
                            last.then_inc(gs.o_done, 1)
                        if i < 2 * LT - 1:
                            half = slice(eo * CHUNK, (eo + 1) * CHUNK)
                            mm(bank(b0 + 2)[:, 256:512], L.KS[half, t * P:(t + 1) * P],
                               GV[half, t, h * G_DV:(h + 1) * G_DV], start=True, stop=True).then_inc(gs.upd, 1)
            end(pe, "pe")
            begin(pe, "pe", 11)
            for t in range(LT):
                pe.wait_ge(mg.scaled, t + 1)
                if t >= 2:
                    pe.wait_ge(mg.evac, t - 1)
                for k in range(KD):
                    last = nc.tensor.transpose(bank(2 * (t % 2) + k // 4)[:, (k % 4) * P:(k % 4 + 1) * P],
                                               GO[:, t, k * P:(k + 1) * P], ident)
                last.then_inc(mg.turned, 1)
            end(pe, "pe")
            begin(pe, "pe", 12)
            out_projection(1, LT, OT)
            end(pe, "pe")
            begin(pe, "pe", 13)
            norm_turn(1, 1, LT)
            route(1, LT)
            end(pe, "pe")
            begin(pe, "pe", 14)
            experts(1)
            end(pe, "pe")

        @block.vector
        def _(dve):
            v = nc.vector

            def modulation(l):
                dve.wait_ge(ada_s[l].products, l + 1)
                dve_after(v.tensor_tensor(MCOL[:, :, :], bank(0)[:, 0:96].rearrange("p (j w) -> p j w", w=2),
                                          VCOL[:, l, 0:48].unsqueeze(2).to_broadcast([P, 48, 2]), ALU.add))
                for i in range(2):
                    v.scalar_tensor_tensor(out=ACOL[:, i], in0=MCOL[:, (1 + 3 * i) * KD:(2 + 3 * i) * KD, :], scalar=1.0,
                                           in1=VCOL[:, l, 48 + 8 * i:56 + 8 * i].unsqueeze(2).to_broadcast([P, KD, 2]),
                                           op0=ALU.add, op1=ALU.mult)

            def norm(l, w, tiles):
                s = norm_s[(l, w)]
                dve.wait_ge(s.sumsq, s.n.sumsq + tiles)
                dve_after(v.tensor_scalar(MSR[:, 0:tiles], STAT[:, 304:304 + tiles], 1.0 / D, EPS, ALU.mult, ALU.add))
                v.reciprocal(STAT[:, 8:8 + tiles], MSR[:, 0:tiles]).then_inc(s.inverse, 1)
                dve.wait_ge(s.rstd, s.n.rstd + 1)
                for t in range(tiles + 1):
                    if t < tiles:
                        if t >= 2:
                            dve.wait_ge(s.turned, s.n.turned + t - 1)
                            if w:
                                dve.wait_ge((s.stored0, s.stored1)[t % 2], s.n.stored0 + 16 * (t // 2))
                        v.tensor_scalar(xhat[:, t % 2, :], H[:, t, :], MSR[:, t:t + 1], None, ALU.mult).then_inc(s.xhat, 1)
                    if t:
                        u = t - 1
                        dve.wait_ge(s.turned, s.n.turned + u + 1)
                        st = 0 if u < LT else 1
                        for k in range(4, KD):
                            last = v.tensor_scalar(UT[:, k, u * P:(u + 1) * P],
                                                   bank(2 * (u % 2) + 1)[:, (k - 4) * P:(k - 3) * P],
                                                   ACOL[:, w, k, st:st + 1], MCOL[:, 3 * w * KD + k, st:st + 1],
                                                   ALU.mult, ALU.add)
                        last.then_inc(s.evac_dve, 1)

            def residual(l, tiles):
                s = outp[l]
                dve.wait_ge(s.gate_turned, s.n.gate_turned + 1)
                dve_after(v.tensor_copy(MROW[:, 1, :], bank(6, 2)))
                dve.wait_ge(s.gate_act, s.n.gate_act + 1)
                tmp = xr(0, D)
                for t in range(tiles):
                    dve.wait_ge(s.product, s.n.product + t + 1)
                    dve_after(v.tensor_tensor(tmp, bank(2 * (t % 2), 2), MROW[:, 0 if t < LT else 1, :], ALU.mult))
                    last = v.tensor_tensor(H[:, t, :], H[:, t, :], tmp, ALU.add)
                    dve_after(last)
                    v.engine_nop().then_inc(s.added, 1)

            def route(l, tiles):
                s = rt[l]
                lg, af, small = xr(3400, TT, E), xr(3100, TT, 48), STAT[:, 0:16]
                affT, work = xr(4000, LAT), xr(4600, 64)
                idx = xr(4700, 64).bitcast(U32)
                dve_after(v.memset(af[:, 0:tiles], 0.0))
                dve_after(v.memset(affT[0:48], -1.0))
                dve.wait_ge(s.logits, s.n.logits + 1)
                ps = bank(4)[:, 0:tiles * E].rearrange("p (t e) -> p t e", e=E)
                dve_after(v.tensor_reduce(small[:, 0:tiles], ps, X_AXIS, ALU.max))
                v.tensor_tensor(lg[:, 0:tiles], ps, small[:, 0:tiles].unsqueeze(2).to_broadcast([P, tiles, E]),
                                ALU.subtract).then_inc(s.shifted, 1)
                dve.wait_ge(s.exps, s.n.exps + 1)
                dve_after(v.tensor_reduce(small[:, 0:tiles], lg[:, 0:tiles], X_AXIS, ALU.add))
                dve_after(v.reciprocal(small[:, 8:8 + tiles], small[:, 0:tiles]))
                for lo, hi, at in ((0, LT, 0), (LT, tiles, 32))[:1 if tiles == LT else 2]:
                    last = v.tensor_tensor(af[:, lo:hi, at:at + E], lg[:, lo:hi],
                                           small[:, 8 + lo:8 + hi].unsqueeze(2).to_broadcast([P, hi - lo, E]), ALU.mult)
                    dve_after(last)
                v.engine_nop().then_inc(s.aff, 1)
                dve.wait_ge(s.turned, s.n.turned + 1)
                dve_after(v.tensor_copy(affT[0:E, :], bank(5)[0:E, :]))
                if tiles > LT:
                    dve_after(v.tensor_copy(affT[32:48, 0:CTX], bank(6)[32:48, 0:CTX]))
                for r in range(CAP_L // 8):
                    g8 = work[0:48, r * 8:(r + 1) * 8]
                    dve_after(v.max(g8, affT[0:48]))
                    dve_after(v.max_index(idx[0:48, r * 8:(r + 1) * 8], g8, affT[0:48]))
                    dve_after(v.match_replace(affT[0:48], g8, affT[0:48], -2.0))
                pack = STAT[0:E, 96:288]
                dve_after(v.tensor_copy(pack[:, 0:CAP_L], idx[0:E, :]))
                dve_after(v.tensor_copy(pack[:, 96:96 + CAP_L], work[0:E, :]))
                if tiles > LT:
                    dve_after(v.tensor_scalar(pack[:, CAP_L:96], idx[32:48, 0:CAP_C], float(LAT), None, ALU.add))
                    dve_after(v.tensor_copy(pack[:, 96 + CAP_L:192], work[32:48, 0:CAP_C]))
                v.engine_nop().then_inc(s.packed, 1)
                dve.wait_ge(s.routed, s.n.routed + 1)
                n = NSLOT[l]
                dve_after(v.memset(IDXT[:, :], 0))
                dve_after(v.tensor_copy(IDXT[0:n, 0:E], bank(4)[0:n, 128:128 + E]))
                dve_after(v.tensor_copy(GATET[0:n, :], bank(4)[0:n, 128 + E:128 + 2 * E]))
                dve.wait_ge(s.gate_turned, s.n.gate_turned + 1)
                v.tensor_copy(MROW[:, 1, :], bank(2, 2)).then_inc(s.gate_dve, 1)

            def experts(l):
                s, n = moe[l], NSLOT[l]
                XT, HID, HT = xr(1024, KD, 96), xr(1792, D), xr(2816, KD, 96)
                SIL, Y = xr(3584, D), xr(4608, D)
                ZERO = xr(5700, D)
                v.memset(ZERO, 0.0).then_inc(s.zeroed, 1)
                v.memset(STAT[:, 296:297], 0.0).then_inc(s.ht_dve, 1)
                v.memset(STAT[:, 297:298], 0.0).then_inc(s.y_dve, 1)

                def modulate():
                    for k in range(4, KD):
                        b = bank(7)[:, (k - 4) * P:(k - 4) * P + n]
                        for st, lo, hi in ((0, 0, CAP_L), (1, CAP_L, n))[:1 if n == CAP_L else 2]:
                            last = v.tensor_scalar(XT[:, k, lo:hi], b[:, lo:hi], ACOL[:, 1, k, st:st + 1],
                                                   MCOL[:, 3 * KD + k, st:st + 1], ALU.mult, ALU.add)
                    last.then_inc(s.xt_dve, 1)

                dve.wait_ge(s.x_turned, s.n.x_turned + 1)
                modulate()
                with dve.Fori(0, E) as e:
                    dve.wait_ge(s.silu, s.n.silu + e + 1)
                    wait_product(dve, l, UP, e)
                    v.tensor_tensor(HID[0:n], SIL[0:n], bank(2, 2)[0:n], ALU.mult).then_inc(s.hidden, 1)
                    dve.wait_ge(s.x_turned, s.n.x_turned + e + 2)
                    modulate()
                    dve.wait_ge(s.h_turned, s.n.h_turned + e + 1)
                    v.tensor_copy(HT[:, 4:8, 0:n], bank(7).rearrange("p (k t) -> p k t", t=P)[:, :, 0:n]
                                  ).then_inc(s.ht_dve, 1)
                    dve.wait_ge(s.routes, s.n.routes + e + 1)
                    wait_product(dve, l, DOWN, e)
                    v.tensor_scalar(Y[0:n, BW:D], bank(5)[0:n], GCUR[0:n, :], None, ALU.mult).then_inc(s.y_dve, 1)
                buf = xr(0, 2, D)
                dve.wait_ge(rt[l].gate_act, rt[l].n.gate_act + 1)
                for t in range(TT if l == 0 else LT):
                    dve.wait_ge((s.readback0, s.readback1)[t % 2], s.n.readback0 + 16 * (t // 2 + 1))
                    b = buf[:, t % 2, :]
                    dve_after(v.tensor_tensor(b, b, MROW[:, 0 if t < LT else 1, :], ALU.mult))
                    v.tensor_tensor(H[:, t, :], H[:, t, :], b, ALU.add).then_inc(s.added, 1)

            dve.wait_ge(vec_turned, 1)
            dve_after(v.tensor_copy(VCOL[:, :, :], bank(1)[:, 0:176].rearrange("p (l c) -> p l c", l=2)))
            v.engine_nop().then_inc(vec_cols, 1)
            dve.wait_ge(cond_exp, 1)
            cv = VCOL[:, 0, 64:80].rearrange("p (w k) -> p k w", w=2)
            dve_after(v.tensor_scalar(SCT[:, 1], SCT[:, 0], 1.0, None, ALU.add))
            dve_after(v.reciprocal(SCT[:, 0], SCT[:, 1]))
            v.tensor_tensor(SC[:, :, :], SCT[:, 0], cv, ALU.mult).then_inc(cond_ready, 1)
            dve.wait_ge(consts_loaded, CONST_LOADS)
            v.tensor_scalar(GA[:, 0, :], GA[:, 0, :], HD ** -0.5, None, ALU.mult)
            v.tensor_scalar(GB[:, 0:1], GB[:, 0:1], HD ** -0.5, None, ALU.mult)
            modulation(0)
            end(dve, "dve")
            begin(dve, "dve", 1)
            norm(0, 0, TT)
            end(dve, "dve")
            begin(dve, "dve", 2)
            for u, (c, t) in enumerate([(c, t) for c in range(5) for t in range(TT)]):
                if c == 4:
                    dve.wait_ge(prj.product, u + 1)
                    v.engine_nop().then_inc(prj.scaled, 1)
                    continue
                ps = bank(u % 4)
                ph = PH[:, 24 * (u % 2):24 * (u % 2) + 24]
                dve.wait_ge(prj.squares, u + 1)
                dve_after(v.tensor_reduce(ph[:, 0:8], SQ[:, u % 2, :].rearrange("p (h d) -> p h d", d=HD), X_AXIS, ALU.add))
                dve_after(v.tensor_scalar(ph[:, 8:16], ph[:, 0:8], 1.0 / HD, EPS, ALU.mult, ALU.add))
                v.reciprocal(ph[:, 16:24], ph[:, 8:16]).then_inc(prj.inverse, 1)
                dve.wait_ge(prj.rstd, u + 1)
                if u >= 2:
                    dve.wait_ge(prj.turned, u - 1)
                st = STAGE[:, u % 2, :]
                last = v.tensor_tensor(st.rearrange("p (h d) -> p h d", d=HD), ps.rearrange("p (h d) -> p h d", d=HD),
                                       ph[:, 0:8].unsqueeze(2).to_broadcast([P, 8, HD]), ALU.mult)
                last.then_inc(prj.scaled, 1)
                dve.wait_ge(prj.scaled, u + 1)
                if c < 2:
                    nh = 8 if c == 0 else 2
                    a = st[:, 0:nh * HD]
                    dve_after(v.tensor_tensor(a.rearrange("p (h d) -> p h d", d=HD), a.rearrange("p (h d) -> p h d", d=HD),
                                              GA[:, c, :].unsqueeze(1).to_broadcast([P, nh, HD]), ALU.mult))
                    if c == 0:
                        dst = STAGE2[:, u % 2, :].rearrange("p (j a d) -> p a j d", j=4, a=2)
                    else:
                        dst = STAGE2[:, u % 2, 0:nh * HD].rearrange("p (j a d) -> p a j d", j=1, a=2)
                    if t < LT:
                        cos = CONST[:, C_ROPE + t * P:C_ROPE + t * P + HD]
                        sin = CONST[:, C_ROPE + t * P + HD:C_ROPE + (t + 1) * P].rearrange("p (g s i) -> p g s i", g=2, s=2)
                        src4 = a.rearrange("p (h g s i) -> p (h g) s i", g=2, s=2, i=16)
                        rot4 = ROT[:, 0:nh * HD].rearrange("p (h g s i) -> p (h g) s i", g=2, s=2, i=16)
                        for g in range(2):
                            for sd in range(2):
                                dve_after(v.tensor_tensor(
                                    rot4[:, g::2, sd, :], src4[:, g::2, 1 - sd, :],
                                    sin[:, g, sd, :].unsqueeze(1).to_broadcast([P, nh, 16]), ALU.mult))
                        dve_after(v.tensor_tensor(a.rearrange("p (h d) -> p h d", d=HD), a.rearrange("p (h d) -> p h d", d=HD),
                                                  cos.unsqueeze(1).to_broadcast([P, nh, HD]), ALU.mult))
                        for aa in range(2):
                            hh = nh // 2
                            dve_after(v.tensor_tensor(
                                dst[:, aa], a[:, aa * hh * HD:(aa + 1) * hh * HD].rearrange("p (j d) -> p j d", d=HD),
                                ROT[:, aa * hh * HD:(aa + 1) * hh * HD].rearrange("p (j d) -> p j d", d=HD), ALU.add))
                    else:
                        for aa in range(2):
                            hh = nh // 2
                            dve_after(v.tensor_copy(dst[:, aa], a[:, aa * hh * HD:(aa + 1) * hh * HD].rearrange("p (j d) -> p j d", d=HD)))
                    if c == 1:
                        dve_after(v.tensor_copy(STAGE2[:, u % 2, 256:512], st[:, 256:512]))
                v.engine_nop().then_inc(prj.stage, 1)
            end(dve, "dve")
            begin(dve, "dve", 3)
            for i in range(0, BIAS_N, 2):
                dve.wait_ge(bias_flipped, i + 1)
                v.tensor_copy(BIAS[:, i * BW:(i + 1) * BW], bank(i % 4)).then_inc(bias_evac_dve, 1)
            N = len(heads)
            nbias = 0
            for i in range(N + 3):
                if i < N:
                    u = heads[i]
                    b0 = 2 * (i % 2)
                    dve.wait_ge(att.scores, i + 1)
                    sc = bank(b0, 2)[:, (0 if u.t < LT else LAT):TOK]
                    if u.biased:
                        if nbias == 0:
                            dve.wait_ge(bias_evac_act, BIAS_N // 2)
                            dve.wait_ge(bias_evac_dve, BIAS_N // 2)
                        nbias += 1
                        lo = (u.head * NSH + (ROWS - 2 - 2 * u.t)) * GRID_W
                        v.tensor_tensor(bank(b0), bank(b0), BIAS[:, lo:lo + LAT], ALU.add).then_inc(att.biased, 1)
                        dve.wait_ge(att.biased, nbias)
                    dve_after(v.tensor_reduce(SM[:, i % 3:i % 3 + 1], sc, X_AXIS, ALU.max))
                    if i >= 3:
                        dve.wait_ge(att.probs, i - 2)
                    v.tensor_scalar(SM[:, 3 + i % 3:4 + i % 3], SM[:, i % 3:i % 3 + 1], -1.0, None, ALU.mult).then_inc(att.negmax, 1)
                j = i - 1
                if 0 <= j < N:
                    u = heads[j]
                    dve.wait_ge(att.probs, j + 1)
                    dve_after(v.reciprocal(SM[:, 9:10], SM[:, 6 + j % 3:7 + j % 3]))
                    pr = PROB[:, j % 3, (0 if u.t < LT else LAT):TOK]
                    v.tensor_scalar(pr, pr, SM[:, 9:10], None, ALU.mult).then_inc(att.normal, 1)
                    dve.wait_ge(att.normal, j + 1)
                j = i - 2
                if 0 <= j < N:
                    dve.wait_ge(att.turned, j + 1)
                    if j >= 2:
                        dve.wait_ge(att.mixed, j - 1)
                    v.tensor_copy(PROBT[:, j % 2, LAT:TOK], bank(5)[:, 0:CTX]).then_inc(att.evac_dve, 1)
            end(dve, "dve")
            begin(dve, "dve", 4)
            residual(0, TT)
            end(dve, "dve")
            begin(dve, "dve", 5)
            norm(0, 1, TT)
            route(0, TT)
            end(dve, "dve")
            begin(dve, "dve", 6)
            experts(0)
            end(dve, "dve")
            begin(dve, "dve", 7)
            modulation(1)
            end(dve, "dve")
            begin(dve, "dve", 8)
            norm(1, 0, TT)
            end(dve, "dve")
            begin(dve, "dve", 9)
            GTMP = xr(9216, TOK)
            for i, (d, j) in enumerate(gates):
                dve.wait_ge(gp.gate_abs, i + 1)
                bcol = VCOL[:, 1, 80 + 4 * d + j:81 + 4 * d + j]
                v.tensor_scalar(GTMP, bank(4 + 2 * (i % 2), 2)[:, 0:TOK], bcol, 0.0, ALU.add, ALU.min).then_inc(gp.gate_x, 1)
                dve.wait_ge(gp.gate_ln, i + 1)
                dve.wait_ge(gp.gate_x, i + 1)
                dve_after(v.tensor_tensor(GTMP, GTMP, GLN, ALU.subtract))
                cum = CUM[d][:, j, :]
                for lo, hi, m in ((0, LAT, CONST[:, C_RESET:C_RESET + LAT]), (LAT, TOK, CONST[:, C_RESET + 1:C_RESET + 2].to_broadcast([P, CTX]))):
                    o, g = cum[:, lo:hi], GTMP[:, lo:hi]
                    if d:
                        o, g = o[:, ::-1], g[:, ::-1]
                    last = v.tensor_tensor_scan(o, m, g, 0.0, ALU.mult, ALU.add)
                dve_after(last)
                v.engine_nop().then_inc(gp.cum, 1)
            end(dve, "dve")
            begin(dve, "dve", 10)
            for d in range(2):
                dve_after(v.memset(lanes[d].QZ, 0.0))
                dve_after(v.memset(lanes[d].AT, 0.0))
            for h in range(G_H):
                for d in range(2):
                    L = lanes[d]
                    n = 2 * h + d
                    cum = CUM[d][:, h, :]
                    edge = CHUNK - 1 if d == 0 else 0
                    dve.wait_ge(gs.e_pos, n + 1)
                    if h:
                        dve.wait_ge(gs.o_done, lane_o(h - 1, d, LT - 1))
                    e4 = L.TMP[:, 0:LAT].rearrange("p (t x) -> p t x", x=P)
                    q4 = GQ[:, h, :].rearrange("p (t x) -> p t x", x=P)
                    qz4 = L.QZ.rearrange("p (t e x) -> p t e x", e=2, x=P)
                    dve_after(v.tensor_copy(L.DEC, L.TMP[:, edge:LAT:CHUNK]))
                    for eo in range(2):
                        sl = slice(eo * CHUNK, (eo + 1) * CHUNK)
                        last = v.tensor_tensor(qz4[:, :, eo, sl], q4[:, :, sl], e4[:, :, sl], ALU.mult)
                        dve_after(last)
                    v.engine_nop().then_inc(gs.qdec, 1)
                    c3 = cum[:, 0:LAT].rearrange("p (c x) -> p c x", x=CHUNK)
                    dve_after(v.tensor_tensor(L.TMP[:, 0:LAT].rearrange("p (c x) -> p c x", x=CHUNK),
                                              c3[:, :, edge:edge + 1].to_broadcast([P, LAT // CHUNK, CHUNK]), c3, ALU.subtract))
                    cx = LAT + (CTX - 1 if d == 0 else 0)
                    v.tensor_tensor(L.TMP[:, LAT:TOK], cum[:, cx:cx + 1].to_broadcast([P, CTX]), cum[:, LAT:TOK],
                                    ALU.subtract).then_inc(gs.diff, 1)
                    dve.wait_ge(gs.e_neg, n + 1)
                    v.tensor_tensor(L.KI, L.KI, GK[:, h, 0:LAT], ALU.mult).then_inc(gs.kinv, 1)
                    dve.wait_ge(gs.e_diff, n + 1)
                    v.tensor_tensor(L.KS, L.TMP, GK[:, h, :], ALU.mult).then_inc(gs.kst, 1)
                for d in range(2):
                    L = lanes[d]
                    n = 2 * h + d
                    dve.wait_ge(gs.s0, n + 1)
                    v.tensor_copy(L.S[:, 0, :], bank(4 * d + 2)[:, 0:G_DV]).then_inc(gs.s0_out, 1)
                    dve.wait_ge(gs.a_done, n + 1)
                    m = CONST[:, (C_MASKF, C_MASKB)[d]:(C_MASKF, C_MASKB)[d] + P].bitcast(U32)
                    for t in range(LT):
                        last = v.copy_predicated(L.AT[:, t * P:(t + 1) * P], m, bank(4 * d)[:, t * P:(t + 1) * P])
                        dve_after(last)
                    v.engine_nop().then_inc(gs.a_out, 1)
                for i in range(2 * LT):
                    for d in range(2):
                        L = lanes[d]
                        if i < 2 * LT - 1:
                            c = i if d == 0 else 2 * LT - 1 - i
                            dve.wait_ge(gs.upd, lane_state(h, d, i))
                            if i == 0:
                                dve.wait_ge(gs.s0_out, 2 * h + d + 1)
                            else:
                                dve.wait_ge(gs.state, lane_state(h, d, i - 1))
                            v.scalar_tensor_tensor(out=L.S[:, (i + 1) % 2, :], in0=L.S[:, i % 2, :],
                                                   scalar=L.DEC[:, c:c + 1], in1=bank(4 * d + 2)[:, 256:512],
                                                   op0=ALU.mult, op1=ALU.add).then_inc(gs.state, 1)
                        if i % 2:
                            t = (i // 2) if d == 0 else LT - 1 - i // 2
                            ob = bank(4 * d + 1 + 2 * ((i // 2) % 2))[:, 0:G_DV]
                            o = GO[:, t, h * G_DV:(h + 1) * G_DV]
                            k = lane_o(h, d, i // 2)
                            dve.wait_ge(gs.o_done, k)
                            first = (i < LT)
                            if first:
                                v.tensor_copy(o, ob).then_inc(gs.o_out, 1)
                            else:
                                dve.wait_ge(gs.o_out, k - 1)
                                v.tensor_tensor(o, o, ob, ALU.add).then_inc(gs.o_out, 1)
            end(dve, "dve")
            begin(dve, "dve", 11)
            st = STAT[:, 0:48]
            dve.wait_ge(mg.squares, LT * G_H)
            dve_after(v.tensor_scalar(st[:, 16:32], st[:, 0:16], 1.0 / G_DV, EPS, ALU.mult, ALU.add))
            v.reciprocal(st[:, 32:48], st[:, 16:32]).then_inc(mg.inverse, 1)
            dve.wait_ge(mg.rstd, 1)
            for t in range(LT):
                o = GO[:, t, :].rearrange("p (h e) -> p h e", h=G_H)
                dve_after(v.tensor_tensor(o, o, st[:, 4 * t:4 * t + 4].unsqueeze(2).to_broadcast([P, G_H, G_DV]), ALU.mult))
                dve_after(v.tensor_tensor(o, o, ONORM[:, :].unsqueeze(1).to_broadcast([P, G_H, G_DV]), ALU.mult))
                v.tensor_tensor(GO[:, t, :], GO[:, t, :], OG[:, t, :], ALU.mult).then_inc(mg.scaled, 1)
            end(dve, "dve")
            begin(dve, "dve", 12)
            residual(1, LT)
            end(dve, "dve")
            begin(dve, "dve", 13)
            norm(1, 1, LT)
            route(1, LT)
            end(dve, "dve")
            begin(dve, "dve", 14)
            experts(1)
            end(dve, "dve")

        @block.scalar
        def _(act):
            a = nc.scalar.activation

            def norm(l, w, tiles):
                s = norm_s[(l, w)]
                for t in range(tiles):
                    act_after(a(sq_junk, H[:, t, :], ACT.Square, accum_out=STAT[:, 304 + t:305 + t]))
                    act.drain().then_inc(s.sumsq, 1)
                act.wait_ge(s.inverse, s.n.inverse + 1)
                a(MSR[:, 0:tiles], STAT[:, 8:8 + tiles], ACT.Sqrt).then_inc(s.rstd, 1)
                for u in range(tiles):
                    act.wait_ge(s.turned, s.n.turned + u + 1)
                    st = 0 if u < LT else 1
                    for k in range(4):
                        last = a(UT[:, k, u * P:(u + 1) * P], bank(2 * (u % 2))[:, k * P:(k + 1) * P], ACT.Identity,
                                 bias=MCOL[:, 3 * w * KD + k, st:st + 1], scale=ACOL[:, w, k, st:st + 1])
                    last.then_inc(s.evac_act, 1)

            def experts(l):
                s, n = moe[l], NSLOT[l]
                XT, HT, SIL, Y = xr(1024, KD, 96), xr(2816, KD, 96), xr(3584, D), xr(4608, D)
                a(STAT[:, 298:299], STAT[:, 304:305], ACT.Copy).then_inc(s.ht_act, 1)
                a(STAT[:, 299:300], STAT[:, 304:305], ACT.Copy).then_inc(s.y_act, 1)

                def modulate():
                    for k in range(4):
                        b = bank(6)[:, k * P:k * P + n]
                        for st, lo, hi in ((0, 0, CAP_L), (1, CAP_L, n))[:1 if n == CAP_L else 2]:
                            last = a(XT[:, k, lo:hi], b[:, lo:hi], ACT.Identity, bias=MCOL[:, 3 * KD + k, st:st + 1],
                                     scale=ACOL[:, 1, k, st:st + 1])
                    last.then_inc(s.xt_act, 1)

                act.wait_ge(s.x_turned, s.n.x_turned + 1)
                modulate()
                with act.Fori(0, E) as e:
                    wait_product(act, l, GATE, e)
                    a(SIL[0:n], bank(0, 2)[0:n], ACT.Silu).then_inc(s.silu, 1)
                    act.wait_ge(s.x_turned, s.n.x_turned + e + 2)
                    modulate()
                    act.wait_ge(s.h_turned, s.n.h_turned + e + 1)
                    a(HT[:, 0:4, 0:n], bank(6).rearrange("p (k t) -> p k t", t=P)[:, :, 0:n], ACT.Copy
                      ).then_inc(s.ht_act, 1)
                    act.wait_ge(s.routes, s.n.routes + e + 1)
                    wait_product(act, l, DOWN, e)
                    a(Y[0:n, 0:BW], bank(4)[0:n], ACT.Copy, scale=GCUR[0:n, :]).then_inc(s.y_act, 1)

            act.wait_ge(vec_cols, 1)
            a(SCT[:, 0], VCOL[:, 0, 64:80].rearrange("p (w k) -> p k w", w=2), ACT.Exp, scale=-1.0).then_inc(cond_exp, 1)
            end(act, "act")
            begin(act, "act", 1)
            act.wait_ge(h_loaded, 32)
            norm(0, 0, TT)
            end(act, "act")
            begin(act, "act", 2)
            act_units = [(c, t) for c in range(5) for t in range(TT)]

            def evac_heads(u):
                c, t = act_units[u]
                if c == 4:
                    return
                act.wait_ge(prj.turned, u + 1)
                b = bank(4 + u % 2)
                tok = slice(t * P, (t + 1) * P)
                for i, (col, num, dst, gain) in enumerate((
                        ((0, 4, 0, None),), ((0, 1, 4, None), (2, 2, 5, 0)), ((0, 2, 7, 0), (2, 2, 9, 1)), ((0, 2, 11, 1),))[c]):
                    src = b[:, col * P:(col + num) * P].rearrange("p (j x) -> p j x", x=P)
                    if gain is None:
                        last = a(QK[:, dst:dst + num, tok], src, ACT.Copy)
                    else:
                        last = a(QK[:, dst:dst + num, tok], src, ACT.Copy, scale=GB[:, gain:gain + 1])
                last.then_inc(prj.evac, 1)

            for u, (c, t) in enumerate(act_units):
                b = bank(u % 4)
                act.wait_ge(prj.product, u + 1)
                if c < 4:
                    if u >= 2:
                        act.wait_ge(prj.scaled, u - 1)
                    a(SQ[:, u % 2, :], b, ACT.Square).then_inc(prj.squares, 1)
                if c == 1:
                    a(V[:, t, 0:P], b[:, P:2 * P], ACT.Copy).then_inc(prj.v_out, 1)
                elif c == 3:
                    a(V[:, t, P:P + 256], b[:, 256:512], ACT.Copy).then_inc(prj.v_out, 1)
                elif c == 4:
                    a(V[:, t, P + 256:P + 512], b[:, 0:256], ACT.Copy).then_inc(prj.v_out, 1)
                else:
                    act.drain().then_inc(prj.v_out, 1)
                if c < 4:
                    act.wait_ge(prj.inverse, u + 1)
                    ph = PH[:, 24 * (u % 2):24 * (u % 2) + 24]
                    a(ph[:, 0:8], ph[:, 16:24], ACT.Sqrt).then_inc(prj.rstd, 1)
                if u:
                    evac_heads(u - 1)
            end(act, "act")
            begin(act, "act", 3)
            for i in range(1, BIAS_N, 2):
                act.wait_ge(bias_flipped, i + 1)
                a(BIAS[:, i * BW:(i + 1) * BW], bank(i % 4), ACT.Copy).then_inc(bias_evac_act, 1)
            N = len(heads)
            for i in range(N + 3):
                if i < N:
                    u = heads[i]
                    lo = 0 if u.t < LT else LAT
                    act.wait_ge(att.negmax, i + 1)
                    if i >= 3:
                        act.wait_ge(att.turned, i - 2)
                    a(PROB[:, i % 3, lo:TOK], bank(2 * (i % 2), 2)[:, lo:TOK], ACT.Exp, bias=SM[:, 3 + i % 3:4 + i % 3],
                      accum_out=SM[:, 6 + i % 3:7 + i % 3]).then_inc(att.probs, 1)
                j = i - 2
                if 0 <= j < N:
                    act.wait_ge(att.turned, j + 1)
                    if j >= 2:
                        act.wait_ge(att.mixed, j - 1)
                    if heads[j].t < LT:
                        a(PROBT[:, j % 2, 0:LAT], bank(4), ACT.Copy).then_inc(att.evac_act, 1)
                    else:
                        act.drain().then_inc(att.evac_act, 1)
                j = i - 3
                if 0 <= j < N:
                    u = heads[j]
                    act.wait_ge(att.mixed, j + 1)
                    a(UT[u.base:u.base + HD, u.mix, u.t * P:(u.t + 1) * P], bank(6 + j % 2)[u.base:u.base + HD, 0:P],
                      ACT.Copy).then_inc(att.evac_mix, 1)
            end(act, "act")
            begin(act, "act", 4)
            act.wait_ge(outp[0].gate_turned, 1)
            a(MROW[:, 0, :], bank(4, 2), ACT.Copy).then_inc(outp[0].gate_act, 1)
            end(act, "act")

            def route(l, tiles):
                s = rt[l]
                lg = xr(3400, TT, E)[:, 0:tiles]
                act.wait_ge(s.shifted, s.n.shifted + 1)
                a(lg, lg, ACT.Exp).then_inc(s.exps, 1)
                act.wait_ge(s.gate_turned, s.n.gate_turned + 1)
                a(MROW[:, 0, :], bank(0, 2), ACT.Copy).then_inc(s.gate_act, 1)

            begin(act, "act", 5)
            norm(0, 1, TT)
            route(0, TT)
            end(act, "act")
            begin(act, "act", 6)
            experts(0)
            end(act, "act")
            begin(act, "act", 7)
            end(act, "act")
            begin(act, "act", 8)
            norm(1, 0, TT)
            end(act, "act")
            begin(act, "act", 9)
            n_out = 0

            def out_bank():
                act.wait_ge(gp.product, n_out + 1)
                return bank(n_out % 4)

            for c in range(2):
                for j in range(G_H):
                    if c == 0:
                        a(GQ[:, j, :], out_bank(), ACT.Copy, scale=G_DK ** -0.5).then_inc(gp.evac_act, 1)
                        n_out += 1
                    else:
                        for lo, hi in ((0, LAT), (LAT, TOK)):
                            a(GK[:, j, lo:hi], out_bank()[:, 0:hi - lo], ACT.Copy).then_inc(gp.evac_act, 1)
                            n_out += 1
            for lo, hi in ((0, LAT), (LAT, TOK)):
                a(ZT[:, lo:hi], out_bank()[0:48, 0:hi - lo], ACT.Copy).then_inc(gp.evac_act, 1)
                n_out += 1
            for c in range(2, 4):
                for t in range(TT):
                    a(GV[:, t, (c - 2) * BW:(c - 1) * BW], out_bank(), ACT.Copy).then_inc(gp.evac_act, 1)
                    n_out += 1
            for c in range(4, 6):
                for t in range(LT):
                    a(OG[:, t, (c - 4) * BW:(c - 3) * BW], out_bank(), ACT.Silu).then_inc(gp.evac_act, 1)
                    n_out += 1
            for i, (d, j) in enumerate(gates):
                act.wait_ge(gp.raw, i + 1)
                bcol = VCOL[:, 1, 80 + 4 * d + j:81 + 4 * d + j]
                if i:
                    act.wait_ge(gp.cum, i)
                a(GLN, bank(4 + 2 * (i % 2), 2)[:, 0:TOK], ACT.Abs, bias=bcol).then_inc(gp.gate_abs, 1)
                act.wait_ge(gp.gate_abs, i + 1)
                a(GLN, GLN, ACT.Exp, scale=-1.0).then_inc(gp.gate_exp, 1)
                act.wait_ge(gp.gate_exp, i + 1)
                a(GLN, GLN, ACT.Ln, bias=1.0).then_inc(gp.gate_ln, 1)
            end(act, "act")
            begin(act, "act", 10)
            for h in range(G_H):
                for d in range(2):
                    L = lanes[d]
                    n = 2 * h + d
                    cum = CUM[d][:, h, :]
                    if h:
                        act.wait_ge(gs.kst, 2 * (h - 1) + d + 1)
                        act.wait_ge(gs.a_done, 2 * (h - 1) + d + 1)
                    a(L.TMP[:, 0:LAT], cum[:, 0:LAT], ACT.Exp, scale=1.0 / 16).then_inc(gs.e_pos, 1)
                    a(L.KI, cum[:, 0:LAT], ACT.Exp, scale=-1.0 / 16).then_inc(gs.e_neg, 1)
                    act.wait_ge(gs.diff, n + 1)
                    a(L.TMP, L.TMP, ACT.Exp, scale=1.0 / 16).then_inc(gs.e_diff, 1)
                for d in range(2):
                    L = lanes[d]
                    act.wait_ge(gs.kturned, 2 * h + d + 1)
                    a(L.KS, bank(4 * d, 2)[:, 0:TOK], ACT.Copy).then_inc(gs.kst_out, 1)
            end(act, "act")
            begin(act, "act", 11)
            for t in range(LT):
                for h in range(G_H):
                    a(xr(9216, G_DV), GO[:, t, h * G_DV:(h + 1) * G_DV], ACT.Square,
                      accum_out=STAT[:, 4 * t + h:4 * t + h + 1]).then_inc(mg.squares, 1)
                    act.wait_ge(mg.squares, 4 * t + h + 1)
            act.wait_ge(mg.inverse, 1)
            a(STAT[:, 0:16], STAT[:, 32:48], ACT.Sqrt).then_inc(mg.rstd, 1)
            for t in range(LT):
                act.wait_ge(mg.turned, t + 1)
                for n in range(2):
                    last = a(OT[:, 4 * n:4 * n + 4, t * P:(t + 1) * P],
                             bank(2 * (t % 2) + n).rearrange("p (k x) -> p k x", x=P), ACT.Copy)
                last.then_inc(mg.evac, 1)
            end(act, "act")
            begin(act, "act", 12)
            act.wait_ge(outp[1].gate_turned, 2)
            a(MROW[:, 0, :], bank(4, 2), ACT.Copy).then_inc(outp[1].gate_act, 1)
            end(act, "act")
            begin(act, "act", 13)
            norm(1, 1, LT)
            route(1, LT)
            end(act, "act")
            begin(act, "act", 14)
            experts(1)
            end(act, "act")

        @block.gpsimd
        def _(pool):
            g = nc.gpsimd

            def store_rows(l, tiles):
                s = norm_s[(l, 1)]
                for t in range(tiles):
                    pool.wait_ge(s.xhat, s.n.xhat + t + 1)
                    pool.dma_start(XH[l][t * P:(t + 1) * P, :], xhat[:, t % 2, :]).then_inc((s.stored0, s.stored1)[t % 2], 16)
                pool.wait_ge(s.stored0, s.n.stored0 + 16 * ((tiles + 1) // 2))
                pool.wait_ge(s.stored1, s.n.stored1 + 16 * (tiles // 2))

            def experts(l):
                s, n = moe[l], NSLOT[l]
                XG, Y, ZERO = xr(0, D), xr(4608, D), xr(5700, D)
                tiles = TT if l == 0 else LT
                pool_after(g.tensor_copy(IDXG[0:n, :], IDXT[0:n, 0:1]))
                pool.indirect_dma_start(XG[0:n, :], None, XH[l], bass.IndirectOffsetOnAxis(IDXG[0:n, 0:1], 0)
                                        ).then_inc(s.gathered, 16)
                pool.wait_ge(s.zeroed, s.n.zeroed + 1)
                for t in range(tiles):
                    pool.dma_start(ACC[l][t * P:(t + 1) * P, :], ZERO
                                   ).then_inc(acc_cleared[l] if t < tiles - 1 else s.scattered, 16)
                pool.wait_ge(acc_cleared[l], 16 * (tiles - 1))
                with pool.Fori(0, E) as e:
                    pool.wait_ge(s.x_turned, s.n.x_turned + e + 1)
                    pool.wait_ge(s.gathered, s.n.gathered + e * 16 + 16)
                    g.tensor_copy(IDXG[0:n, :], IDXT[0:n, bass.ds(e + 1, 1)]).then_inc(s.idx_next, 1)
                    pool.wait_ge(s.idx_next, s.n.idx_next + e + 1)
                    apart(pool)
                    pool.indirect_dma_start(XG[0:n, :], None, XH[l], bass.IndirectOffsetOnAxis(IDXG[0:n, 0:1], 0)
                                            ).then_inc(s.gathered, 16)
                    pool.wait_ge(s.scattered, s.n.scattered + e * 16 + 16)
                    g.tensor_copy(IDXS[0:n, :], IDXT[0:n, bass.ds(e, 1)])
                    g.tensor_copy(GCUR[0:n, :], GATET[0:n, bass.ds(e, 1)]).then_inc(s.routes, 1)
                    pool.wait_ge(s.routes, s.n.routes + e + 1)
                    pool.wait_ge(s.y_act, s.n.y_act + e + 2)
                    pool.wait_ge(s.y_dve, s.n.y_dve + e + 2)
                    apart(pool)
                    pool.indirect_dma_start(ACC[l], bass.IndirectOffsetOnAxis(IDXS[0:n, 0:1], 0), Y[0:n, :], None,
                                            compute_op=ALU.add).then_inc(s.scattered, 16)
                pool.wait_ge(s.scattered, s.n.scattered + 16 * (E + 1))
                pool.wait_ge(s.gathered, s.n.gathered + 16 * (E + 1))
                pool.wait_ge(s.h_turned, s.n.h_turned + E)
                buf = xr(0, 2, D)
                for t in range(tiles):
                    if t >= 2:
                        pool.wait_ge(s.added, s.n.added + t - 1)
                    pool.dma_start(buf[:, t % 2, :], ACC[l][t * P:(t + 1) * P, :]).then_inc((s.readback0, s.readback1)[t % 2], 16)

            pool_after(g.memset(WZ[:, :, :], 0.0))
            wv = A["gla_w_in"][0].rearrange("(k p) n -> p k n", p=P)
            pool.dma_start(WZ[:, :, 0:16], wv[:, :, 3072:3088]).then_inc(wz_loaded, 16)
            pool.dma_start(WZ[:, :, 32:48], wv[:, :, 3088:3104]).then_inc(wz_loaded, 16)
            pool.wait_ge(wz_loaded, 32)
            end(pool, "pool")
            for n in (1, 2):
                begin(pool, "pool", n)
                end(pool, "pool")
            begin(pool, "pool", 3)
            pool.wait_ge(bias_loaded, 16 * 2 * B_H)
            for half in range(2):
                b = BIAS[half * GRID_W:(half + 1) * GRID_W, :].rearrange("p (s c) -> p s c", c=GRID_W)
                w = GRID_W - NA_COLS
                pool_after(g.affine_select(out=b[:, :, 0:w], in_=b[:, :, 0:w], compare_op=ALU.is_ge, fill=MASKED,
                                           base=NA_COLS // 2 - (GRID_W - 1), pattern=[[0, B_H * NSH], [1, w]], channel_multiplier=1))
                pool_after(g.affine_select(out=b[:, :, NA_COLS:], in_=b[:, :, NA_COLS:], compare_op=ALU.is_ge, fill=MASKED,
                                           base=(GRID_W - 1) + NA_COLS // 2 - 1 - NA_COLS, pattern=[[0, B_H * NSH], [-1, w]],
                                           channel_multiplier=-1))
            pool.drain().then_inc(bias_masked, 1)
            end(pool, "pool")
            begin(pool, "pool", 4)
            end(pool, "pool")
            begin(pool, "pool", 5)
            store_rows(0, TT)
            end(pool, "pool")
            begin(pool, "pool", 6)
            experts(0)
            end(pool, "pool")
            for n in range(7, 13):
                begin(pool, "pool", n)
                end(pool, "pool")
            begin(pool, "pool", 13)
            store_rows(1, LT)
            end(pool, "pool")
            begin(pool, "pool", 14)
            experts(1)
            end(pool, "pool")


_INS = ["x", "c", "ctx", "c_ctx", "ada_w", "ada_b", "norm1_g", "norm2_g", "attn_w_in", "attn_w_out",
        "a_q_norm", "a_k_norm", "b_q_norm", "b_k_norm", "na_rpb", "gla_w_in", "gla_gk_w_f", "gla_gk_b_f",
        "gla_gk_w_b", "gla_gk_b_b", "gla_o_norm", "gla_w_out", "moe_router", "moe_w_gate", "moe_w_up", "moe_w_down"]


def kernel(**inputs):
    import numpy as _np
    import concourse.bacc as _bacc
    from concourse import mybir as _mybir
    from concourse.bass_utils import run_bass_kernel_spmd as _run

    nc = _bacc.Bacc("TRN2", target_bir_lowering=False, num_devices=1)
    arrays, args = {}, {}
    for name in _INS:
        a = _np.ascontiguousarray(inputs[name])
        arrays[f"in_{name}"] = a
        args[name] = nc.dram_tensor(f"in_{name}", a.shape, _mybir.dt.from_np(a.dtype), kind="ExternalInput").ap()
    a = shape_constants()
    arrays["in_shape_constants"] = a
    args["shape_constants"] = nc.dram_tensor("in_shape_constants", a.shape, _mybir.dt.from_np(a.dtype),
                                             kind="ExternalInput").ap()
    out = nc.dram_tensor("out_0", (LAT, D), _mybir.dt.float32, kind="ExternalOutput").ap()
    build(nc, args, out)
    r = _run(nc, [arrays], core_ids=[0])
    return r.results[0]["out_0"].reshape(1, LAT, D)
```

```python
from collections import namedtuple
from contextlib import ExitStack

import numpy as np
import concourse.bass as bass
from concourse import mybir

F32 = mybir.dt.float32
U32 = mybir.dt.uint32
I32 = mybir.dt.int32
ALU = mybir.AluOpType
ACT = mybir.ActivationFunctionType
X_AXIS = mybir.AxisListType.X


def named(**things):
    return namedtuple("Named", list(things))(**things)


P = 128
D = 1024
KD = D // P
LAT, CTX = 512, 256
TOK = LAT + CTX
LT, CT = LAT // P, CTX // P
TT = LT + CT
HD = 64
A_H, A_KV, B_H = 8, 2, 8
ATTN_IN = A_H * HD + 2 * A_KV * HD + 3 * B_H * HD
GRID_W, ROWS, NA_COLS = 64, LAT // 64, 16
DR, DC = 15, 31
E = 16
FF = 1024
CAP_L, CAP_C = 2 * LAT // E, 2 * CTX // E
G_H, G_DK, G_DV, CHUNK = 4, 128, 256, 64
EPS = 1e-6
MASKED = -1e30
BW = 512
SLOTS = 6
SLOT = 4096
NSH = DR - 1

C_ID, C_ROPE, C_MASKF, C_MASKB, C_RESET = 0, 128, 128 + LT * 128, 256 + LT * 128, 384 + LT * 128
C_FLIP = C_RESET + LAT
C_ALL = C_FLIP + P


def shape_constants():
    t = np.arange(LAT)
    half = HD // 2
    inv = (np.float32(10000.0) ** (-np.arange(0, half, 2, dtype=np.float32) / np.float32(half))).astype(np.float32)
    out = np.zeros((P, C_ALL), np.float32)
    out[:, C_ID:C_ID + P] = np.eye(P)
    tabs = []
    for pos in (t // GRID_W, t % GRID_W):
        ang = pos.astype(np.float32)[:, None] * inv[None, :]
        tabs.append((np.cos(ang), np.sin(ang)))
    cos = np.concatenate([tabs[0][0], tabs[0][0], tabs[1][0], tabs[1][0]], 1)
    sin = np.concatenate([-tabs[0][1], tabs[0][1], -tabs[1][1], tabs[1][1]], 1)
    rope = np.concatenate([cos, sin], 1).reshape(LT, P, 2 * HD).transpose(1, 0, 2)
    out[:, C_ROPE:C_ROPE + LT * P] = rope.reshape(P, LT * P)
    j, i = np.arange(P)[:, None], np.arange(P)[None, :]
    same = j // CHUNK == i // CHUNK
    out[:, C_MASKF:C_MASKF + P] = same & (i >= j)
    out[:, C_MASKB:C_MASKB + P] = same & (i <= j)
    out[:, C_RESET:C_RESET + LAT] = (t % CHUNK != 0)[None, :]
    out[:, C_FLIP:] = np.kron(np.eye(2), np.eye(GRID_W)[::-1])
    return out


def build(nc, A, out, stop=None):
    ctx = ExitStack()
    with ctx:
        def sb(name, shape, dt=F32):
            return ctx.enter_context(nc.sbuf_tensor(name, shape, dt))

        def sem(name):
            return ctx.enter_context(nc.semaphore(name))

        H = sb("H", [P, TT, D])
        UT = sb("UT", [P, KD, TOK])
        RING = sb("RING", [P, SLOTS, SLOT])
        CONST = sb("CONST", [P, C_ALL])
        VCOL = sb("VCOL", [P, 2, 88])
        SC = sb("SC", [P, KD, 2])
        SCT = sb("SCT", [P, 2, KD, 2])
        MCOL = sb("MCOL", [P, 2, 48, 2])
        ACOL = sb("ACOL", [P, 2, 2, KD, 2])
        MROW = sb("MROW", [P, 2, D])
        GA = sb("GA", [P, 2, HD])
        GB = sb("GB", [P, 2])
        RW = sb("RW", [P, 2, KD, E])
        ONORM = sb("ONORM", [P, G_DV])
        GKW = sb("GKW", [48, G_H * G_DK])
        WZ = sb("WZ", [P, KD, 48])
        STAT = sb("STAT", [P, 320])
        XR = sb("XR", [P, 9984])
        PS = ctx.enter_context(nc.psum_tensor("PS", [P, 8 * BW], F32))

        def bank(b, n=1):
            return PS[:, b * BW:(b + n) * BW]

        def xr(at, *shape):
            n = int(np.prod(shape))
            assert at + n <= 9984
            v = XR[:, at:at + n]
            return v if len(shape) == 1 else v.rearrange(
                "p (a b) -> p a b" if len(shape) == 2 else "p (a b c) -> p a b c",
                **dict(zip("abc", shape)))

        ident = CONST[:, C_ID:C_ID + P]

        RPB = nc.dram_tensor("rpb_scratch", (96 + B_H * DR * DC + 96,), F32, kind="Internal").ap()
        XH = [nc.dram_tensor(f"xhat_{l}", ((TOK, LAT)[l], D), F32, kind="Internal").ap() for l in range(2)]
        ACC = [nc.dram_tensor(f"moe_sum_{l}", ((TOK, LAT)[l], D), F32, kind="Internal").ap() for l in range(2)]

        ACT_CONSTS, POOL_CONSTS = 16 * 4, 16 * 16

        passed = sem("passed")

        plan = [(("ada", 0, c), c) for c in range(4)]
        plan += [(("win", c), c % 2) for c in range(5)]
        plan += [(("ada", l, c), 5) for l in range(2) for c in range(12) if (l, c) > (0, 3)]
        plan += [(("wout", 0, h), s) for h, s in enumerate((2, 5))]
        plan += [(("moe", 0, e, s), s) for e in range(E) for s in range(SLOTS)]
        plan += [(("gla", c), 3 + c % 3) for c in range(6)]
        plan += [(("wout", 1, h), s) for h, s in enumerate((5, 3))]
        plan += [(("moe", 1, e, s), s) for e in range(E) for s in range(SLOTS)]
        place, filled = {}, [0] * SLOTS
        for name, s in plan:
            place[name] = (s, filled[s])
            filled[s] += 1

        slot_full = [sem(f"slot_full{s}") for s in range(SLOTS)]
        slot_free = [sem(f"slot_free{s}") for s in range(SLOTS)]
        consts_loaded, small_loaded = sem("consts_loaded"), sem("small_loaded")
        engine_done = {k: sem(f"phase_done_{k}") for k in ("pe", "dve", "act", "pool")}

        def slot(name, k=KD):
            return RING[:, place[name][0], :].rearrange("p (k n) -> p k n", k=k)

        def wait_full(eng, name):
            s, n = place[name]
            eng.wait_ge(slot_full[s], 16 * (n + 1))

        GATE, UP, DOWN = 1, 3, 5

        def wait_product(eng, l, matrix, e):
            eng.wait_ge(slot_free[matrix], e + (place[("moe", l, 0, matrix)][1] + 1))

        def apart(eng):
            eng.sem_inc(passed, 1)

        def free(name):
            return slot_free[place[name][0]]

        def begin(eng, me, n):
            for k, s in engine_done.items():
                if k != me:
                    eng.wait_ge(s, n)

        def end(eng, me):
            eng.drain().then_inc(engine_done[me], 1)

        h_loaded = sem("h_loaded")
        bias_copied = sem("bias_copied")
        bias_loaded = sem("bias_loaded")
        bias_masked = sem("bias_masked")
        vec_loaded = sem("vec_loaded")
        bias_flipped, bias_evac_dve, bias_evac_act = sem("bias_flipped"), sem("bias_evac_dve"), sem("bias_evac_act")
        out_stored = sem("out_stored")
        dve_step, act_step, pool_step = sem("dve_step"), sem("act_step"), sem("pool_step")
        cond_ready, cond_exp = sem("cond_ready"), sem("cond_exp")
        steps = {"dve": 0, "act": 0, "pool": 0}

        def dve_after(ins):
            steps["dve"] += 1
            ins.then_inc(dve_step, 1)
            nc.vector.wait_ge(dve_step, steps["dve"])

        def act_after(ins):
            steps["act"] += 1
            ins.then_inc(act_step, 1)
            nc.scalar.wait_ge(act_step, steps["act"])

        def pool_after(ins):
            steps["pool"] += 1
            ins.then_inc(pool_step, 1)
            nc.gpsimd.wait_ge(pool_step, steps["pool"])

        def group(tag, *names):
            return named(**{n: sem(f"{n}_{tag}") for n in names})

        def uses(sems, counts):
            sems = sems._asdict()
            out, before = [], {k: 0 for k in sems}
            for c in counts:
                out.append(named(**sems, n=named(**before)))
                before = {k: before[k] + c[k] for k in before}
            return out

        ada_s = group("ada", "product", "rows", "turned", "cols")
        norm_s = dict(zip(((0, 0), (0, 1), (1, 0), (1, 1)), uses(
            group("norm", "sumsq", "inverse", "rstd", "xhat", "turned", "evac_act", "evac_dve", "stored0", "stored1"),
            [dict(sumsq=t, inverse=1, rstd=1, xhat=t, turned=t, evac_act=t, evac_dve=t, stored0=8 * t * w,
                  stored1=8 * t * w) for t, w in ((TT, 0), (TT, 1), (TT, 0), (LT, 1))])))
        prj = group("prj", "product", "squares", "inverse", "rstd", "v_out", "scaled", "stage",
                    "turned", "evac")
        att = group("att", "scores", "biased", "negmax", "probs", "normal", "turned", "evac_act",
                    "evac_dve", "mixed", "evac_mix")
        outp = uses(group("out", "gate_turned", "gate_act", "product", "added"),
                    [dict(gate_turned=1, gate_act=1, product=t, added=t) for t in (TT, LT)])
        routing = ("logits", "shifted", "exps", "aff", "turned", "packed", "routed", "gate_turned", "gate_act")
        rt = uses(group("route", *routing), [dict.fromkeys(routing, 1)] * 2)
        once = ("silu", "hidden", "h_turned", "routes", "idx_next")
        ahead = ("x_turned", "xt_act", "xt_dve", "ht_act", "ht_dve", "y_act", "y_dve")
        moe = uses(group("moe", "zeroed", "gathered", "scattered", "readback0", "readback1", "added", *once, *ahead),
                   [dict(zeroed=1, gathered=16 * (E + 1), scattered=16 * (E + 1), readback0=8 * t, readback1=8 * t,
                         added=t, **dict.fromkeys(once, E), **dict.fromkeys(ahead, E + 1)) for t in (TT, LT)])
        gp = group("gp", "product", "evac_act", "z_out", "gate_x", "gate_abs", "gate_exp", "gate_ln", "cum", "raw")
        gs = group("gs", "e_pos", "e_neg", "diff", "e_diff", "qdec", "kinv", "kst", "kturned", "kst_out",
                   "s0", "s0_out", "a_done", "a_out", "upd", "state", "o_done", "o_out")
        mg = group("mg", "squares", "inverse", "rstd", "scaled", "turned", "evac")

        block = ctx.enter_context(nc.Block())

        wout_a2 = sem("wout_a2")
        wz_loaded = sem("wz_loaded")
        acc_cleared = [sem(f"moe_sum_cleared{l}") for l in range(2)]
        IDXT, GATET = sb("IDXT", [96, E + 1], I32), sb("GATET", [96, E])
        IDXG, IDXS, GCUR = sb("IDXG", [96, 1], I32), sb("IDXS", [96, 1], I32), sb("GCUR", [96, 1])

        NSLOT = [CAP_L + CAP_C, CAP_L]

        def ada_steps(l, vectors):
            return [x for v in vectors for x in (("chunk", l, 2 * v), ("chunk", l, 2 * v + 1), ("turn", l, v))]

        ada_at = {(0, i): [x] for i, x in enumerate(ada_steps(0, (0, 1)))}
        ada_at |= {(2, 2 * i + 1): [x] for i, x in enumerate(ada_steps(0, (2, 3, 4, 5)))}
        ada_at |= {(3, 5 * i + 3): [x] for i, x in enumerate(ada_steps(1, range(6)))}
        ADA_ROWS = XR[0:2, 7800:8824]

        V = xr(0, TT, (A_KV + B_H) * HD)
        QK_A = RING[:, 2, 0:5 * TOK].rearrange("p (j t) -> p j t", j=5)
        QK_B = RING[:, 3:5, :].rearrange("p s n -> p (s n)")[:, 0:8 * TOK].rearrange("p (j t) -> p j t", j=8)

        def qk(j, n=1):
            return QK_A[:, j:j + n] if j < 5 else QK_B[:, j - 5:j - 5 + n]

        BIAS = RING[:, 0:2, :].rearrange("p s n -> p (s n)")[:, 0:B_H * NSH * GRID_W]
        BIAS_N = B_H * NSH * GRID_W // BW
        PROB = xr(3840, 3, TOK)
        PROBT = xr(3840 + 3 * TOK, 2, TOK)
        SQ = xr(3840, 2, BW)
        STAGE = xr(3840 + 1024, 2, BW)
        ROT = xr(3840 + 2048, BW)
        STAGE2 = xr(3840 + 2560, 2, BW)
        heads = [named(head=h, t=t, base=HD * (h // 4), q=h % 4, k=4, v=0, mix=h % 4, biased=False)
                 for h in range(A_H) for t in range(TT)]
        N_A = len(heads)
        heads += [named(head=h, t=t, base=HD * (h % 2), q=5 + h // 2, k=9 + h // 2, v=P + (h // 2) * P, mix=4 + h // 2,
                        biased=t < LT) for h in range(B_H) for t in range(TT)]
        ring012 = RING[:, 0:3, :].rearrange("p s n -> p (s n)")
        GV = ring012[:, 0:TT * D].rearrange("p (t n) -> p t n", t=TT)
        OG = ring012[:, TT * D:(TT + LT) * D].rearrange("p (t n) -> p t n", t=LT)
        GQ = ring012[:, (TT + LT) * D:].rearrange("p (j n) -> p j n", j=G_H)
        GK = xr(0, G_H, TOK)
        CUM = [xr(3072, G_H, TOK), xr(6144, G_H, TOK)]
        GLN, ZT = MROW[:, 0, 0:TOK], MROW[0:48, 1, 0:TOK]
        GO = UT[:, :, :].rearrange("p k t -> p (k t)")[:, 0:LT * D].rearrange("p (t n) -> p t n", t=LT)
        OT = RING[:, 4, :].rearrange("p (k t) -> p k t", k=KD)
        gates = [(d, j) for d in range(2) for j in range(G_H)]

        def lane(d):
            r = RING[:, 3 + d, :]
            return named(QZ=r[:, 0:1024], TMP=r[:, 1024:1792], KI=r[:, 1792:2304], KS=r[:, 2304:3072],
                         AT=r[:, 3072:3584], S=r[:, 3584:4096].rearrange("p (b e) -> p b e", b=2),
                         DEC=STAT[:, 80 + 8 * d:88 + 8 * d],
                         qz=lambda t, eo: r[:, (2 * t + eo) * P:(2 * t + eo + 1) * P],
                         qview=lambda t: r[:, 2 * t * P:2 * t * P + 384].rearrange("p (e x) -> p e x", e=2)[:, :, 0:CHUNK])

        lanes = [lane(0), lane(1)]

        def lane_o(h, d, pair):
            return 2 * LT * h + 2 * pair + d + 1

        def lane_state(h, d, i):
            return 2 * (2 * LT - 1) * h + 2 * i + d + 1

        def by_slice(row):
            return row.rearrange("p (x k) -> p k x", k=KD)

        MSR = STAT[:, 0:16]
        PH = STAT[:, 16:64]
        SM = STAT[:, 64:80]
        xhat = xr(0, TT, D)
        sq_junk = xr(6144, D)

        @block.sync
        def _(sp):
            sp.dma_start(H[:, 0:LT, :], A["x"][0].rearrange("(t p) d -> p t d", p=P)).then_inc(h_loaded, 16)

            def load(name, src, dst=None):
                s, n = place[name]
                if n:
                    sp.wait_ge(slot_free[s], n)
                sp.dma_start(slot(name) if dst is None else dst, src).then_inc(slot_full[s], 16)

            def load_ada(l, c):
                load(("ada", l, c), A["ada_w"][l].rearrange("(p k) n -> p k n", p=P)[:, :, c * BW:(c + 1) * BW])

            def after_phase(n):
                for done in engine_done.values():
                    sp.wait_ge(done, n)

            def load_experts(l, ready):
                w3 = [A[w][l].rearrange("e (p k) n -> p e k n", p=P)
                      for w in ("moe_w_gate", "moe_w_up", "moe_w_down")]

                def half_matrix(s, e):
                    return w3[s // 2][:, bass.ds(e, 1) if not isinstance(e, int) else slice(e, e + 1),
                                      4 * (s % 2):4 * (s % 2) + 4, :].rearrange("p e k n -> p (e k) n")

                for s, wait in ready:
                    wait()
                    sp.wait_ge(slot_free[s], place[("moe", l, 0, s)][1])
                    sp.dma_start(RING[:, s, :].rearrange("p (k n) -> p k n", k=4), half_matrix(s, 0)).then_inc(slot_full[s], 16)
                with sp.Fori(1, E) as e:
                    for s in range(SLOTS):
                        sp.wait_ge(slot_free[s], e + place[("moe", l, 0, s)][1])
                        sp.dma_start(RING[:, s, :].rearrange("p (k n) -> p k n", k=4), half_matrix(s, e)
                                     ).then_inc(slot_full[s], 16)

            def load_win(c):
                lo, hi = c * BW, min((c + 1) * BW, ATTN_IN)
                load(("win", c), A["attn_w_in"][0].rearrange("(p k) n -> p k n", p=P)[:, :, lo:hi],
                     slot(("win", c))[:, :, 0:hi - lo])

            for c in range(2):
                load_ada(0, c)
            sp.dma_start(H[:, LT:TT, :], A["ctx"][0].rearrange("(t p) d -> p t d", p=P)).then_inc(h_loaded, 16)
            for c in range(2, 4):
                load_ada(0, c)
            for c in (0, 1):
                load_win(c)
            for i, c in enumerate(range(4, 12)):
                load_ada(0, c)
                if i in (1, 3, 5):
                    load_win(2 + i // 2)
            load_ada(1, 0)
            after_phase(3)
            sp.wait_ge(bias_copied, 48)
            for half in range(2):
                for h in range(B_H):
                    src = bass.AP(RPB.tensor, 96 + h * DR * DC + (1 - half) * DC + NA_COLS - GRID_W,
                                  [[1, GRID_W], [DC, NSH], [1, GRID_W]])
                    sp.dma_start(BIAS[half * GRID_W:(half + 1) * GRID_W, h * NSH * GRID_W:(h + 1) * NSH * GRID_W]
                                 .rearrange("p (s c) -> p s c", s=NSH), src).then_inc(bias_loaded, 16)
            for c in range(1, 9):
                load_ada(1, c)
            sp.wait_ge(att.scores, N_A)
            dst = RING[:, place[("wout", 0, 0)][0], :].rearrange("p (k n) -> p k n", k=4)
            for a, arrived in enumerate((slot_full[place[("wout", 0, 0)][0]], wout_a2)):
                sp.dma_start(dst[a * HD:(a + 1) * HD],
                             A["attn_w_out"][0][a * 256:(a + 1) * 256, :].rearrange("(j p) n -> p j n", p=HD)
                             ).then_inc(arrived, 16)
            for c in range(9, 12):
                load_ada(1, c)

            load(("wout", 0, 1), A["attn_w_out"][0][512:1024, :].rearrange("(k p) n -> p k n", p=P),
                 slot(("wout", 0, 1), 4))
            load_experts(0, [(s, {0: lambda: sp.wait_ge(att.biased, B_H * LT),
                                  3: lambda: after_phase(4)}.get(s, lambda: None)) for s in (0, 1, 3, 4, 2, 5)])
            w = A["gla_w_in"][0].rearrange("(p k) n -> p k n", p=P)
            for c in range(6):
                load(("gla", c), w[:, :, c * BW:(c + 1) * BW])
            after_phase(11)
            for h in range(2):
                load(("wout", 1, h), A["gla_w_out"][0][h * 512:(h + 1) * 512, :].rearrange("(k p) n -> p k n", p=P),
                     slot(("wout", 1, h), 4))
            load_experts(1, [(s, {0: lambda: after_phase(12),
                                  4: lambda: after_phase(13)}.get(s, lambda: None)) for s in (0, 1, 2, 5, 3, 4)])
            after_phase(15)
            sp.dma_start(out.rearrange("(t p) d -> p t d", p=P), H[:, 0:LT, :]).then_inc(out_stored, 16)
            sp.wait_ge(out_stored, 16)

        @block.tensor
        def _(pe):
            mm = nc.tensor.matmul

            def ada(where):
                for what, l, i in ada_at.get(where, ()):
                    if what == "chunk":
                        g = 12 * l + i
                        wait_full(pe, ("ada", l, i))
                        if g:
                            pe.wait_ge(ada_s.rows, g)
                        if g % 2 == 0 and g:
                            pe.wait_ge(ada_s.cols, g // 2)
                        for k in range(KD):
                            last = mm(bank(7)[0:2, :], SC[:, k, :], slot(("ada", l, i))[:, k, :],
                                      start=(k == 0), stop=(k == KD - 1))
                        last.then_inc(ada_s.product, 1)
                        pe.drain().then_inc(free(("ada", l, i)), 1)
                    else:
                        pe.wait_ge(ada_s.rows, 12 * l + 2 * i + 2)
                        for k in range(KD):
                            last = nc.tensor.transpose(bank(7)[:, 2 * k:2 * k + 2], ADA_ROWS[:, k::KD], ident[0:2, 0:2])
                        last.then_inc(ada_s.turned, 1)

            def norm_turn(l, w, tiles):
                s = norm_s[(l, w)]

                def logits(t):
                    pe.wait_ge(s.evac_act, s.n.evac_act + t + 1)
                    pe.wait_ge(s.evac_dve, s.n.evac_dve + t + 1)
                    for k in range(KD):
                        last = mm(bank(4)[:, t * E:(t + 1) * E], UT[:, k, t * P:(t + 1) * P], RW[:, l, k, :],
                                  start=(k == 0), stop=(k == KD - 1))
                    if t == tiles - 1:
                        last.then_inc(rt[l].logits, 1)

                for t in range(tiles):
                    if w and t:
                        logits(t - 1)
                    pe.wait_ge(s.xhat, s.n.xhat + t + 1)
                    if t >= 2:
                        pe.wait_ge(s.evac_act, s.n.evac_act + t - 1)
                        pe.wait_ge(s.evac_dve, s.n.evac_dve + t - 1)
                    for k in range(KD):
                        last = nc.tensor.transpose(bank(2 * (t % 2) + k // 4)[:, (k % 4) * P:(k % 4 + 1) * P],
                                                   xhat[:, t, k::KD], ident)
                    last.then_inc(s.turned, 1)
                if w:
                    logits(tiles - 1)

            def gate_rows(s, l, vec, b0):
                for w in range(2):
                    for k in range(KD):
                        last = mm(bank(b0 + 2 * w + k // 4)[:, (k % 4) * P:(k % 4 + 1) * P],
                                  MCOL[:, l, vec * KD + k, w:w + 1].to_broadcast([P, P]), ident, start=True, stop=True)
                last.then_inc(s.gate_turned, 1)

            def out_projection(l, tiles, MIXT):
                s = outp[l]
                gate_rows(s, l, 2, 4)
                wait_full(pe, ("wout", l, 0))
                if l == 0:
                    pe.wait_ge(wout_a2, 16)
                wait_full(pe, ("wout", l, 1))
                for t in range(tiles):
                    if t >= 2:
                        pe.wait_ge(s.added, s.n.added + t - 1)
                    for n in range(2):
                        for k in range(KD):
                            wv = RING[:, place[("wout", l, k // 4)][0], :].rearrange("p (k n) -> p k n", k=4)
                            last = mm(bank(2 * (t % 2) + n), MIXT[:, k, t * P:(t + 1) * P],
                                      wv[:, k % 4, n * BW:(n + 1) * BW], start=(k == 0), stop=(k == KD - 1))
                    last.then_inc(s.product, 1)
                pe.drain().then_inc(free(("wout", l, 0)), 1)
                pe.drain().then_inc(free(("wout", l, 1)), 1)

            def route(l, tiles):
                s = rt[l]
                gate_rows(s, l, 5, 0)
                pe.wait_ge(s.aff, s.n.aff + 1)
                for t in range(tiles):
                    last = nc.tensor.transpose(bank(5 + t // 4)[0:48, (t % 4) * P:(t % 4 + 1) * P],
                                               xr(7300, TT, 48)[:, t, :], ident)
                last.then_inc(s.turned, 1)
                pe.wait_ge(s.packed, s.n.packed + 1)
                n = NSLOT[l]
                for i in range(2):
                    last = nc.tensor.transpose(bank(4)[0:n, 128 + i * E:128 + (i + 1) * E],
                                               STAT[0:E, 96 + i * 96:96 + i * 96 + n], ident[0:E, 0:E])
                last.then_inc(s.routed, 1)

            def experts(l):
                s, n = moe[l], NSLOT[l]
                XG, XT, HID, HT = xr(0, D), xr(1024, KD, 96), xr(1792, D), xr(2816, KD, 96)

                def turn_rows(src, done):
                    for k in range(KD):
                        last = nc.tensor.transpose(bank(6 + k // 4)[:, (k % 4) * P:(k % 4) * P + n],
                                                   src[0:n, k::KD], ident[0:n, 0:n])
                    last.then_inc(done, 1)

                pe.wait_ge(s.gathered, s.n.gathered + 16)
                turn_rows(XG, s.x_turned)
                with pe.Fori(0, E) as e:
                    pe.wait_ge(s.xt_act, s.n.xt_act + e + 1)
                    pe.wait_ge(s.xt_dve, s.n.xt_dve + e + 1)
                    for sl in range(4):
                        pe.wait_ge(slot_full[sl], e * 16 + 16 * (place[("moe", l, 0, sl)][1] + 1))
                        w = RING[:, sl, :].rearrange("p (k n) -> p k n", k=4)
                        for k in range(4):
                            for nn in range(2):
                                last = mm(bank(2 * (sl // 2) + nn)[0:n, :], XT[:, (sl % 2) * 4 + k, 0:n],
                                          w[:, k, nn * BW:(nn + 1) * BW], start=(sl % 2 == 0 and k == 0),
                                          stop=(sl % 2 == 1 and k == 3))
                        last.then_inc(slot_free[sl], 1)
                    pe.wait_ge(s.gathered, s.n.gathered + e * 16 + 32)
                    pe.wait_ge(s.ht_act, s.n.ht_act + e + 1)
                    pe.wait_ge(s.ht_dve, s.n.ht_dve + e + 1)
                    apart(pe)
                    turn_rows(XG, s.x_turned)
                    pe.wait_ge(s.hidden, s.n.hidden + e + 1)
                    pe.wait_ge(s.xt_act, s.n.xt_act + e + 2)
                    pe.wait_ge(s.xt_dve, s.n.xt_dve + e + 2)
                    apart(pe)
                    turn_rows(HID, s.h_turned)
                    pe.wait_ge(s.ht_act, s.n.ht_act + e + 2)
                    pe.wait_ge(s.ht_dve, s.n.ht_dve + e + 2)
                    pe.wait_ge(s.y_act, s.n.y_act + e + 1)
                    pe.wait_ge(s.y_dve, s.n.y_dve + e + 1)
                    for sl in range(4, 6):
                        pe.wait_ge(slot_full[sl], e * 16 + 16 * (place[("moe", l, 0, sl)][1] + 1))
                        w = RING[:, sl, :].rearrange("p (k n) -> p k n", k=4)
                        for k in range(4):
                            for nn in range(2):
                                last = mm(bank(4 + nn)[0:n, :], HT[:, (sl - 4) * 4 + k, 0:n],
                                          w[:, k, nn * BW:(nn + 1) * BW], start=(sl == 4 and k == 0),
                                          stop=(sl == 5 and k == 3))
                        last.then_inc(slot_free[sl], 1)

            pe.wait_ge(consts_loaded, ACT_CONSTS)
            pe.wait_ge(small_loaded, POOL_CONSTS)
            pe.wait_ge(cond_ready, 1)
            for i in range(6):
                ada((0, i))
            end(pe, "pe")
            begin(pe, "pe", 1)
            norm_turn(0, 0, TT)
            end(pe, "pe")
            begin(pe, "pe", 2)
            units = [(c, t) for c in range(5) for t in range(TT)]

            def turn_heads(u):
                c, t = units[u]
                if c == 4:
                    return
                pe.wait_ge(prj.stage, u + 1)
                if u >= 2:
                    pe.wait_ge(prj.evac, u - 1)
                src = STAGE2[:, u % 2, :] if c < 2 else STAGE[:, u % 2, :]
                for cols in ((0, 1, 2, 3), (0, 2, 3), (0, 1, 2, 3), (0, 1))[c]:
                    last = nc.tensor.transpose(bank(4 + u % 2)[:, cols * P:(cols + 1) * P],
                                               src[:, cols * P:(cols + 1) * P], ident)
                last.then_inc(prj.turned, 1)

            for u, (c, t) in enumerate(units):
                w = min(BW, ATTN_IN - c * BW)
                if t == 0:
                    wait_full(pe, ("win", c))
                if u >= 4:
                    pe.wait_ge(prj.scaled, u - 3)
                    pe.wait_ge(prj.v_out, u - 3)
                for k in range(KD):
                    last = mm(bank(u % 4)[:, 0:w], UT[:, k, t * P:(t + 1) * P], slot(("win", c))[:, k, 0:w],
                              start=(k == 0), stop=(k == KD - 1))
                last.then_inc(prj.product, 1)
                if t == TT - 1:
                    pe.drain().then_inc(free(("win", c)), 1)
                if u:
                    turn_heads(u - 1)
                ada((2, u))
            end(pe, "pe")
            begin(pe, "pe", 3)
            def attend(first, N):
                for i in range(first, N + 3):
                    if i < N:
                        u = heads[i]
                        if i >= 2:
                            pe.wait_ge(att.probs, i - 1)
                        q = qk(u.q)[u.base:u.base + HD, 0, u.t * P:(u.t + 1) * P]
                        key = qk(u.k)[u.base:u.base + HD, 0]
                        b0 = 2 * (i % 2)
                        if u.t < LT:
                            mm(bank(b0), q, key[:, 0:LAT], start=True, stop=True)
                        mm(bank(b0 + 1)[:, 0:CTX], q, key[:, LAT:TOK], start=True, stop=True).then_inc(att.scores, 1)
                        ada((3, i))
                    j = i - 2
                    if first <= j < N:
                        u = heads[j]
                        pe.wait_ge(att.normal, j + 1)
                        if j >= 1:
                            pe.wait_ge(att.evac_act, j)
                            pe.wait_ge(att.evac_dve, j)
                        for kt in range(0 if u.t < LT else LT, TT):
                            last = nc.tensor.transpose(bank(4 + kt // 4)[:, (kt % 4) * P:(kt % 4 + 1) * P],
                                                       PROB[:, j % 3, kt * P:(kt + 1) * P], ident)
                        last.then_inc(att.turned, 1)
                    j = i - 3
                    if first <= j < N:
                        u = heads[j]
                        pe.wait_ge(att.evac_act, j + 1)
                        pe.wait_ge(att.evac_dve, j + 1)
                        if j >= 1:
                            pe.wait_ge(att.evac_mix, j)
                        kts = range(0 if u.t < LT else LT, TT)
                        for kt in kts:
                            last = mm(bank(6)[:, 0:P], V[:, kt, u.v:u.v + P],
                                      PROBT[:, j % 2, kt * P:(kt + 1) * P], start=(kt == kts[0]), stop=(kt == TT - 1))
                        last.then_inc(att.mixed, 1)

            attend(0, N_A)
            pe.wait_ge(bias_masked, 1)
            pe.wait_ge(att.probs, N_A)
            for i in range(BIAS_N):
                if i >= 4:
                    pe.wait_ge((bias_evac_dve, bias_evac_act)[i % 2], i // 2 - 1)
                mm(bank(i % 4), CONST[:, C_FLIP:C_FLIP + P], BIAS[:, i * BW:(i + 1) * BW], start=True, stop=True
                   ).then_inc(bias_flipped, 1)
            pe.wait_ge(bias_evac_dve, BIAS_N // 2)
            pe.wait_ge(bias_evac_act, BIAS_N // 2)
            attend(N_A, len(heads))
            end(pe, "pe")
            begin(pe, "pe", 4)
            out_projection(0, TT, UT)
            end(pe, "pe")
            begin(pe, "pe", 5)
            norm_turn(0, 1, TT)
            route(0, TT)
            end(pe, "pe")
            begin(pe, "pe", 6)
            experts(0)
            end(pe, "pe")
            begin(pe, "pe", 7)
            end(pe, "pe")
            begin(pe, "pe", 8)
            norm_turn(1, 0, TT)
            end(pe, "pe")
            begin(pe, "pe", 9)
            n_out = [0]

            def next_bank():
                i = n_out[0]
                if i >= 4:
                    pe.wait_ge(gp.evac_act, i - 3)
                n_out[0] += 1
                return bank(i % 4)

            for c in range(2):
                wait_full(pe, ("gla", c))
                for j in range(G_H):
                    for lo, hi in ((0, LAT), (LAT, TOK))[:1 + c]:
                        b = next_bank()
                        for k in range(KD):
                            last = mm(b[:, 0:hi - lo], slot(("gla", c))[:, k, j * P:(j + 1) * P], UT[:, k, lo:hi],
                                      start=(k == 0), stop=(k == KD - 1))
                        last.then_inc(gp.product, 1)
                pe.drain().then_inc(free(("gla", c)), 1)
            for lo, hi in ((0, LAT), (LAT, TOK)):
                b = next_bank()
                for k in range(KD):
                    last = mm(b[0:48, 0:hi - lo], WZ[:, k, :], UT[:, k, lo:hi], start=(k == 0), stop=(k == KD - 1))
                last.then_inc(gp.product, 1)
            for c in range(2, 6):
                wait_full(pe, ("gla", c))
                for t in range(TT if c < 4 else LT):
                    b = next_bank()
                    for k in range(KD):
                        last = mm(b, UT[:, k, t * P:(t + 1) * P], slot(("gla", c))[:, k, :],
                                  start=(k == 0), stop=(k == KD - 1))
                    last.then_inc(gp.product, 1)
                pe.drain().then_inc(free(("gla", c)), 1)
            pe.wait_ge(gp.evac_act, n_out[0])
            for i, (d, j) in enumerate(gates):
                b0 = 4 + 2 * (i % 2)
                if i >= 2:
                    pe.wait_ge(gp.gate_x, i - 1)
                    pe.wait_ge(gp.gate_abs, i - 1)
                for lo, hi in ((0, LAT), (LAT, TOK)):
                    last = mm(bank(b0, 2)[:, lo:hi], GKW[32 * d:32 * d + 16, j * P:(j + 1) * P],
                              ZT[32 * d:32 * d + 16, lo:hi], start=True, stop=True)
                last.then_inc(gp.raw, 1)
            end(pe, "pe")
            begin(pe, "pe", 10)
            for h in range(G_H):
                for d in range(2):
                    L = lanes[d]
                    n = 2 * h + d
                    b0 = 4 * d
                    pe.wait_ge(gs.kst, n + 1)
                    if h:
                        pe.wait_ge(gs.o_out, lane_o(h - 1, d, LT - 1))
                    for t in range(TT):
                        last = nc.tensor.transpose(bank(b0 + t // 4)[:, (t % 4) * P:(t % 4 + 1) * P],
                                                   L.KS[:, t * P:(t + 1) * P], ident)
                    last.then_inc(gs.kturned, 1)
                for d in range(2):
                    L = lanes[d]
                    n = 2 * h + d
                    b0 = 4 * d
                    pe.wait_ge(gs.kst_out, n + 1)
                    for i in range(CT):
                        last = mm(bank(b0 + 2)[:, 0:G_DV], L.KS[:, (LT + i) * P:(LT + i + 1) * P],
                                  GV[:, LT + i, h * G_DV:(h + 1) * G_DV], start=(i == 0), stop=(i == CT - 1))
                    last.then_inc(gs.s0, 1)
                    pe.wait_ge(gs.qdec, n + 1)
                    pe.wait_ge(gs.kinv, n + 1)
                    for t in range(LT):
                        last = mm(bank(b0)[:, t * P:(t + 1) * P], L.KI[:, t * P:(t + 1) * P], L.qview(t),
                                  start=True, stop=True)
                    last.then_inc(gs.a_done, 1)
                for d in range(2):
                    n = 2 * h + d
                    pe.wait_ge(gs.a_out, n + 1)
                    pe.wait_ge(gs.s0_out, n + 1)
                for i in range(2 * LT):
                    for d in range(2):
                        L = lanes[d]
                        b0 = 4 * d
                        c = i if d == 0 else 2 * LT - 1 - i
                        t, eo = c // 2, c % 2
                        ob = bank(b0 + 1 + 2 * ((i // 2) % 2))[:, 0:G_DV]
                        v = GV[:, t, h * G_DV:(h + 1) * G_DV]
                        if i % 2 == 0:
                            if i >= 4:
                                pe.wait_ge(gs.o_out, lane_o(h, d, i // 2 - 2))
                            mm(ob, L.AT[:, t * P:(t + 1) * P], v, start=True, stop=False)
                        if i:
                            pe.wait_ge(gs.state, lane_state(h, d, i - 1))
                        last = mm(ob, L.qz(t, eo), L.S[:, i % 2, :], start=False, stop=(i % 2 == 1))
                        if i % 2:
                            last.then_inc(gs.o_done, 1)
                        if i < 2 * LT - 1:
                            half = slice(eo * CHUNK, (eo + 1) * CHUNK)
                            mm(bank(b0 + 2)[:, 256:512], L.KS[half, t * P:(t + 1) * P],
                               GV[half, t, h * G_DV:(h + 1) * G_DV], start=True, stop=True).then_inc(gs.upd, 1)
            end(pe, "pe")
            begin(pe, "pe", 11)
            for t in range(LT):
                pe.wait_ge(mg.scaled, t + 1)
                if t >= 2:
                    pe.wait_ge(mg.evac, t - 1)
                for k in range(KD):
                    last = nc.tensor.transpose(bank(2 * (t % 2) + k // 4)[:, (k % 4) * P:(k % 4 + 1) * P],
                                               GO[:, t, k * P:(k + 1) * P], ident)
                last.then_inc(mg.turned, 1)
            end(pe, "pe")
            begin(pe, "pe", 12)
            out_projection(1, LT, OT)
            end(pe, "pe")
            begin(pe, "pe", 13)
            norm_turn(1, 1, LT)
            route(1, LT)
            end(pe, "pe")
            begin(pe, "pe", 14)
            experts(1)
            end(pe, "pe")

        @block.vector
        def _(dve):
            v = nc.vector

            def ada(where):
                for what, l, i in ada_at.get(where, ()):
                    if what == "turn":
                        dve.wait_ge(ada_s.turned, 6 * l + i + 1)
                        v.tensor_tensor(MCOL[:, l, i * KD:(i + 1) * KD, :],
                                        bank(7)[:, 0:16].rearrange("p (k w) -> p k w", w=2),
                                        VCOL[:, l, i * KD:(i + 1) * KD].unsqueeze(2).to_broadcast([P, KD, 2]),
                                        ALU.add).then_inc(ada_s.cols, 1)
                        if i in (1, 4):
                            dve.wait_ge(ada_s.cols, 6 * l + i + 1)
                            at = 48 + KD * (i // 3)
                            v.scalar_tensor_tensor(out=ACOL[:, l, i // 3], in0=MCOL[:, l, i * KD:(i + 1) * KD, :], scalar=1.0,
                                                   in1=VCOL[:, l, at:at + KD].unsqueeze(2).to_broadcast([P, KD, 2]),
                                                   op0=ALU.add, op1=ALU.mult)

            def norm(l, w, tiles):
                s = norm_s[(l, w)]
                dve.wait_ge(s.sumsq, s.n.sumsq + tiles)
                dve_after(v.tensor_scalar(MSR[:, 0:tiles], STAT[:, 304:304 + tiles], 1.0 / D, EPS, ALU.mult, ALU.add))
                v.reciprocal(STAT[:, 8:8 + tiles], MSR[:, 0:tiles]).then_inc(s.inverse, 1)
                dve.wait_ge(s.rstd, s.n.rstd + 1)
                for t in range(tiles + 1):
                    if t < tiles:
                        v.tensor_scalar(xhat[:, t, :], H[:, t, :], MSR[:, t:t + 1], None, ALU.mult).then_inc(s.xhat, 1)
                    if t:
                        u = t - 1
                        dve.wait_ge(s.turned, s.n.turned + u + 1)
                        st = 0 if u < LT else 1
                        for k in range(4, KD):
                            last = v.tensor_scalar(UT[:, k, u * P:(u + 1) * P],
                                                   bank(2 * (u % 2) + 1)[:, (k - 4) * P:(k - 3) * P],
                                                   ACOL[:, l, w, k, st:st + 1], MCOL[:, l, 3 * w * KD + k, st:st + 1],
                                                   ALU.mult, ALU.add)
                        last.then_inc(s.evac_dve, 1)

            def residual(l, tiles):
                s = outp[l]
                dve.wait_ge(s.gate_turned, s.n.gate_turned + 1)
                dve_after(v.tensor_copy(by_slice(MROW[:, 1, :]), bank(6, 2).rearrange("p (k x) -> p k x", k=KD)))
                dve.wait_ge(s.gate_act, s.n.gate_act + 1)
                tmp = xr(0, D)
                for t in range(tiles):
                    dve.wait_ge(s.product, s.n.product + t + 1)
                    dve_after(v.tensor_tensor(tmp, bank(2 * (t % 2), 2), MROW[:, 0 if t < LT else 1, :], ALU.mult))
                    last = v.tensor_tensor(H[:, t, :], H[:, t, :], tmp, ALU.add)
                    dve_after(last)
                    v.engine_nop().then_inc(s.added, 1)

            def route(l, tiles):
                s = rt[l]
                lg, af, small = xr(7200, TT, E), xr(7300, TT, 48), STAT[:, 0:16]
                affT, work = xr(7600, LAT), xr(8120, 64)
                idx = xr(8190, 64).bitcast(U32)
                dve_after(v.memset(af[:, 0:tiles], 0.0))
                dve_after(v.memset(affT[0:48], -1.0))
                dve.wait_ge(s.logits, s.n.logits + 1)
                ps = bank(4)[:, 0:tiles * E].rearrange("p (t e) -> p t e", e=E)
                dve_after(v.tensor_reduce(small[:, 0:tiles], ps, X_AXIS, ALU.max))
                v.tensor_tensor(lg[:, 0:tiles], ps, small[:, 0:tiles].unsqueeze(2).to_broadcast([P, tiles, E]),
                                ALU.subtract).then_inc(s.shifted, 1)
                dve.wait_ge(s.exps, s.n.exps + 1)
                dve_after(v.tensor_reduce(small[:, 0:tiles], lg[:, 0:tiles], X_AXIS, ALU.add))
                dve_after(v.reciprocal(small[:, 8:8 + tiles], small[:, 0:tiles]))
                for lo, hi, at in ((0, LT, 0), (LT, tiles, 32))[:1 if tiles == LT else 2]:
                    last = v.tensor_tensor(af[:, lo:hi, at:at + E], lg[:, lo:hi],
                                           small[:, 8 + lo:8 + hi].unsqueeze(2).to_broadcast([P, hi - lo, E]), ALU.mult)
                    dve_after(last)
                v.engine_nop().then_inc(s.aff, 1)
                dve.wait_ge(s.turned, s.n.turned + 1)
                dve_after(v.tensor_copy(affT[0:E, :], bank(5)[0:E, :]))
                if tiles > LT:
                    dve_after(v.tensor_copy(affT[32:48, 0:CTX], bank(6)[32:48, 0:CTX]))
                for r in range(CAP_L // 8):
                    g8 = work[0:48, r * 8:(r + 1) * 8]
                    dve_after(v.max(g8, affT[0:48]))
                    dve_after(v.max_index(idx[0:48, r * 8:(r + 1) * 8], g8, affT[0:48]))
                    dve_after(v.match_replace(affT[0:48], g8, affT[0:48], -2.0))
                pack = STAT[0:E, 96:288]
                dve_after(v.tensor_copy(pack[:, 0:CAP_L], idx[0:E, :]))
                dve_after(v.tensor_copy(pack[:, 96:96 + CAP_L], work[0:E, :]))
                if tiles > LT:
                    dve_after(v.tensor_scalar(pack[:, CAP_L:96], idx[32:48, 0:CAP_C], float(LAT), None, ALU.add))
                    dve_after(v.tensor_copy(pack[:, 96 + CAP_L:192], work[32:48, 0:CAP_C]))
                v.engine_nop().then_inc(s.packed, 1)
                dve.wait_ge(s.routed, s.n.routed + 1)
                n = NSLOT[l]
                dve_after(v.memset(IDXT[:, :], 0))
                dve_after(v.tensor_copy(IDXT[0:n, 0:E], bank(4)[0:n, 128:128 + E]))
                dve_after(v.tensor_copy(GATET[0:n, :], bank(4)[0:n, 128 + E:128 + 2 * E]))

            def experts(l):
                s, n = moe[l], NSLOT[l]
                XT, HID, HT = xr(1024, KD, 96), xr(1792, D), xr(2816, KD, 96)
                SIL, Y = xr(3584, D), xr(4608, D)
                ZERO = xr(5700, D)
                v.memset(ZERO, 0.0).then_inc(s.zeroed, 1)
                v.memset(STAT[:, 296:297], 0.0).then_inc(s.ht_dve, 1)
                v.memset(STAT[:, 297:298], 0.0).then_inc(s.y_dve, 1)

                def modulate():
                    for k in range(4, KD):
                        b = bank(7)[:, (k - 4) * P:(k - 4) * P + n]
                        for st, lo, hi in ((0, 0, CAP_L), (1, CAP_L, n))[:1 if n == CAP_L else 2]:
                            last = v.tensor_scalar(XT[:, k, lo:hi], b[:, lo:hi], ACOL[:, l, 1, k, st:st + 1],
                                                   MCOL[:, l, 3 * KD + k, st:st + 1], ALU.mult, ALU.add)
                    last.then_inc(s.xt_dve, 1)

                dve.wait_ge(s.x_turned, s.n.x_turned + 1)
                modulate()
                with dve.Fori(0, E) as e:
                    dve.wait_ge(s.silu, s.n.silu + e + 1)
                    wait_product(dve, l, UP, e)
                    v.tensor_tensor(HID[0:n], SIL[0:n], bank(2, 2)[0:n], ALU.mult).then_inc(s.hidden, 1)
                    dve.wait_ge(s.x_turned, s.n.x_turned + e + 2)
                    modulate()
                    dve.wait_ge(s.h_turned, s.n.h_turned + e + 1)
                    v.tensor_copy(HT[:, 4:8, 0:n], bank(7).rearrange("p (k t) -> p k t", t=P)[:, :, 0:n]
                                  ).then_inc(s.ht_dve, 1)
                    dve.wait_ge(s.routes, s.n.routes + e + 1)
                    wait_product(dve, l, DOWN, e)
                    v.tensor_scalar(Y[0:n, BW:D], bank(5)[0:n], GCUR[0:n, :], None, ALU.mult).then_inc(s.y_dve, 1)
                buf = xr(0, 2, D)
                dve.wait_ge(rt[l].gate_act, rt[l].n.gate_act + 1)
                for t in range(TT if l == 0 else LT):
                    dve.wait_ge((s.readback0, s.readback1)[t % 2], s.n.readback0 + 16 * (t // 2 + 1))
                    b = buf[:, t % 2, :]
                    dve_after(v.tensor_tensor(b, b, MROW[:, 0 if t < LT else 1, :], ALU.mult))
                    v.tensor_tensor(H[:, t, :], H[:, t, :], b, ALU.add).then_inc(s.added, 1)

            dve.wait_ge(cond_exp, 1)
            cv = VCOL[:, 0, 64:80].rearrange("p (w k) -> p k w", w=2)
            dve_after(v.tensor_scalar(SCT[:, 1], SCT[:, 0], 1.0, None, ALU.add))
            dve_after(v.reciprocal(SCT[:, 0], SCT[:, 1]))
            v.tensor_tensor(SC[:, :, :], SCT[:, 0], cv, ALU.mult).then_inc(cond_ready, 1)
            dve.wait_ge(consts_loaded, ACT_CONSTS)
            dve.wait_ge(small_loaded, POOL_CONSTS)
            v.tensor_scalar(GA[:, 0, :], GA[:, 0, :], HD ** -0.5, None, ALU.mult)
            v.tensor_scalar(GB[:, 0:1], GB[:, 0:1], HD ** -0.5, None, ALU.mult)
            for i in range(6):
                ada((0, i))
            end(dve, "dve")
            begin(dve, "dve", 1)
            norm(0, 0, TT)
            end(dve, "dve")
            begin(dve, "dve", 2)
            for u, (c, t) in enumerate([(c, t) for c in range(5) for t in range(TT)]):
                if c == 4:
                    dve.wait_ge(prj.product, u + 1)
                    v.engine_nop().then_inc(prj.scaled, 1)
                    ada((2, u))
                    continue
                ps = bank(u % 4)
                ph = PH[:, 24 * (u % 2):24 * (u % 2) + 24]
                dve.wait_ge(prj.squares, u + 1)
                dve_after(v.tensor_reduce(ph[:, 0:8], SQ[:, u % 2, :].rearrange("p (h d) -> p h d", d=HD), X_AXIS, ALU.add))
                dve_after(v.tensor_scalar(ph[:, 8:16], ph[:, 0:8], 1.0 / HD, EPS, ALU.mult, ALU.add))
                v.reciprocal(ph[:, 16:24], ph[:, 8:16]).then_inc(prj.inverse, 1)
                dve.wait_ge(prj.rstd, u + 1)
                if u >= 2:
                    dve.wait_ge(prj.turned, u - 1)
                st = STAGE[:, u % 2, :]
                last = v.tensor_tensor(st.rearrange("p (h d) -> p h d", d=HD), ps.rearrange("p (h d) -> p h d", d=HD),
                                       ph[:, 0:8].unsqueeze(2).to_broadcast([P, 8, HD]), ALU.mult)
                last.then_inc(prj.scaled, 1)
                dve.wait_ge(prj.scaled, u + 1)
                if c < 2:
                    nh = 8 if c == 0 else 2
                    a = st[:, 0:nh * HD]
                    dve_after(v.tensor_tensor(a.rearrange("p (h d) -> p h d", d=HD), a.rearrange("p (h d) -> p h d", d=HD),
                                              GA[:, c, :].unsqueeze(1).to_broadcast([P, nh, HD]), ALU.mult))
                    if c == 0:
                        dst = STAGE2[:, u % 2, :].rearrange("p (j a d) -> p a j d", j=4, a=2)
                    else:
                        dst = STAGE2[:, u % 2, 0:nh * HD].rearrange("p (j a d) -> p a j d", j=1, a=2)
                    if t < LT:
                        cos = CONST[:, C_ROPE + t * P:C_ROPE + t * P + HD]
                        sin = CONST[:, C_ROPE + t * P + HD:C_ROPE + (t + 1) * P].rearrange("p (g s i) -> p g s i", g=2, s=2)
                        src4 = a.rearrange("p (h g s i) -> p (h g) s i", g=2, s=2, i=16)
                        rot4 = ROT[:, 0:nh * HD].rearrange("p (h g s i) -> p (h g) s i", g=2, s=2, i=16)
                        for g in range(2):
                            for sd in range(2):
                                dve_after(v.tensor_tensor(
                                    rot4[:, g::2, sd, :], src4[:, g::2, 1 - sd, :],
                                    sin[:, g, sd, :].unsqueeze(1).to_broadcast([P, nh, 16]), ALU.mult))
                        dve_after(v.tensor_tensor(a.rearrange("p (h d) -> p h d", d=HD), a.rearrange("p (h d) -> p h d", d=HD),
                                                  cos.unsqueeze(1).to_broadcast([P, nh, HD]), ALU.mult))
                        for aa in range(2):
                            hh = nh // 2
                            dve_after(v.tensor_tensor(
                                dst[:, aa], a[:, aa * hh * HD:(aa + 1) * hh * HD].rearrange("p (j d) -> p j d", d=HD),
                                ROT[:, aa * hh * HD:(aa + 1) * hh * HD].rearrange("p (j d) -> p j d", d=HD), ALU.add))
                    else:
                        for aa in range(2):
                            hh = nh // 2
                            dve_after(v.tensor_copy(dst[:, aa], a[:, aa * hh * HD:(aa + 1) * hh * HD].rearrange("p (j d) -> p j d", d=HD)))
                    if c == 1:
                        dve_after(v.tensor_copy(STAGE2[:, u % 2, 256:512], st[:, 256:512]))
                v.engine_nop().then_inc(prj.stage, 1)
                ada((2, u))
            end(dve, "dve")
            begin(dve, "dve", 3)
            def softmax(first, N):
                nbias = 0
                for i in range(first, N + 3):
                    if i < N:
                        u = heads[i]
                        b0 = 2 * (i % 2)
                        dve.wait_ge(att.scores, i + 1)
                        sc = bank(b0, 2)[:, (0 if u.t < LT else LAT):TOK]
                        if u.biased:
                            nbias += 1
                            lo = (u.head * NSH + (ROWS - 2 - 2 * u.t)) * GRID_W
                            v.tensor_tensor(bank(b0), bank(b0), BIAS[:, lo:lo + LAT], ALU.add).then_inc(att.biased, 1)
                            dve.wait_ge(att.biased, nbias)
                        dve_after(v.tensor_reduce(SM[:, i % 3:i % 3 + 1], sc, X_AXIS, ALU.max))
                        if i >= 3:
                            dve.wait_ge(att.probs, i - 2)
                        v.tensor_scalar(SM[:, 3 + i % 3:4 + i % 3], SM[:, i % 3:i % 3 + 1], -1.0, None, ALU.mult
                                        ).then_inc(att.negmax, 1)
                    j = i - 1
                    if first <= j < N:
                        u = heads[j]
                        dve.wait_ge(att.probs, j + 1)
                        dve_after(v.reciprocal(SM[:, 9:10], SM[:, 6 + j % 3:7 + j % 3]))
                        pr = PROB[:, j % 3, (0 if u.t < LT else LAT):TOK]
                        v.tensor_scalar(pr, pr, SM[:, 9:10], None, ALU.mult).then_inc(att.normal, 1)
                        dve.wait_ge(att.normal, j + 1)
                    if i < N:
                        ada((3, i))
                    j = i - 2
                    if first <= j < N:
                        dve.wait_ge(att.turned, j + 1)
                        if j >= 2:
                            dve.wait_ge(att.mixed, j - 1)
                        v.tensor_copy(PROBT[:, j % 2, LAT:TOK], bank(5)[:, 0:CTX]).then_inc(att.evac_dve, 1)

            softmax(0, N_A)
            for i in range(0, BIAS_N, 2):
                dve.wait_ge(bias_flipped, i + 1)
                v.tensor_copy(BIAS[:, i * BW:(i + 1) * BW], bank(i % 4)).then_inc(bias_evac_dve, 1)
            dve.wait_ge(bias_evac_act, BIAS_N // 2)
            dve.wait_ge(bias_evac_dve, BIAS_N // 2)
            softmax(N_A, len(heads))
            end(dve, "dve")
            begin(dve, "dve", 4)
            residual(0, TT)
            end(dve, "dve")
            begin(dve, "dve", 5)
            norm(0, 1, TT)
            route(0, TT)
            end(dve, "dve")
            begin(dve, "dve", 6)
            experts(0)
            end(dve, "dve")
            begin(dve, "dve", 7)
            end(dve, "dve")
            begin(dve, "dve", 8)
            norm(1, 0, TT)
            end(dve, "dve")
            begin(dve, "dve", 9)
            GTMP = xr(9216, TOK)
            for i, (d, j) in enumerate(gates):
                dve.wait_ge(gp.gate_abs, i + 1)
                bcol = VCOL[:, 1, 80 + 4 * d + j:81 + 4 * d + j]
                v.tensor_scalar(GTMP, bank(4 + 2 * (i % 2), 2)[:, 0:TOK], bcol, 0.0, ALU.add, ALU.min).then_inc(gp.gate_x, 1)
                dve.wait_ge(gp.gate_ln, i + 1)
                dve.wait_ge(gp.gate_x, i + 1)
                dve_after(v.tensor_tensor(GTMP, GTMP, GLN, ALU.subtract))
                cum = CUM[d][:, j, :]
                for lo, hi, m in ((0, LAT, CONST[:, C_RESET:C_RESET + LAT]), (LAT, TOK, CONST[:, C_RESET + 1:C_RESET + 2].to_broadcast([P, CTX]))):
                    o, g = cum[:, lo:hi], GTMP[:, lo:hi]
                    if d:
                        o, g = o[:, ::-1], g[:, ::-1]
                    last = v.tensor_tensor_scan(o, m, g, 0.0, ALU.mult, ALU.add)
                dve_after(last)
                v.engine_nop().then_inc(gp.cum, 1)
            end(dve, "dve")
            begin(dve, "dve", 10)
            for d in range(2):
                dve_after(v.memset(lanes[d].QZ, 0.0))
                dve_after(v.memset(lanes[d].AT, 0.0))
            for h in range(G_H):
                for d in range(2):
                    L = lanes[d]
                    n = 2 * h + d
                    cum = CUM[d][:, h, :]
                    edge = CHUNK - 1 if d == 0 else 0
                    dve.wait_ge(gs.e_pos, n + 1)
                    if h:
                        dve.wait_ge(gs.o_done, lane_o(h - 1, d, LT - 1))
                    e4 = L.TMP[:, 0:LAT].rearrange("p (t x) -> p t x", x=P)
                    q4 = GQ[:, h, :].rearrange("p (t x) -> p t x", x=P)
                    qz4 = L.QZ.rearrange("p (t e x) -> p t e x", e=2, x=P)
                    dve_after(v.tensor_copy(L.DEC, L.TMP[:, edge:LAT:CHUNK]))
                    for eo in range(2):
                        sl = slice(eo * CHUNK, (eo + 1) * CHUNK)
                        last = v.tensor_tensor(qz4[:, :, eo, sl], q4[:, :, sl], e4[:, :, sl], ALU.mult)
                        dve_after(last)
                    v.engine_nop().then_inc(gs.qdec, 1)
                    c3 = cum[:, 0:LAT].rearrange("p (c x) -> p c x", x=CHUNK)
                    dve_after(v.tensor_tensor(L.TMP[:, 0:LAT].rearrange("p (c x) -> p c x", x=CHUNK),
                                              c3[:, :, edge:edge + 1].to_broadcast([P, LAT // CHUNK, CHUNK]), c3, ALU.subtract))
                    cx = LAT + (CTX - 1 if d == 0 else 0)
                    v.tensor_tensor(L.TMP[:, LAT:TOK], cum[:, cx:cx + 1].to_broadcast([P, CTX]), cum[:, LAT:TOK],
                                    ALU.subtract).then_inc(gs.diff, 1)
                    dve.wait_ge(gs.e_neg, n + 1)
                    v.tensor_tensor(L.KI, L.KI, GK[:, h, 0:LAT], ALU.mult).then_inc(gs.kinv, 1)
                    dve.wait_ge(gs.e_diff, n + 1)
                    v.tensor_tensor(L.KS, L.TMP, GK[:, h, :], ALU.mult).then_inc(gs.kst, 1)
                for d in range(2):
                    L = lanes[d]
                    n = 2 * h + d
                    dve.wait_ge(gs.s0, n + 1)
                    v.tensor_copy(L.S[:, 0, :], bank(4 * d + 2)[:, 0:G_DV]).then_inc(gs.s0_out, 1)
                    dve.wait_ge(gs.a_done, n + 1)
                    m = CONST[:, (C_MASKF, C_MASKB)[d]:(C_MASKF, C_MASKB)[d] + P].bitcast(U32)
                    for t in range(LT):
                        last = v.copy_predicated(L.AT[:, t * P:(t + 1) * P], m, bank(4 * d)[:, t * P:(t + 1) * P])
                        dve_after(last)
                    v.engine_nop().then_inc(gs.a_out, 1)
                for i in range(2 * LT):
                    for d in range(2):
                        L = lanes[d]
                        if i < 2 * LT - 1:
                            c = i if d == 0 else 2 * LT - 1 - i
                            dve.wait_ge(gs.upd, lane_state(h, d, i))
                            if i == 0:
                                dve.wait_ge(gs.s0_out, 2 * h + d + 1)
                            else:
                                dve.wait_ge(gs.state, lane_state(h, d, i - 1))
                            v.scalar_tensor_tensor(out=L.S[:, (i + 1) % 2, :], in0=L.S[:, i % 2, :],
                                                   scalar=L.DEC[:, c:c + 1], in1=bank(4 * d + 2)[:, 256:512],
                                                   op0=ALU.mult, op1=ALU.add).then_inc(gs.state, 1)
                        if i % 2:
                            t = (i // 2) if d == 0 else LT - 1 - i // 2
                            ob = bank(4 * d + 1 + 2 * ((i // 2) % 2))[:, 0:G_DV]
                            o = GO[:, t, h * G_DV:(h + 1) * G_DV]
                            k = lane_o(h, d, i // 2)
                            dve.wait_ge(gs.o_done, k)
                            first = (i < LT)
                            if first:
                                v.tensor_copy(o, ob).then_inc(gs.o_out, 1)
                            else:
                                dve.wait_ge(gs.o_out, k - 1)
                                v.tensor_tensor(o, o, ob, ALU.add).then_inc(gs.o_out, 1)
            end(dve, "dve")
            begin(dve, "dve", 11)
            st = STAT[:, 0:48]
            dve.wait_ge(mg.squares, LT * G_H)
            dve_after(v.tensor_scalar(st[:, 16:32], st[:, 0:16], 1.0 / G_DV, EPS, ALU.mult, ALU.add))
            v.reciprocal(st[:, 32:48], st[:, 16:32]).then_inc(mg.inverse, 1)
            dve.wait_ge(mg.rstd, 1)
            for t in range(LT):
                o = GO[:, t, :].rearrange("p (h e) -> p h e", h=G_H)
                dve_after(v.tensor_tensor(o, o, st[:, 4 * t:4 * t + 4].unsqueeze(2).to_broadcast([P, G_H, G_DV]), ALU.mult))
                dve_after(v.tensor_tensor(o, o, ONORM[:, :].unsqueeze(1).to_broadcast([P, G_H, G_DV]), ALU.mult))
                v.tensor_tensor(GO[:, t, :], GO[:, t, :], OG[:, t, :], ALU.mult).then_inc(mg.scaled, 1)
            end(dve, "dve")
            begin(dve, "dve", 12)
            residual(1, LT)
            end(dve, "dve")
            begin(dve, "dve", 13)
            norm(1, 1, LT)
            route(1, LT)
            end(dve, "dve")
            begin(dve, "dve", 14)
            experts(1)
            end(dve, "dve")

        @block.scalar
        def _(act):
            a = nc.scalar.activation

            def ada(where):
                for what, l, i in ada_at.get(where, ()):
                    if what == "chunk":
                        act.wait_ge(ada_s.product, 12 * l + i + 1)
                        if i % 2 == 0 and (l, i) != (0, 0):
                            act.wait_ge(ada_s.turned, 6 * l + i // 2)
                        a(ADA_ROWS[:, (i % 2) * BW:(i % 2 + 1) * BW], bank(7)[0:2, :], ACT.Copy).then_inc(ada_s.rows, 1)

            def norm(l, w, tiles):
                s = norm_s[(l, w)]
                for t in range(tiles):
                    act_after(a(sq_junk, H[:, t, :], ACT.Square, accum_out=STAT[:, 304 + t:305 + t]))
                    act.drain().then_inc(s.sumsq, 1)
                act.wait_ge(s.inverse, s.n.inverse + 1)
                a(MSR[:, 0:tiles], STAT[:, 8:8 + tiles], ACT.Sqrt).then_inc(s.rstd, 1)
                for u in range(tiles):
                    act.wait_ge(s.turned, s.n.turned + u + 1)
                    st = 0 if u < LT else 1
                    for k in range(4):
                        last = a(UT[:, k, u * P:(u + 1) * P], bank(2 * (u % 2))[:, k * P:(k + 1) * P], ACT.Identity,
                                 bias=MCOL[:, l, 3 * w * KD + k, st:st + 1], scale=ACOL[:, l, w, k, st:st + 1])
                    last.then_inc(s.evac_act, 1)

            def experts(l):
                s, n = moe[l], NSLOT[l]
                XT, HT, SIL, Y = xr(1024, KD, 96), xr(2816, KD, 96), xr(3584, D), xr(4608, D)
                a(STAT[:, 298:299], STAT[:, 304:305], ACT.Copy).then_inc(s.ht_act, 1)
                a(STAT[:, 299:300], STAT[:, 304:305], ACT.Copy).then_inc(s.y_act, 1)

                def modulate():
                    for k in range(4):
                        b = bank(6)[:, k * P:k * P + n]
                        for st, lo, hi in ((0, 0, CAP_L), (1, CAP_L, n))[:1 if n == CAP_L else 2]:
                            last = a(XT[:, k, lo:hi], b[:, lo:hi], ACT.Identity, bias=MCOL[:, l, 3 * KD + k, st:st + 1],
                                     scale=ACOL[:, l, 1, k, st:st + 1])
                    last.then_inc(s.xt_act, 1)

                act.wait_ge(s.x_turned, s.n.x_turned + 1)
                modulate()
                with act.Fori(0, E) as e:
                    wait_product(act, l, GATE, e)
                    a(SIL[0:n], bank(0, 2)[0:n], ACT.Silu).then_inc(s.silu, 1)
                    act.wait_ge(s.x_turned, s.n.x_turned + e + 2)
                    modulate()
                    act.wait_ge(s.h_turned, s.n.h_turned + e + 1)
                    a(HT[:, 0:4, 0:n], bank(6).rearrange("p (k t) -> p k t", t=P)[:, :, 0:n], ACT.Copy
                      ).then_inc(s.ht_act, 1)
                    act.wait_ge(s.routes, s.n.routes + e + 1)
                    wait_product(act, l, DOWN, e)
                    a(Y[0:n, 0:BW], bank(4)[0:n], ACT.Copy, scale=GCUR[0:n, :]).then_inc(s.y_act, 1)

            def vectors(eng, l, what):
                for at, src in what:
                    n = int(np.prod(src.shape)) // D
                    eng.dma_start(VCOL[:, l, at:at + KD * n].rearrange("p (v k) -> p v k", k=KD),
                                  src.rearrange("(v p k) -> p v k", p=P, k=KD)).then_inc(
                                      vec_loaded if at >= 64 else consts_loaded, 16)

            vectors(act, 0, ((64, A["c"][0]), (72, A["c_ctx"])))
            act.dma_start(CONST[:, :], A["shape_constants"]).then_inc(consts_loaded, 16)
            vectors(act, 0, ((48, A["norm1_g"][0]), (0, A["ada_b"][0]), (56, A["norm2_g"][0])))
            act.wait_ge(vec_loaded, 32)
            a(SCT[:, 0], VCOL[:, 0, 64:80].rearrange("p (w k) -> p k w", w=2), ACT.Exp, scale=-1.0).then_inc(cond_exp, 1)
            for i in range(6):
                ada((0, i))
            end(act, "act")
            begin(act, "act", 1)
            act.wait_ge(h_loaded, 32)
            norm(0, 0, TT)
            end(act, "act")
            begin(act, "act", 2)
            act_units = [(c, t) for c in range(5) for t in range(TT)]

            def evac_heads(u):
                c, t = act_units[u]
                if c == 4:
                    return
                act.wait_ge(prj.turned, u + 1)
                b = bank(4 + u % 2)
                tok = slice(t * P, (t + 1) * P)
                for i, (col, num, dst, gain) in enumerate((
                        ((0, 4, 0, None),), ((0, 1, 4, None), (2, 2, 5, 0)), ((0, 2, 7, 0), (2, 2, 9, 1)), ((0, 2, 11, 1),))[c]):
                    src = b[:, col * P:(col + num) * P].rearrange("p (j x) -> p j x", x=P)
                    if gain is None:
                        last = a(qk(dst, num)[:, :, tok], src, ACT.Copy)
                    else:
                        last = a(qk(dst, num)[:, :, tok], src, ACT.Copy, scale=GB[:, gain:gain + 1])
                last.then_inc(prj.evac, 1)

            for u, (c, t) in enumerate(act_units):
                b = bank(u % 4)
                act.wait_ge(prj.product, u + 1)
                if c < 4:
                    if u >= 2:
                        act.wait_ge(prj.scaled, u - 1)
                    a(SQ[:, u % 2, :], b, ACT.Square).then_inc(prj.squares, 1)
                if c == 1:
                    a(V[:, t, 0:P], b[:, P:2 * P], ACT.Copy).then_inc(prj.v_out, 1)
                elif c == 3:
                    a(V[:, t, P:P + 256], b[:, 256:512], ACT.Copy).then_inc(prj.v_out, 1)
                elif c == 4:
                    a(V[:, t, P + 256:P + 512], b[:, 0:256], ACT.Copy).then_inc(prj.v_out, 1)
                else:
                    act.drain().then_inc(prj.v_out, 1)
                if c < 4:
                    act.wait_ge(prj.inverse, u + 1)
                    ph = PH[:, 24 * (u % 2):24 * (u % 2) + 24]
                    a(ph[:, 0:8], ph[:, 16:24], ACT.Sqrt).then_inc(prj.rstd, 1)
                if u:
                    evac_heads(u - 1)
                ada((2, u))
            end(act, "act")
            begin(act, "act", 3)
            def exponentials(first, N):
                for i in range(first, N + 3):
                    if i < N:
                        u = heads[i]
                        lo = 0 if u.t < LT else LAT
                        act.wait_ge(att.negmax, i + 1)
                        if i >= 3:
                            act.wait_ge(att.turned, i - 2)
                        a(PROB[:, i % 3, lo:TOK], bank(2 * (i % 2), 2)[:, lo:TOK], ACT.Exp, bias=SM[:, 3 + i % 3:4 + i % 3],
                          accum_out=SM[:, 6 + i % 3:7 + i % 3]).then_inc(att.probs, 1)
                        ada((3, i))
                    j = i - 2
                    if first <= j < N:
                        act.wait_ge(att.turned, j + 1)
                        if j >= 2:
                            act.wait_ge(att.mixed, j - 1)
                        if heads[j].t < LT:
                            a(PROBT[:, j % 2, 0:LAT], bank(4), ACT.Copy).then_inc(att.evac_act, 1)
                        else:
                            act.drain().then_inc(att.evac_act, 1)
                    j = i - 3
                    if first <= j < N:
                        u = heads[j]
                        act.wait_ge(att.mixed, j + 1)
                        a(UT[u.base:u.base + HD, u.mix, u.t * P:(u.t + 1) * P], bank(6)[u.base:u.base + HD, 0:P],
                          ACT.Copy).then_inc(att.evac_mix, 1)

            exponentials(0, N_A)
            for i in range(1, BIAS_N, 2):
                act.wait_ge(bias_flipped, i + 1)
                a(BIAS[:, i * BW:(i + 1) * BW], bank(i % 4), ACT.Copy).then_inc(bias_evac_act, 1)
            exponentials(N_A, len(heads))
            end(act, "act")
            begin(act, "act", 4)
            act.wait_ge(outp[0].gate_turned, 1)
            a(by_slice(MROW[:, 0, :]), bank(4, 2).rearrange("p (k x) -> p k x", k=KD), ACT.Copy).then_inc(outp[0].gate_act, 1)
            end(act, "act")

            def route(l, tiles):
                s = rt[l]
                act.wait_ge(s.gate_turned, s.n.gate_turned + 1)
                for w in range(2):
                    act_after(a(by_slice(MROW[:, w, :]), bank(2 * w, 2).rearrange("p (k x) -> p k x", k=KD), ACT.Copy))
                act.drain().then_inc(s.gate_act, 1)
                lg = xr(7200, TT, E)[:, 0:tiles]
                act.wait_ge(s.shifted, s.n.shifted + 1)
                a(lg, lg, ACT.Exp).then_inc(s.exps, 1)

            begin(act, "act", 5)
            norm(0, 1, TT)
            route(0, TT)
            end(act, "act")
            begin(act, "act", 6)
            experts(0)
            end(act, "act")
            begin(act, "act", 7)
            end(act, "act")
            begin(act, "act", 8)
            norm(1, 0, TT)
            end(act, "act")
            begin(act, "act", 9)
            n_out = 0

            def out_bank():
                act.wait_ge(gp.product, n_out + 1)
                return bank(n_out % 4)

            for c in range(2):
                for j in range(G_H):
                    if c == 0:
                        a(GQ[:, j, :], out_bank(), ACT.Copy, scale=G_DK ** -0.5).then_inc(gp.evac_act, 1)
                        n_out += 1
                    else:
                        for lo, hi in ((0, LAT), (LAT, TOK)):
                            a(GK[:, j, lo:hi], out_bank()[:, 0:hi - lo], ACT.Copy).then_inc(gp.evac_act, 1)
                            n_out += 1
            for lo, hi in ((0, LAT), (LAT, TOK)):
                a(ZT[:, lo:hi], out_bank()[0:48, 0:hi - lo], ACT.Copy).then_inc(gp.evac_act, 1)
                n_out += 1
            for c in range(2, 4):
                for t in range(TT):
                    a(GV[:, t, (c - 2) * BW:(c - 1) * BW], out_bank(), ACT.Copy).then_inc(gp.evac_act, 1)
                    n_out += 1
            for c in range(4, 6):
                for t in range(LT):
                    a(OG[:, t, (c - 4) * BW:(c - 3) * BW], out_bank(), ACT.Silu).then_inc(gp.evac_act, 1)
                    n_out += 1
            for i, (d, j) in enumerate(gates):
                act.wait_ge(gp.raw, i + 1)
                bcol = VCOL[:, 1, 80 + 4 * d + j:81 + 4 * d + j]
                if i:
                    act.wait_ge(gp.cum, i)
                a(GLN, bank(4 + 2 * (i % 2), 2)[:, 0:TOK], ACT.Abs, bias=bcol).then_inc(gp.gate_abs, 1)
                act.wait_ge(gp.gate_abs, i + 1)
                a(GLN, GLN, ACT.Exp, scale=-1.0).then_inc(gp.gate_exp, 1)
                act.wait_ge(gp.gate_exp, i + 1)
                a(GLN, GLN, ACT.Ln, bias=1.0).then_inc(gp.gate_ln, 1)
            end(act, "act")
            begin(act, "act", 10)
            for h in range(G_H):
                for d in range(2):
                    L = lanes[d]
                    n = 2 * h + d
                    cum = CUM[d][:, h, :]
                    if h:
                        act.wait_ge(gs.kst, 2 * (h - 1) + d + 1)
                        act.wait_ge(gs.a_done, 2 * (h - 1) + d + 1)
                    a(L.TMP[:, 0:LAT], cum[:, 0:LAT], ACT.Exp, scale=1.0 / 16).then_inc(gs.e_pos, 1)
                    a(L.KI, cum[:, 0:LAT], ACT.Exp, scale=-1.0 / 16).then_inc(gs.e_neg, 1)
                    act.wait_ge(gs.diff, n + 1)
                    a(L.TMP, L.TMP, ACT.Exp, scale=1.0 / 16).then_inc(gs.e_diff, 1)
                for d in range(2):
                    L = lanes[d]
                    act.wait_ge(gs.kturned, 2 * h + d + 1)
                    a(L.KS, bank(4 * d, 2)[:, 0:TOK], ACT.Copy).then_inc(gs.kst_out, 1)
            end(act, "act")
            begin(act, "act", 11)
            for t in range(LT):
                for h in range(G_H):
                    a(xr(9216, G_DV), GO[:, t, h * G_DV:(h + 1) * G_DV], ACT.Square,
                      accum_out=STAT[:, 4 * t + h:4 * t + h + 1]).then_inc(mg.squares, 1)
                    act.wait_ge(mg.squares, 4 * t + h + 1)
            act.wait_ge(mg.inverse, 1)
            a(STAT[:, 0:16], STAT[:, 32:48], ACT.Sqrt).then_inc(mg.rstd, 1)
            for t in range(LT):
                act.wait_ge(mg.turned, t + 1)
                for n in range(2):
                    last = a(OT[:, 4 * n:4 * n + 4, t * P:(t + 1) * P],
                             bank(2 * (t % 2) + n).rearrange("p (k x) -> p k x", x=P), ACT.Copy)
                last.then_inc(mg.evac, 1)
            end(act, "act")
            begin(act, "act", 12)
            act.wait_ge(outp[1].gate_turned, 2)
            a(by_slice(MROW[:, 0, :]), bank(4, 2).rearrange("p (k x) -> p k x", k=KD), ACT.Copy).then_inc(outp[1].gate_act, 1)
            end(act, "act")
            begin(act, "act", 13)
            norm(1, 1, LT)
            route(1, LT)
            end(act, "act")
            begin(act, "act", 14)
            experts(1)
            end(act, "act")

        @block.gpsimd
        def _(pool):
            g = nc.gpsimd

            for i, g_ in enumerate(("a_q_norm", "a_k_norm")):
                pool.dma_start(GA[:, i, :], A[g_][0:1, :].to_broadcast([P, HD])).then_inc(small_loaded, 16)
            for i, g_ in enumerate(("b_q_norm", "b_k_norm")):
                for half in range(2):
                    pool.dma_start(GB[half * HD:(half + 1) * HD, i:i + 1],
                                   A[g_].rearrange("a d -> d a")).then_inc(small_loaded, 16)
            for l in range(2):
                pool.dma_start(RW[:, l], A["moe_router"][l].rearrange("(p k) e -> p k e", p=P)).then_inc(small_loaded, 16)
            for at, src in ((48, A["norm1_g"][1]), (0, A["ada_b"][1]), (56, A["norm2_g"][1])):
                n = int(np.prod(src.shape)) // D
                pool.dma_start(VCOL[:, 1, at:at + KD * n].rearrange("p (v k) -> p v k", k=KD),
                               src.rearrange("(v p k) -> p v k", p=P, k=KD)).then_inc(small_loaded, 16)
            for at, src in ((80, A["gla_gk_b_f"]), (84, A["gla_gk_b_b"])):
                pool.dma_start(VCOL[:, 1, at:at + 4], src[0].rearrange("(j p) -> p j", p=P), allow_slow_non_contiguous=True).then_inc(small_loaded, 16)
            pool.dma_start(ONORM[:, :], A["gla_o_norm"][0:1, :].to_broadcast([P, G_DV])).then_inc(small_loaded, 16)
            pool.dma_start(GKW[0:16, :], A["gla_gk_w_f"][0]).then_inc(small_loaded, 16)
            pool.dma_start(GKW[32:48, :], A["gla_gk_w_b"][0]).then_inc(small_loaded, 16)
            n = B_H * DR * DC
            flat = A["na_rpb"][0].rearrange("h a b -> (h a b)")
            pool.dma_start(RPB[96:96 + n], flat).then_inc(bias_copied, 16)
            pool.dma_start(RPB[0:96], flat[0:96]).then_inc(bias_copied, 16)
            pool.dma_start(RPB[96 + n:192 + n], flat[0:96]).then_inc(bias_copied, 16)

            def store_rows(l, tiles):
                s = norm_s[(l, 1)]
                for t in range(tiles):
                    pool.wait_ge(s.xhat, s.n.xhat + t + 1)
                    pool.dma_start(XH[l][t * P:(t + 1) * P, :], xhat[:, t, :]).then_inc((s.stored0, s.stored1)[t % 2], 16)
                pool.wait_ge(s.stored0, s.n.stored0 + 16 * ((tiles + 1) // 2))
                pool.wait_ge(s.stored1, s.n.stored1 + 16 * (tiles // 2))

            def experts(l):
                s, n = moe[l], NSLOT[l]
                XG, Y, ZERO = xr(0, D), xr(4608, D), xr(5700, D)
                tiles = TT if l == 0 else LT
                pool_after(g.tensor_copy(IDXG[0:n, :], IDXT[0:n, 0:1]))
                pool.indirect_dma_start(XG[0:n, :], None, XH[l], bass.IndirectOffsetOnAxis(IDXG[0:n, 0:1], 0)
                                        ).then_inc(s.gathered, 16)
                pool.wait_ge(s.zeroed, s.n.zeroed + 1)
                for t in range(tiles):
                    pool.dma_start(ACC[l][t * P:(t + 1) * P, :], ZERO
                                   ).then_inc(acc_cleared[l] if t < tiles - 1 else s.scattered, 16)
                pool.wait_ge(acc_cleared[l], 16 * (tiles - 1))
                with pool.Fori(0, E) as e:
                    pool.wait_ge(s.x_turned, s.n.x_turned + e + 1)
                    pool.wait_ge(s.gathered, s.n.gathered + e * 16 + 16)
                    g.tensor_copy(IDXG[0:n, :], IDXT[0:n, bass.ds(e + 1, 1)]).then_inc(s.idx_next, 1)
                    pool.wait_ge(s.idx_next, s.n.idx_next + e + 1)
                    apart(pool)
                    pool.indirect_dma_start(XG[0:n, :], None, XH[l], bass.IndirectOffsetOnAxis(IDXG[0:n, 0:1], 0)
                                            ).then_inc(s.gathered, 16)
                    pool.wait_ge(s.scattered, s.n.scattered + e * 16 + 16)
                    g.tensor_copy(IDXS[0:n, :], IDXT[0:n, bass.ds(e, 1)])
                    g.tensor_copy(GCUR[0:n, :], GATET[0:n, bass.ds(e, 1)]).then_inc(s.routes, 1)
                    pool.wait_ge(s.routes, s.n.routes + e + 1)
                    pool.wait_ge(s.y_act, s.n.y_act + e + 2)
                    pool.wait_ge(s.y_dve, s.n.y_dve + e + 2)
                    apart(pool)
                    pool.indirect_dma_start(ACC[l], bass.IndirectOffsetOnAxis(IDXS[0:n, 0:1], 0), Y[0:n, :], None,
                                            compute_op=ALU.add).then_inc(s.scattered, 16)
                pool.wait_ge(s.scattered, s.n.scattered + 16 * (E + 1))
                pool.wait_ge(s.gathered, s.n.gathered + 16 * (E + 1))
                pool.wait_ge(s.h_turned, s.n.h_turned + E)
                buf = xr(0, 2, D)
                for t in range(tiles):
                    if t >= 2:
                        pool.wait_ge(s.added, s.n.added + t - 1)
                    pool.dma_start(buf[:, t % 2, :], ACC[l][t * P:(t + 1) * P, :]).then_inc((s.readback0, s.readback1)[t % 2], 16)

            pool_after(g.memset(WZ[:, :, :], 0.0))
            wv = A["gla_w_in"][0].rearrange("(p k) n -> p k n", p=P)
            pool.dma_start(WZ[:, :, 0:16], wv[:, :, 3072:3088]).then_inc(wz_loaded, 16)
            pool.dma_start(WZ[:, :, 32:48], wv[:, :, 3088:3104]).then_inc(wz_loaded, 16)
            pool.wait_ge(wz_loaded, 32)
            end(pool, "pool")
            for n in (1, 2):
                begin(pool, "pool", n)
                end(pool, "pool")
            begin(pool, "pool", 3)
            pool.wait_ge(bias_loaded, 16 * 2 * B_H)
            for half in range(2):
                b = BIAS[half * GRID_W:(half + 1) * GRID_W, :].rearrange("p (s c) -> p s c", c=GRID_W)
                w = GRID_W - NA_COLS
                pool_after(g.affine_select(out=b[:, :, 0:w], in_=b[:, :, 0:w], compare_op=ALU.is_ge, fill=MASKED,
                                           base=NA_COLS // 2 - (GRID_W - 1), pattern=[[0, B_H * NSH], [1, w]], channel_multiplier=1))
                pool_after(g.affine_select(out=b[:, :, NA_COLS:], in_=b[:, :, NA_COLS:], compare_op=ALU.is_ge, fill=MASKED,
                                           base=(GRID_W - 1) + NA_COLS // 2 - 1 - NA_COLS, pattern=[[0, B_H * NSH], [-1, w]],
                                           channel_multiplier=-1))
            pool.drain().then_inc(bias_masked, 1)
            end(pool, "pool")
            begin(pool, "pool", 4)
            end(pool, "pool")
            begin(pool, "pool", 5)
            store_rows(0, TT)
            end(pool, "pool")
            begin(pool, "pool", 6)
            experts(0)
            end(pool, "pool")
            for n in range(7, 13):
                begin(pool, "pool", n)
                end(pool, "pool")
            begin(pool, "pool", 13)
            store_rows(1, LT)
            end(pool, "pool")
            begin(pool, "pool", 14)
            experts(1)
            end(pool, "pool")


_INS = ["x", "c", "ctx", "c_ctx", "ada_w", "ada_b", "norm1_g", "norm2_g", "attn_w_in", "attn_w_out",
        "a_q_norm", "a_k_norm", "b_q_norm", "b_k_norm", "na_rpb", "gla_w_in", "gla_gk_w_f", "gla_gk_b_f",
        "gla_gk_w_b", "gla_gk_b_b", "gla_o_norm", "gla_w_out", "moe_router", "moe_w_gate", "moe_w_up", "moe_w_down"]


def kernel(**inputs):
    import numpy as _np
    import concourse.bacc as _bacc
    from concourse import mybir as _mybir
    from concourse.bass_utils import run_bass_kernel_spmd as _run

    nc = _bacc.Bacc("TRN2", target_bir_lowering=False, num_devices=1)
    arrays, args = {}, {}
    for name in _INS:
        a = _np.ascontiguousarray(inputs[name])
        arrays[f"in_{name}"] = a
        args[name] = nc.dram_tensor(f"in_{name}", a.shape, _mybir.dt.from_np(a.dtype), kind="ExternalInput").ap()
    a = shape_constants()
    arrays["in_shape_constants"] = a
    args["shape_constants"] = nc.dram_tensor("in_shape_constants", a.shape, _mybir.dt.from_np(a.dtype),
                                             kind="ExternalInput").ap()
    out = nc.dram_tensor("out_0", (LAT, D), _mybir.dt.float32, kind="ExternalOutput").ap()
    build(nc, args, out)
    r = _run(nc, [arrays], core_ids=[0])
    return r.results[0]["out_0"].reshape(1, LAT, D)
```

```python
from collections import namedtuple
from contextlib import ExitStack

import numpy as np
import concourse.bass as bass
from concourse import mybir

F32R = mybir.dt.float32r
WBUF = 4
F32 = mybir.dt.float32
U32 = mybir.dt.uint32
I32 = mybir.dt.int32
ALU = mybir.AluOpType
ACT = mybir.ActivationFunctionType
X_AXIS = mybir.AxisListType.X


def named(**things):
    return namedtuple("Named", list(things))(**things)


P = 128
D = 1024
KD = D // P
LAT, CTX = 512, 256
TOK = LAT + CTX
LT, CT = LAT // P, CTX // P
TT = LT + CT
HD = 64
A_H, A_KV, B_H = 8, 2, 8
ATTN_IN = A_H * HD + 2 * A_KV * HD + 3 * B_H * HD
GRID_W, ROWS, NA_COLS = 64, LAT // 64, 16
DR, DC = 15, 31
E = 16
FF = 1024
CAP_L, CAP_C = 2 * LAT // E, 2 * CTX // E
G_H, G_DK, G_DV, CHUNK = 4, 128, 256, 64
EPS = 1e-6
MASKED = -1e30
BW = 512
SLOTS = 6
SLOT = 4096
NSH = DR - 1

C_ID, C_ROPE, C_MASKF, C_MASKB, C_RESET = 0, 128, 128 + LT * 128, 256 + LT * 128, 384 + LT * 128
C_FLIP = C_RESET + LAT
C_ALL = C_FLIP + P


def shape_constants():
    t = np.arange(LAT)
    half = HD // 2
    inv = (np.float32(10000.0) ** (-np.arange(0, half, 2, dtype=np.float32) / np.float32(half))).astype(np.float32)
    out = np.zeros((P, C_ALL), np.float32)
    out[:, C_ID:C_ID + P] = np.eye(P)
    tabs = []
    for pos in (t // GRID_W, t % GRID_W):
        ang = pos.astype(np.float32)[:, None] * inv[None, :]
        tabs.append((np.cos(ang), np.sin(ang)))
    cos = np.concatenate([tabs[0][0], tabs[0][0], tabs[1][0], tabs[1][0]], 1)
    sin = np.concatenate([-tabs[0][1], tabs[0][1], -tabs[1][1], tabs[1][1]], 1)
    rope = np.concatenate([cos, sin], 1).reshape(LT, P, 2 * HD).transpose(1, 0, 2)
    out[:, C_ROPE:C_ROPE + LT * P] = rope.reshape(P, LT * P)
    j, i = np.arange(P)[:, None], np.arange(P)[None, :]
    same = j // CHUNK == i // CHUNK
    out[:, C_MASKF:C_MASKF + P] = same & (i >= j)
    out[:, C_MASKB:C_MASKB + P] = same & (i <= j)
    out[:, C_RESET:C_RESET + LAT] = (t % CHUNK != 0)[None, :]
    out[:, C_FLIP:] = np.kron(np.eye(2), np.eye(GRID_W)[::-1])
    return out


def build(nc, A, out, stop=None):
    ctx = ExitStack()
    with ctx:
        def sb(name, shape, dt=F32):
            return ctx.enter_context(nc.sbuf_tensor(name, shape, dt))

        def sem(name):
            return ctx.enter_context(nc.semaphore(name))

        H = sb("H", [P, TT, D])
        RING = sb("RING", [P, SLOTS, SLOT])
        CONST = sb("CONST", [P, C_ALL])
        VCOL = sb("VCOL", [P, 2, 88])
        SC = sb("SC", [P, KD, 2])
        SCT = sb("SCT", [P, 2, KD, 2])
        MCOL = sb("MCOL", [P, 2, 48, 2])
        ACOL = sb("ACOL", [P, 2, 2, KD, 2])
        MROW = sb("MROW", [P, 2, D])
        GA = sb("GA", [P, 2, HD])
        GB = sb("GB", [P, 2])
        RW = sb("RW", [P, 2, KD, E])
        ONORM = sb("ONORM", [P, G_DV])
        GKW = sb("GKW", [48, G_H * G_DK])
        WZ = sb("WZ", [P, KD, 48])
        STAT = sb("STAT", [P, 320])
        PS = ctx.enter_context(nc.psum_tensor("PS", [P, 8 * BW], F32))

        def bank(b, n=1):
            return PS[:, b * BW:(b + n) * BW]

        ident = CONST[:, C_ID:C_ID + P]

        RPB = nc.dram_tensor("rpb_scratch", (96 + B_H * DR * DC + 96,), F32, kind="Internal").ap()
        XH = [nc.dram_tensor(f"xhat_{l}", ((TOK, LAT)[l], D), F32, kind="Internal").ap() for l in range(2)]
        ACC = [nc.dram_tensor("residual_0", (TOK, D), F32, kind="Internal").ap(), out]

        ACT_CONSTS, POOL_CONSTS = 16 * 4, 16 * 16

        passed = sem("passed")

        plan = [(("ada", 0, c), c) for c in range(4)]
        plan += [(("win", c), c % 2) for c in range(5)]
        plan += [(("ada", l, c), 5) for l in range(2) for c in range(12) if (0, 3) < (l, c) < (1, 8)]
        plan += [(("wout", 0, h), s) for h, s in enumerate((2, 5))]
        plan += [(("ada", 1, 8 + h), s) for h, s in enumerate((2, 5))]
        plan += [(("moe", 0, e, s), s) for e in range(E) for s in range(SLOTS)]
        plan += [(("gla", c), 3 + c % 3) for c in range(6)]
        plan += [(("wout", 1, h), s) for h, s in enumerate((5, 3))]
        plan += [(("ada", 1, 10 + h), s) for h, s in enumerate((5, 3))]
        plan += [(("moe", 1, e, s), s) for e in range(E) for s in range(SLOTS)]
        place, filled = {}, [0] * SLOTS
        for name, s in plan:
            place[name] = (s, filled[s])
            filled[s] += 1

        slot_full = [sem(f"slot_full{s}") for s in range(SLOTS)]
        slot_free = [sem(f"slot_free{s}") for s in range(SLOTS)]
        consts_loaded, small_loaded = sem("consts_loaded"), sem("small_loaded")
        engine_done = {k: sem(f"phase_done_{k}") for k in ("pe", "dve", "act", "pool")}

        def slot(name, k=KD):
            return RING[:, place[name][0], :].rearrange("p (k n) -> p k n", k=k)

        def wait_full(eng, name):
            s, n = place[name]
            eng.wait_ge(slot_full[s], 16 * (n + 1))

        GU, DN = 16, 8

        def first_slice(e):
            if isinstance(e, int):
                return min(max(0, e * (GU + DN) - DN), E * (GU + DN))
            return e * (GU + DN) - DN

        def slices(e):
            last = isinstance(e, int) and e == E
            first = isinstance(e, int) and e == 0
            gu = [] if last else [(i, i // 4, i % 4, e) for i in range(GU)]
            dn = [] if first else [(i, i // 4, i % 4, e - 1) for i in range(GU, GU + DN)]
            return [(x - (GU if last else 0), *rest) for x, *rest in gu + dn]

        def buffer_of(e, i):
            return (first_slice(e) + i) % WBUF if isinstance(e, int) else (first_slice(1) + i) % WBUF

        def parts_done(e, i):
            if isinstance(e, int):
                g = first_slice(e) + i
                return g - g // 4 + (0 if g % 4 == 3 else 1)
            g = first_slice(1) + i
            return (e - 1) * 18 + g - g // 4 + (0 if g % 4 == 3 else 1)

        def apart(eng):
            eng.sem_inc(passed, 1)

        def free(name):
            return slot_free[place[name][0]]

        def begin(eng, me, n):
            for k, s in engine_done.items():
                if k != me:
                    eng.wait_ge(s, n)

        def end(eng, me):
            eng.drain().then_inc(engine_done[me], 1)

        h_loaded = sem("h_loaded")
        bias_copied = sem("bias_copied")
        bias_loaded = sem("bias_loaded")
        bias_masked = sem("bias_masked")
        vec_loaded = sem("vec_loaded")
        bias_flipped, bias_evac_dve, bias_evac_act = sem("bias_flipped"), sem("bias_evac_dve"), sem("bias_evac_act")
        dve_step, act_step, pool_step = sem("dve_step"), sem("act_step"), sem("pool_step")
        cond_ready, cond_exp = sem("cond_ready"), sem("cond_exp")
        steps = {"dve": 0, "act": 0, "pool": 0}

        def dve_after(ins):
            steps["dve"] += 1
            ins.then_inc(dve_step, 1)
            nc.vector.wait_ge(dve_step, steps["dve"])

        def act_after(ins):
            steps["act"] += 1
            ins.then_inc(act_step, 1)
            nc.scalar.wait_ge(act_step, steps["act"])

        def pool_after(ins):
            steps["pool"] += 1
            ins.then_inc(pool_step, 1)
            nc.gpsimd.wait_ge(pool_step, steps["pool"])

        def group(tag, *names):
            return named(**{n: sem(f"{n}_{tag}") for n in names})

        def uses(sems, counts):
            sems = sems._asdict()
            out, before = [], {k: 0 for k in sems}
            for c in counts:
                out.append(named(**sems, n=named(**before)))
                before = {k: before[k] + c[k] for k in before}
            return out

        ada_s = group("ada", "product", "rows", "turned", "cols")
        norm_s = dict(zip(((0, 0), (0, 1), (1, 0), (1, 1)), uses(
            group("norm", "sumsq", "inverse", "rstd", "xhat", "turned", "evac_act", "evac_dve", "stored0", "stored1"),
            [dict(sumsq=t, inverse=1, rstd=1, xhat=t, turned=t, evac_act=t, evac_dve=t, stored0=8 * t * w,
                  stored1=8 * t * w) for t, w in ((TT, 0), (TT, 1), (TT, 0), (LT, 1))])))
        prj = group("prj", "product", "squares", "inverse", "rstd", "v_out", "scaled", "stage",
                    "turned", "evac")
        att = group("att", "scores", "biased", "negmax", "probs", "normal", "turned", "evac_act",
                    "evac_dve", "mixed", "evac_mix")
        outp = uses(group("out", "gate_turned", "gate_act", "product", "added"),
                    [dict(gate_turned=1, gate_act=1, product=t, added=t) for t in (TT, LT)])
        routing = ("logits", "shifted", "exps", "aff", "turned", "packed", "routed", "gate_turned", "gate_act")
        rt = uses(group("route", *routing), [dict.fromkeys(routing, 1)] * 2)
        once = ("silu", "hidden", "h_turned", "routes", "idx_next", "ht_high", "ht_low", "weighed")
        ahead = ("x_turned", "xt_act", "xt_dve", "xt_high", "xt_low")
        moe = uses(group("moe", "gathered", "scattered", "readback0", "readback1", *once, *ahead,
                         "padded", "high", "low", "used"),
                   [dict(gathered=16 * (E + 1), scattered=16 * (E + 1), readback0=16, readback1=16,
                         padded=1, high=24 * E, low=18 * E, used=24 * E, **dict.fromkeys(once, E), **dict.fromkeys(ahead, E + 1)) for t in (TT, LT)])
        gp = group("gp", "product", "evac_act", "z_out", "gate_x", "gate_abs", "gate_exp", "gate_ln", "cum", "raw")
        gs = group("gs", "e_pos", "e_neg", "diff", "e_diff", "qdec", "kinv", "kst", "kturned", "kst_out",
                   "s0", "s0_out", "a_done", "a_out", "upd", "state", "o_done", "o_out")
        mg = group("mg", "squares", "inverse", "rstd", "scaled", "turned", "evac")

        block = ctx.enter_context(nc.Block())

        wout_a2 = sem("wout_a2")
        wz_loaded = sem("wz_loaded")
        IDXT, GATET = sb("IDXT", [96, E + 1], I32), sb("GATET", [96, E])
        IDXG, IDXS, GCUR = sb("IDXG", [96, 1], I32), sb("IDXS", [96, 1], I32), sb("GCUR", [96, 1])

        NSLOT = [CAP_L + CAP_C, CAP_L]
        NPAD = CAP_L + CAP_C

        with ExitStack() as shared:
            UT = shared.enter_context(nc.sbuf_tensor("UT", [P, KD, TOK], F32))
            XR = shared.enter_context(nc.sbuf_tensor("XR", [P, 9984], F32))
        WSPLIT = sb("WSPLIT", [P, WBUF, 2, D], F32R)
        sb("XR_below", [P, KD * TOK + 9984 - 2 * WBUF * D - 4 * KD * NPAD])
        XSPLIT = sb("XSPLIT", [P, 2, KD, NPAD], F32R)
        HSPLIT = sb("HSPLIT", [P, 2, KD, NPAD], F32R)

        def xr(at, *shape):
            n = int(np.prod(shape))
            assert at + n <= 9984
            v = XR[:, at:at + n]
            return v if len(shape) == 1 else v.rearrange(
                "p (a b) -> p a b" if len(shape) == 2 else "p (a b c) -> p a b c",
                **dict(zip("abc", shape)))

        def ada_steps(l, vectors):
            return [x for v in vectors for x in (("chunk", l, 2 * v), ("chunk", l, 2 * v + 1), ("turn", l, v))]

        ada_at = {(0, i): [x] for i, x in enumerate(ada_steps(0, (0, 1)))}
        ada_at |= {(2, 2 * i + 1): [x] for i, x in enumerate(ada_steps(0, (2, 3, 4, 5)))}
        ada_at |= {(3, 7 * i + 3): [x] for i, x in enumerate(ada_steps(1, range(4)))}
        ada_at |= {("route", 0, i): [x] for i, x in enumerate(ada_steps(1, (4,)))}
        ada_at |= {("route", 1, i): [x] for i, x in enumerate(ada_steps(1, (5,)))}
        ADA_ROWS = XR[0:2, 8800:9824]

        V = xr(0, TT, (A_KV + B_H) * HD)
        QK_A = RING[:, 2, 0:5 * TOK].rearrange("p (j t) -> p j t", j=5)
        QK_B = RING[:, 3:5, :].rearrange("p s n -> p (s n)")[:, 0:8 * TOK].rearrange("p (j t) -> p j t", j=8)

        def qk(j, n=1):
            return QK_A[:, j:j + n] if j < 5 else QK_B[:, j - 5:j - 5 + n]

        BIAS = RING[:, 0:2, :].rearrange("p s n -> p (s n)")[:, 0:B_H * NSH * GRID_W]
        BIAS_N = B_H * NSH * GRID_W // BW
        PROB = xr(3840, 3, TOK)
        PROBT = xr(3840 + 3 * TOK, 2, TOK)
        SQ = xr(3840, 2, BW)
        STAGE = xr(3840 + 1024, 2, BW)
        ROT = xr(3840 + 2048, BW)
        STAGE2 = xr(3840 + 2560, 2, BW)
        TILE_ORDER = (0, 4, 1, 2, 5, 3)
        heads = [named(head=h, t=t, base=HD * (h // 4), q=h % 4, k=4, v=0, mix=h % 4, biased=False)
                 for h in range(A_H) for t in TILE_ORDER]
        N_A = len(heads)
        heads += [named(head=h, t=t, base=HD * (h % 2), q=5 + h // 2, k=9 + h // 2, v=P + (h // 2) * P, mix=4 + h // 2,
                        biased=t < LT) for h in range(B_H) for t in TILE_ORDER]
        ring012 = RING[:, 0:3, :].rearrange("p s n -> p (s n)")
        GV = ring012[:, 0:TT * D].rearrange("p (t n) -> p t n", t=TT)
        OG = ring012[:, TT * D:(TT + LT) * D].rearrange("p (t n) -> p t n", t=LT)
        GQ = ring012[:, (TT + LT) * D:].rearrange("p (j n) -> p j n", j=G_H)
        GK = xr(0, G_H, TOK)
        CUM = [xr(3072, G_H, TOK), xr(6144, G_H, TOK)]
        GLN, ZT = MROW[:, 0, 0:TOK], MROW[0:48, 1, 0:TOK]
        GO = UT[:, :, :].rearrange("p k t -> p (k t)")[:, 0:LT * D].rearrange("p (t n) -> p t n", t=LT)
        OT = RING[:, 4, :].rearrange("p (k t) -> p k t", k=KD)
        gates = [(d, j) for d in range(2) for j in range(G_H)]

        def lane(d):
            r = RING[:, 3 + d, :]
            return named(QZ=r[:, 0:1024], TMP=r[:, 1024:1792], KI=r[:, 1792:2304], KS=r[:, 2304:3072],
                         AT=r[:, 3072:3584], S=r[:, 3584:4096].rearrange("p (b e) -> p b e", b=2),
                         DEC=STAT[:, 80 + 8 * d:88 + 8 * d],
                         qz=lambda t, eo: r[:, (2 * t + eo) * P:(2 * t + eo + 1) * P],
                         qview=lambda t: r[:, 2 * t * P:2 * t * P + 384].rearrange("p (e x) -> p e x", e=2)[:, :, 0:CHUNK])

        lanes = [lane(0), lane(1)]

        def lane_o(h, d, pair):
            return 2 * LT * h + 2 * pair + d + 1

        def lane_state(h, d, i):
            return 2 * (2 * LT - 1) * h + 2 * i + d + 1

        def by_slice(row):
            return row.rearrange("p (x k) -> p k x", k=KD)

        MSR = STAT[:, 0:16]
        PH = STAT[:, 16:64]
        SM = STAT[:, 64:80]
        xhat = xr(0, TT, D)
        sq_junk = xr(6144, D)

        @block.sync
        def _(sp):
            def load(name, src, dst=None):
                s, n = place[name]
                if n:
                    sp.wait_ge(slot_free[s], n)
                sp.dma_start(slot(name) if dst is None else dst, src).then_inc(slot_full[s], 16)

            def load_ada(l, c):
                load(("ada", l, c), A["ada_w"][l].rearrange("(p k) n -> p k n", p=P)[:, :, c * BW:(c + 1) * BW])

            def after_phase(n):
                for done in engine_done.values():
                    sp.wait_ge(done, n)

            def load_experts(l, ready):
                w3 = [A[w][l].rearrange("e (p k) n -> p e k n", p=P)
                      for w in ("moe_w_gate", "moe_w_up", "moe_w_down")]

                def half_matrix(s, e):
                    return w3[s // 2][:, bass.ds(e, 1) if not isinstance(e, int) else slice(e, e + 1),
                                      4 * (s % 2):4 * (s % 2) + 4, :].rearrange("p e k n -> p (e k) n")

                for s, wait in ready:
                    wait()
                    sp.wait_ge(slot_free[s], place[("moe", l, 0, s)][1])
                    sp.dma_start(RING[:, s, :].rearrange("p (k n) -> p k n", k=4), half_matrix(s, 0)).then_inc(slot_full[s], 16)

                def refill(slots, e):
                    for s in slots:
                        sp.wait_ge(slot_free[s], e + place[("moe", l, 0, s)][1])
                        sp.dma_start(RING[:, s, :].rearrange("p (k n) -> p k n", k=4), half_matrix(s, e)
                                     ).then_inc(slot_full[s], 16)

                refill(range(4), 1)
                with sp.Fori(2, E) as e:
                    refill(range(4), e)
                    refill(range(4, 6), e - 1)
                refill(range(4, 6), E - 1)

            def load_win(c):
                lo, hi = c * BW, min((c + 1) * BW, ATTN_IN)
                load(("win", c), A["attn_w_in"][0].rearrange("(p k) n -> p k n", p=P)[:, :, lo:hi],
                     slot(("win", c))[:, :, 0:hi - lo])

            load_ada(0, 0)
            sp.wait_ge(consts_loaded, ACT_CONSTS)
            load_ada(0, 1)
            for c in range(2, 4):
                load_ada(0, c)
            sp.dma_start(H[:, 0:LT, :], A["x"][0].rearrange("(t p) d -> p t d", p=P)).then_inc(h_loaded, 16)
            sp.dma_start(H[:, LT:TT, :], A["ctx"][0].rearrange("(t p) d -> p t d", p=P)).then_inc(h_loaded, 16)
            for c in (0, 1):
                load_win(c)
            for i, c in enumerate(range(4, 12)):
                load_ada(0, c)
                if i in (1, 3, 5):
                    load_win(2 + i // 2)
            load_ada(1, 0)
            after_phase(3)
            sp.wait_ge(bias_copied, 48)
            for half in range(2):
                for h in range(B_H):
                    src = bass.AP(RPB.tensor, 96 + h * DR * DC + (1 - half) * DC + NA_COLS - GRID_W,
                                  [[1, GRID_W], [DC, NSH], [1, GRID_W]])
                    sp.dma_start(BIAS[half * GRID_W:(half + 1) * GRID_W, h * NSH * GRID_W:(h + 1) * NSH * GRID_W]
                                 .rearrange("p (s c) -> p s c", s=NSH), src).then_inc(bias_loaded, 16)
            for c in range(1, 7):
                load_ada(1, c)
            sp.wait_ge(att.scores, N_A)
            dst = RING[:, place[("wout", 0, 0)][0], :].rearrange("p (k n) -> p k n", k=4)
            for a, arrived in enumerate((slot_full[place[("wout", 0, 0)][0]], wout_a2)):
                sp.dma_start(dst[a * HD:(a + 1) * HD],
                             A["attn_w_out"][0][a * 256:(a + 1) * 256, :].rearrange("(j p) n -> p j n", p=HD)
                             ).then_inc(arrived, 16)
            load_ada(1, 7)

            load(("wout", 0, 1), A["attn_w_out"][0][512:1024, :].rearrange("(k p) n -> p k n", p=P),
                 slot(("wout", 0, 1), 4))
            load_experts(0, [(s, {0: lambda: sp.wait_ge(att.biased, B_H * LT),
                                  3: lambda: after_phase(4),
                                  2: lambda: [load_ada(1, c) for c in (8, 9)]}.get(s, lambda: None)) for s in (0, 1, 3, 4, 2, 5)])
            w = A["gla_w_in"][0].rearrange("(p k) n -> p k n", p=P)
            for c in range(6):
                load(("gla", c), w[:, :, c * BW:(c + 1) * BW])
                if c == 0:
                    sp.wait_ge(moe[0].readback0, 16)
                    sp.wait_ge(moe[0].readback1, 16)
            after_phase(11)
            for h in range(2):
                load(("wout", 1, h), A["gla_w_out"][0][h * 512:(h + 1) * 512, :].rearrange("(k p) n -> p k n", p=P),
                     slot(("wout", 1, h), 4))
            load_experts(1, [(s, {0: lambda: after_phase(12),
                                  1: lambda: [load_ada(1, c) for c in (10, 11)],
                                  4: lambda: after_phase(13)}.get(s, lambda: None)) for s in (0, 1, 2, 5, 3, 4)])
            after_phase(15)

        @block.tensor
        def _(pe):
            mm = nc.tensor.matmul

            def ada(where):
                for what, l, i in ada_at.get(where, ()):
                    if what == "chunk":
                        g = 12 * l + i
                        wait_full(pe, ("ada", l, i))
                        if g:
                            pe.wait_ge(ada_s.rows, g)
                        if g % 2 == 0 and g:
                            pe.wait_ge(ada_s.cols, g // 2)
                        for k in range(KD):
                            last = mm(bank(7)[0:2, :], SC[:, k, :], slot(("ada", l, i))[:, k, :],
                                      start=(k == 0), stop=(k == KD - 1))
                        last.then_inc(ada_s.product, 1)
                        pe.drain().then_inc(free(("ada", l, i)), 1)
                    else:
                        pe.wait_ge(ada_s.rows, 12 * l + 2 * i + 2)
                        for k in range(KD):
                            last = nc.tensor.transpose(bank(7)[:, 2 * k:2 * k + 2], ADA_ROWS[:, k::KD], ident[0:2, 0:2])
                        last.then_inc(ada_s.turned, 1)

            def norm_turn(l, w, tiles):
                s = norm_s[(l, w)]

                def logits(t):
                    pe.wait_ge(s.evac_act, s.n.evac_act + t + 1)
                    pe.wait_ge(s.evac_dve, s.n.evac_dve + t + 1)
                    for k in range(KD):
                        last = mm(bank(4)[:, t * E:(t + 1) * E], UT[:, k, t * P:(t + 1) * P], RW[:, l, k, :],
                                  start=(k == 0), stop=(k == KD - 1))
                    if t == tiles - 1:
                        last.then_inc(rt[l].logits, 1)

                for t in range(tiles):
                    pe.wait_ge(s.xhat, s.n.xhat + t + 1)
                    if t >= 2:
                        pe.wait_ge(s.evac_act, s.n.evac_act + t - 1)
                        pe.wait_ge(s.evac_dve, s.n.evac_dve + t - 1)
                    for k in range(KD):
                        last = nc.tensor.transpose(bank(2 * (t % 2) + k // 4)[:, (k % 4) * P:(k % 4 + 1) * P],
                                                   xhat[:, t, k::KD], ident)
                    last.then_inc(s.turned, 1)
                    if w and t:
                        logits(t - 1)
                if w:
                    logits(tiles - 1)

            def gate_rows(s, l, vec, b0):
                for w in range(2):
                    for k in range(KD):
                        last = mm(bank(b0 + 2 * w + k // 4)[:, (k % 4) * P:(k % 4 + 1) * P],
                                  MCOL[:, l, vec * KD + k, w:w + 1].to_broadcast([P, P]), ident, start=True, stop=True)
                last.then_inc(s.gate_turned, 1)

            def out_projection(l, tiles, MIXT):
                s = outp[l]
                gate_rows(s, l, 2, 4)
                wait_full(pe, ("wout", l, 0))
                if l == 0:
                    pe.wait_ge(wout_a2, 16)
                wait_full(pe, ("wout", l, 1))
                for t in range(tiles):
                    if t >= 2:
                        pe.wait_ge(s.added, s.n.added + t - 1)
                    for n in range(2):
                        for k in range(KD):
                            wv = RING[:, place[("wout", l, k // 4)][0], :].rearrange("p (k n) -> p k n", k=4)
                            last = mm(bank(2 * (t % 2) + n), MIXT[:, k, t * P:(t + 1) * P],
                                      wv[:, k % 4, n * BW:(n + 1) * BW], start=(k == 0), stop=(k == KD - 1))
                    last.then_inc(s.product, 1)
                pe.drain().then_inc(free(("wout", l, 0)), 1)
                pe.drain().then_inc(free(("wout", l, 1)), 1)

            def route(l, tiles):
                s = rt[l]
                pe.wait_ge(s.aff, s.n.aff + 1)
                for t in range(tiles):
                    last = nc.tensor.transpose(bank(5 + t // 4)[0:48, (t % 4) * P:(t % 4 + 1) * P],
                                               xr(7300, TT, 48)[:, t, :], ident)
                last.then_inc(s.turned, 1)
                if l == 0:
                    gate_rows(s, l, 5, 0)
                for i in range(3):
                    ada(("route", l, i))
                if l == 1:
                    pe.wait_ge(ada_s.cols, 12)
                    gate_rows(s, l, 5, 0)
                pe.wait_ge(s.packed, s.n.packed + 1)
                n = NSLOT[l]
                for i in range(2):
                    last = nc.tensor.transpose(bank(4)[0:n, 128 + i * E:128 + (i + 1) * E],
                                               STAT[0:E, 96 + i * 96:96 + i * 96 + n], ident[0:E, 0:E])
                last.then_inc(s.routed, 1)

            def experts(l):
                s, n = moe[l], NSLOT[l]
                XG, HID = xr(2048, D), xr(3840, D)

                def turn_rows(src, done):
                    for k in range(KD):
                        last = nc.tensor.transpose(bank(6 + k // 4)[:, (k % 4) * P:(k % 4) * P + n],
                                                   src[0:n, k::KD], ident[0:n, 0:n])
                    last.then_inc(done, 1)

                def product(e, i, sl, k, first, out, X):
                    if k == 3:
                        pe.wait_ge(slot_free[sl], place[("moe", l, 0, sl)][1] + 1 + (e if sl < 4 else e - 1))
                    else:
                        pe.wait_ge(s.low, s.n.low + parts_done(e, i))
                    w, kk = WSPLIT[:, buffer_of(e, i)], (sl % 2) * 4 + k
                    for x_part, w_part in ((0, 0), (0, 1), (1, 0)):
                        for nn in range(2):
                            last = mm(bank(out + nn)[0:NPAD, :], X[:, x_part, kk, :], w[:, w_part, nn * BW:(nn + 1) * BW],
                                      start=(kk == 0 and x_part + w_part == 0), stop=(kk == KD - 1 and x_part == 1))
                    last.then_inc(s.used, 1)

                def step(e):
                    first, final = isinstance(e, int) and e == 0, isinstance(e, int) and e == E
                    for i, sl, k, _ in slices(e):
                        if sl == 0 and k == 0:
                            pe.wait_ge(s.xt_low, s.n.xt_low + e + 1)
                        if sl == 2 and k == 0:
                            pe.wait_ge(s.gathered, s.n.gathered + e * 16 + 32)
                            if not first:
                                pe.wait_ge(s.ht_low, s.n.ht_low + e)
                            apart(pe)
                            turn_rows(XG, s.x_turned)
                        if sl == 4 and k == 0:
                            pe.wait_ge(s.ht_low, s.n.ht_low + e)
                            if not (isinstance(e, int) and e == 1):
                                pe.wait_ge(s.weighed, s.n.weighed + e - 1)
                        product(e, i, sl, k, first, (0, 2, 4)[sl // 2], XSPLIT if sl < 4 else HSPLIT)
                    if not final:
                        pe.wait_ge(s.hidden, s.n.hidden + e + 1)
                        pe.wait_ge(s.xt_act, s.n.xt_act + e + 2)
                        pe.wait_ge(s.xt_dve, s.n.xt_dve + e + 2)
                        apart(pe)
                        turn_rows(HID, s.h_turned)

                pe.wait_ge(s.gathered, s.n.gathered + 16)
                turn_rows(XG, s.x_turned)
                pe.wait_ge(s.padded, s.n.padded + 1)
                step(0)
                step(1)
                with pe.Fori(2, E) as e:
                    step(e)
                step(E)

            pe.wait_ge(cond_ready, 1)
            pe.wait_ge(consts_loaded, ACT_CONSTS)
            for i in range(6):
                ada((0, i))
            end(pe, "pe")
            begin(pe, "pe", 1)
            norm_turn(0, 0, TT)
            end(pe, "pe")
            begin(pe, "pe", 2)
            units = [(c, t) for c in range(5) for t in range(TT)]

            def turn_heads(u):
                c, t = units[u]
                if c == 4:
                    return
                pe.wait_ge(prj.stage, u + 1)
                if u >= 2:
                    pe.wait_ge(prj.evac, u - 1)
                src = STAGE2[:, u % 2, :] if c < 2 else STAGE[:, u % 2, :]
                for cols in ((0, 1, 2, 3), (0, 2, 3), (0, 1, 2, 3), (0, 1))[c]:
                    last = nc.tensor.transpose(bank(4 + u % 2)[:, cols * P:(cols + 1) * P],
                                               src[:, cols * P:(cols + 1) * P], ident)
                last.then_inc(prj.turned, 1)

            for u, (c, t) in enumerate(units):
                w = min(BW, ATTN_IN - c * BW)
                if t == 0:
                    wait_full(pe, ("win", c))
                if u >= 4:
                    pe.wait_ge(prj.scaled, u - 3)
                    pe.wait_ge(prj.v_out, u - 3)
                for k in range(KD):
                    last = mm(bank(u % 4)[:, 0:w], UT[:, k, t * P:(t + 1) * P], slot(("win", c))[:, k, 0:w],
                              start=(k == 0), stop=(k == KD - 1))
                last.then_inc(prj.product, 1)
                if t == TT - 1:
                    pe.drain().then_inc(free(("win", c)), 1)
                if u:
                    turn_heads(u - 1)
                ada((2, u))
            end(pe, "pe")
            begin(pe, "pe", 3)
            def attend(first, N):
                for i in range(first, N + 3):
                    if i < N:
                        u = heads[i]
                        if i >= 2:
                            pe.wait_ge(att.probs, i - 1)
                        q = qk(u.q)[u.base:u.base + HD, 0, u.t * P:(u.t + 1) * P]
                        key = qk(u.k)[u.base:u.base + HD, 0]
                        b0 = 2 * (i % 2)
                        if u.t < LT:
                            mm(bank(b0), q, key[:, 0:LAT], start=True, stop=True)
                        mm(bank(b0 + 1)[:, 0:CTX], q, key[:, LAT:TOK], start=True, stop=True).then_inc(att.scores, 1)
                        ada((3, i))
                    j = i - 2
                    if first <= j < N:
                        u = heads[j]
                        pe.wait_ge(att.normal, j + 1)
                        if j >= 1:
                            pe.wait_ge(att.evac_act, j)
                            pe.wait_ge(att.evac_dve, j)
                        for kt in range(0 if u.t < LT else LT, TT):
                            last = nc.tensor.transpose(bank(4 + kt // 4)[:, (kt % 4) * P:(kt % 4 + 1) * P],
                                                       PROB[:, j % 3, kt * P:(kt + 1) * P], ident)
                        last.then_inc(att.turned, 1)
                    j = i - 3
                    if first <= j < N:
                        u = heads[j]
                        pe.wait_ge(att.evac_act, j + 1)
                        pe.wait_ge(att.evac_dve, j + 1)
                        if j >= 1:
                            pe.wait_ge(att.evac_mix, j)
                        kts = range(0 if u.t < LT else LT, TT)
                        for kt in kts:
                            last = mm(bank(6)[:, 0:P], V[:, kt, u.v:u.v + P],
                                      PROBT[:, j % 2, kt * P:(kt + 1) * P], start=(kt == kts[0]), stop=(kt == TT - 1))
                        last.then_inc(att.mixed, 1)

            attend(0, N_A)
            pe.wait_ge(bias_masked, 1)
            pe.wait_ge(att.probs, N_A)
            for i in range(BIAS_N):
                if i >= 4:
                    pe.wait_ge((bias_evac_dve, bias_evac_act)[i % 2], i // 2 - 1)
                mm(bank(i % 4), CONST[:, C_FLIP:C_FLIP + P], BIAS[:, i * BW:(i + 1) * BW], start=True, stop=True
                   ).then_inc(bias_flipped, 1)
            pe.wait_ge(bias_evac_dve, BIAS_N // 2)
            pe.wait_ge(bias_evac_act, BIAS_N // 2)
            attend(N_A, len(heads))
            end(pe, "pe")
            begin(pe, "pe", 4)
            out_projection(0, TT, UT)
            end(pe, "pe")
            begin(pe, "pe", 5)
            norm_turn(0, 1, TT)
            route(0, TT)
            end(pe, "pe")
            begin(pe, "pe", 6)
            experts(0)
            end(pe, "pe")
            begin(pe, "pe", 7)
            end(pe, "pe")
            begin(pe, "pe", 8)
            norm_turn(1, 0, TT)
            end(pe, "pe")
            begin(pe, "pe", 9)
            n_out = [0]

            def next_bank():
                i = n_out[0]
                if i >= 4:
                    pe.wait_ge(gp.evac_act, i - 3)
                n_out[0] += 1
                return bank(i % 4)

            for c in range(2):
                wait_full(pe, ("gla", c))
                for j in range(G_H):
                    for lo, hi in ((0, LAT), (LAT, TOK))[:1 + c]:
                        b = next_bank()
                        for k in range(KD):
                            last = mm(b[:, 0:hi - lo], slot(("gla", c))[:, k, j * P:(j + 1) * P], UT[:, k, lo:hi],
                                      start=(k == 0), stop=(k == KD - 1))
                        last.then_inc(gp.product, 1)
                pe.drain().then_inc(free(("gla", c)), 1)
            for lo, hi in ((0, LAT), (LAT, TOK)):
                b = next_bank()
                for k in range(KD):
                    last = mm(b[0:48, 0:hi - lo], WZ[:, k, :], UT[:, k, lo:hi], start=(k == 0), stop=(k == KD - 1))
                last.then_inc(gp.product, 1)
            pe.wait_ge(gp.evac_act, n_out[0])

            def gate_inputs(i):
                d, j = gates[i]
                b0 = 4 + 2 * (i % 2)
                if i >= 2:
                    pe.wait_ge(gp.gate_x, i - 1)
                    pe.wait_ge(gp.gate_abs, i - 1)
                for lo, hi in ((0, LAT), (LAT, TOK)):
                    last = mm(bank(b0, 2)[:, lo:hi], GKW[32 * d:32 * d + 16, j * P:(j + 1) * P],
                              ZT[32 * d:32 * d + 16, lo:hi], start=True, stop=True)
                last.then_inc(gp.raw, 1)

            for c in range(2, 6):
                wait_full(pe, ("gla", c))
                for t in range(TT if c < 4 else LT):
                    b = next_bank()
                    for k in range(KD):
                        last = mm(b, UT[:, k, t * P:(t + 1) * P], slot(("gla", c))[:, k, :],
                                  start=(k == 0), stop=(k == KD - 1))
                    last.then_inc(gp.product, 1)
                    if c < 4 and (c - 2) * TT + t < len(gates):
                        gate_inputs((c - 2) * TT + t)
                pe.drain().then_inc(free(("gla", c)), 1)
            end(pe, "pe")
            begin(pe, "pe", 10)
            for h in range(G_H):
                for d in range(2):
                    L = lanes[d]
                    n = 2 * h + d
                    b0 = 4 * d
                    pe.wait_ge(gs.kst, n + 1)
                    if h:
                        pe.wait_ge(gs.o_out, lane_o(h - 1, d, LT - 1))
                    for t in range(TT):
                        last = nc.tensor.transpose(bank(b0 + t // 4)[:, (t % 4) * P:(t % 4 + 1) * P],
                                                   L.KS[:, t * P:(t + 1) * P], ident)
                    last.then_inc(gs.kturned, 1)
                for d in range(2):
                    L = lanes[d]
                    n = 2 * h + d
                    b0 = 4 * d
                    pe.wait_ge(gs.kst_out, n + 1)
                    for i in range(CT):
                        last = mm(bank(b0 + 2)[:, 0:G_DV], L.KS[:, (LT + i) * P:(LT + i + 1) * P],
                                  GV[:, LT + i, h * G_DV:(h + 1) * G_DV], start=(i == 0), stop=(i == CT - 1))
                    last.then_inc(gs.s0, 1)
                    pe.wait_ge(gs.qdec, n + 1)
                    pe.wait_ge(gs.kinv, n + 1)
                    for t in range(LT):
                        last = mm(bank(b0)[:, t * P:(t + 1) * P], L.KI[:, t * P:(t + 1) * P], L.qview(t),
                                  start=True, stop=True)
                    last.then_inc(gs.a_done, 1)
                for d in range(2):
                    n = 2 * h + d
                    pe.wait_ge(gs.a_out, n + 1)
                    pe.wait_ge(gs.s0_out, n + 1)
                for i in range(2 * LT):
                    for d in range(2):
                        L = lanes[d]
                        b0 = 4 * d
                        c = i if d == 0 else 2 * LT - 1 - i
                        t, eo = c // 2, c % 2
                        ob = bank(b0 + 1 + 2 * ((i // 2) % 2))[:, 0:G_DV]
                        v = GV[:, t, h * G_DV:(h + 1) * G_DV]
                        if i % 2 == 0:
                            if i >= 4:
                                pe.wait_ge(gs.o_out, lane_o(h, d, i // 2 - 2))
                            mm(ob, L.AT[:, t * P:(t + 1) * P], v, start=True, stop=False)
                        if i:
                            pe.wait_ge(gs.state, lane_state(h, d, i - 1))
                        last = mm(ob, L.qz(t, eo), L.S[:, i % 2, :], start=False, stop=(i % 2 == 1))
                        if i % 2:
                            last.then_inc(gs.o_done, 1)
                        if i < 2 * LT - 1:
                            half = slice(eo * CHUNK, (eo + 1) * CHUNK)
                            mm(bank(b0 + 2)[:, 256:512], L.KS[half, t * P:(t + 1) * P],
                               GV[half, t, h * G_DV:(h + 1) * G_DV], start=True, stop=True).then_inc(gs.upd, 1)
            end(pe, "pe")
            begin(pe, "pe", 11)
            for t in range(LT):
                pe.wait_ge(mg.scaled, t + 1)
                if t >= 2:
                    pe.wait_ge(mg.evac, t - 1)
                for k in range(KD):
                    last = nc.tensor.transpose(bank(2 * (t % 2) + k // 4)[:, (k % 4) * P:(k % 4 + 1) * P],
                                               GO[:, t, k * P:(k + 1) * P], ident)
                last.then_inc(mg.turned, 1)
            end(pe, "pe")
            begin(pe, "pe", 12)
            out_projection(1, LT, OT)
            end(pe, "pe")
            begin(pe, "pe", 13)
            norm_turn(1, 1, LT)
            route(1, LT)
            end(pe, "pe")
            begin(pe, "pe", 14)
            experts(1)
            end(pe, "pe")

        @block.vector
        def _(dve):
            v = nc.vector

            def ada(where):
                for what, l, i in ada_at.get(where, ()):
                    if what == "turn":
                        dve.wait_ge(ada_s.turned, 6 * l + i + 1)
                        v.tensor_tensor(MCOL[:, l, i * KD:(i + 1) * KD, :],
                                        bank(7)[:, 0:16].rearrange("p (k w) -> p k w", w=2),
                                        VCOL[:, l, i * KD:(i + 1) * KD].unsqueeze(2).to_broadcast([P, KD, 2]),
                                        ALU.add).then_inc(ada_s.cols, 1)
                        if i in (1, 4):
                            dve.wait_ge(ada_s.cols, 6 * l + i + 1)
                            at = 48 + KD * (i // 3)
                            v.scalar_tensor_tensor(out=ACOL[:, l, i // 3], in0=MCOL[:, l, i * KD:(i + 1) * KD, :], scalar=1.0,
                                                   in1=VCOL[:, l, at:at + KD].unsqueeze(2).to_broadcast([P, KD, 2]),
                                                   op0=ALU.add, op1=ALU.mult)

            def norm(l, w, tiles):
                s = norm_s[(l, w)]
                dve.wait_ge(s.sumsq, s.n.sumsq + tiles)
                dve_after(v.tensor_scalar(MSR[:, 0:tiles], STAT[:, 304:304 + tiles], 1.0 / D, EPS, ALU.mult, ALU.add))
                v.reciprocal(STAT[:, 8:8 + tiles], MSR[:, 0:tiles]).then_inc(s.inverse, 1)
                dve.wait_ge(s.rstd, s.n.rstd + 1)
                for t in range(tiles + 1):
                    if t < tiles:
                        v.tensor_scalar(xhat[:, t, :], H[:, t, :], MSR[:, t:t + 1], None, ALU.mult).then_inc(s.xhat, 1)
                    if t:
                        u = t - 1
                        dve.wait_ge(s.turned, s.n.turned + u + 1)
                        st = 0 if u < LT else 1
                        for k in range(4, KD):
                            last = v.tensor_scalar(UT[:, k, u * P:(u + 1) * P],
                                                   bank(2 * (u % 2) + 1)[:, (k - 4) * P:(k - 3) * P],
                                                   ACOL[:, l, w, k, st:st + 1], MCOL[:, l, 3 * w * KD + k, st:st + 1],
                                                   ALU.mult, ALU.add)
                        last.then_inc(s.evac_dve, 1)

            def residual(l, tiles):
                s = outp[l]
                dve.wait_ge(s.gate_turned, s.n.gate_turned + 1)
                dve_after(v.tensor_copy(by_slice(MROW[:, 1, :]), bank(6, 2).rearrange("p (k x) -> p k x", k=KD)))
                dve.wait_ge(s.gate_act, s.n.gate_act + 1)
                tmp = xr(0, D)
                for t in range(tiles):
                    dve.wait_ge(s.product, s.n.product + t + 1)
                    dve_after(v.tensor_tensor(tmp, bank(2 * (t % 2), 2), MROW[:, 0 if t < LT else 1, :], ALU.mult))
                    last = v.tensor_tensor(H[:, t, :], H[:, t, :], tmp, ALU.add)
                    dve_after(last)
                    v.engine_nop().then_inc(s.added, 1)

            def route(l, tiles):
                s = rt[l]
                lg, af, small = xr(7200, TT, E), xr(7300, TT, 48), STAT[:, 0:16]
                affT, work = xr(7600, LAT), xr(8120, 64)
                idx = xr(8190, 64).bitcast(U32)
                dve_after(v.memset(af[:, 0:tiles], 0.0))
                dve_after(v.memset(affT[0:48], -1.0))
                dve.wait_ge(s.logits, s.n.logits + 1)
                ps = bank(4)[:, 0:tiles * E].rearrange("p (t e) -> p t e", e=E)
                dve_after(v.tensor_reduce(small[:, 0:tiles], ps, X_AXIS, ALU.max))
                v.tensor_tensor(lg[:, 0:tiles], ps, small[:, 0:tiles].unsqueeze(2).to_broadcast([P, tiles, E]),
                                ALU.subtract).then_inc(s.shifted, 1)
                dve.wait_ge(s.exps, s.n.exps + 1)
                dve_after(v.tensor_reduce(small[:, 0:tiles], lg[:, 0:tiles], X_AXIS, ALU.add))
                dve_after(v.reciprocal(small[:, 8:8 + tiles], small[:, 0:tiles]))
                for lo, hi, at in ((0, LT, 0), (LT, tiles, 32))[:1 if tiles == LT else 2]:
                    last = v.tensor_tensor(af[:, lo:hi, at:at + E], lg[:, lo:hi],
                                           small[:, 8 + lo:8 + hi].unsqueeze(2).to_broadcast([P, hi - lo, E]), ALU.mult)
                    dve_after(last)
                v.engine_nop().then_inc(s.aff, 1)
                dve.wait_ge(s.turned, s.n.turned + 1)
                dve_after(v.tensor_copy(affT[0:E, :], bank(5)[0:E, :]))
                if tiles > LT:
                    dve_after(v.tensor_copy(affT[32:48, 0:CTX], bank(6)[32:48, 0:CTX]))
                for r in range(CAP_L // 8):
                    g8 = work[0:48, r * 8:(r + 1) * 8]
                    dve_after(v.max(g8, affT[0:48]))
                    dve_after(v.max_index(idx[0:48, r * 8:(r + 1) * 8], g8, affT[0:48]))
                    dve_after(v.match_replace(affT[0:48], g8, affT[0:48], -2.0))
                    if r == CAP_L // 8 - 2:
                        ada(("route", l, 2))
                pack = STAT[0:E, 96:288]
                dve_after(v.tensor_copy(pack[:, 0:CAP_L], idx[0:E, :]))
                dve_after(v.tensor_copy(pack[:, 96:96 + CAP_L], work[0:E, :]))
                if tiles > LT:
                    dve_after(v.tensor_scalar(pack[:, CAP_L:96], idx[32:48, 0:CAP_C], float(LAT), None, ALU.add))
                    dve_after(v.tensor_copy(pack[:, 96 + CAP_L:192], work[32:48, 0:CAP_C]))
                v.engine_nop().then_inc(s.packed, 1)
                dve.wait_ge(s.routed, s.n.routed + 1)
                n = NSLOT[l]
                dve_after(v.memset(IDXT[:, :], 0))
                dve_after(v.tensor_copy(IDXT[0:n, 0:E], bank(4)[0:n, 128:128 + E]))
                dve_after(v.tensor_copy(GATET[0:n, :], bank(4)[0:n, 128 + E:128 + 2 * E]))

            def experts(l):
                s, n = moe[l], NSLOT[l]
                XT, HID = xr(3072, KD, NPAD), xr(3840, D)
                SIL, Y = xr(4864, D), xr(5888, D)
                if n < NPAD:
                    dve_after(v.memset(Y[:, 0:KD * (NPAD - n)], 0.0))
                    zeros = Y[:, 0:KD * (NPAD - n)].rearrange("p (k t) -> p k t", k=KD)
                    v.tensor_copy(XT[:, :, n:], zeros)
                    for part in range(2):
                        dve_after(v.tensor_copy(HSPLIT[:, part, :, n:], zeros))
                v.engine_nop().then_inc(s.padded, 1)

                def modulate(e):
                    dve.wait_ge(s.x_turned, s.n.x_turned + e + 1)
                    for k in range(4, KD):
                        b = bank(7)[:, (k - 4) * P:(k - 4) * P + n]
                        for st, lo, hi in ((0, 0, CAP_L), (1, CAP_L, n))[:1 if n == CAP_L else 2]:
                            last = v.tensor_scalar(XT[:, k, lo:hi], b[:, lo:hi], ACOL[:, l, 1, k, st:st + 1],
                                                   MCOL[:, l, 3 * KD + k, st:st + 1], ALU.mult, ALU.add)
                    last.then_inc(s.xt_dve, 1)

                def lower_rows(e):
                    dve.wait_ge(s.xt_high, s.n.xt_high + e + 1)
                    v.tensor_tensor(XSPLIT[:, 1], XT, XSPLIT[:, 0].bitcast(F32), ALU.subtract).then_inc(s.xt_low, 1)

                def lower_hidden(e):
                    dve.wait_ge(s.ht_high, s.n.ht_high + e + 1)
                    v.tensor_tensor(HSPLIT[:, 1, :, 0:n], bank(6, 2).rearrange("p (k t) -> p k t", t=P)[:, :, 0:n],
                                    HSPLIT[:, 0, :, 0:n].bitcast(F32), ALU.subtract).then_inc(s.ht_low, 1)

                def weigh(e):
                    dve.wait_ge(s.routes, s.n.routes + e + 1)
                    dve.wait_ge(s.used, s.n.used + first_slice(e + 2))
                    v.scalar_tensor_tensor(out=Y[0:n], in0=bank(4, 2)[0:n], scalar=GCUR[0:n, :], in1=MROW[0:n, 0, :],
                                           op0=ALU.mult, op1=ALU.mult).then_inc(s.weighed, 1)

                def step(e):
                    first, final = isinstance(e, int) and e == 0, isinstance(e, int) and e == E
                    second = isinstance(e, int) and e == 1
                    if final:
                        lower_hidden(e - 1)
                        weigh(e - 2)
                    for i, sl, k, _ in slices(e):
                        dve.wait_ge(s.high, s.n.high + first_slice(e) + i + 1)
                        w = WSPLIT[:, buffer_of(e, i)]
                        v.tensor_tensor(w[:, 1], RING[:, sl, k * D:(k + 1) * D], w[:, 0].bitcast(F32), ALU.subtract
                                        ).then_inc(slot_free[sl] if k == 3 else s.low, 1)
                        if first and i == WBUF - 1:
                            modulate(0)
                            lower_rows(0)
                        if i == 3 and not first and not final:
                            lower_hidden(e - 1)
                            if not second:
                                weigh(e - 2)
                        if i == 11:
                            modulate(e + 1)
                        if i == (GU - 1 if first else GU + 2):
                            dve.wait_ge(s.silu, s.n.silu + e + 1)
                            dve.wait_ge(s.used, s.n.used + first_slice(e) + GU)
                            v.tensor_tensor(HID[0:n], SIL[0:n], bank(2, 2)[0:n], ALU.mult).then_inc(s.hidden, 1)
                            lower_rows(e + 1)

                dve.wait_ge(rt[l].gate_act, rt[l].n.gate_act + 1)
                step(0)
                step(1)
                with dve.Fori(2, E) as e:
                    step(e)
                step(E)
                weigh(E - 1)

            dve.wait_ge(cond_exp, 1)
            cv = VCOL[:, 0, 64:80].rearrange("p (w k) -> p k w", w=2)
            dve_after(v.tensor_scalar(SCT[:, 1], SCT[:, 0], 1.0, None, ALU.add))
            dve_after(v.reciprocal(SCT[:, 0], SCT[:, 1]))
            v.tensor_tensor(SC[:, :, :], SCT[:, 0], cv, ALU.mult).then_inc(cond_ready, 1)
            dve.wait_ge(consts_loaded, ACT_CONSTS)
            for i in range(6):
                ada((0, i))
            dve.wait_ge(small_loaded, POOL_CONSTS)
            v.tensor_scalar(GA[:, 0, :], GA[:, 0, :], HD ** -0.5, None, ALU.mult)
            v.tensor_scalar(GB[:, 0:1], GB[:, 0:1], HD ** -0.5, None, ALU.mult)
            end(dve, "dve")
            begin(dve, "dve", 1)
            norm(0, 0, TT)
            end(dve, "dve")
            begin(dve, "dve", 2)
            for u, (c, t) in enumerate([(c, t) for c in range(5) for t in range(TT)]):
                if c == 4:
                    dve.wait_ge(prj.product, u + 1)
                    v.engine_nop().then_inc(prj.scaled, 1)
                    ada((2, u))
                    continue
                ps = bank(u % 4)
                ph = PH[:, 24 * (u % 2):24 * (u % 2) + 24]
                dve.wait_ge(prj.squares, u + 1)
                dve_after(v.tensor_reduce(ph[:, 0:8], SQ[:, u % 2, :].rearrange("p (h d) -> p h d", d=HD), X_AXIS, ALU.add))
                dve_after(v.tensor_scalar(ph[:, 8:16], ph[:, 0:8], 1.0 / HD, EPS, ALU.mult, ALU.add))
                v.reciprocal(ph[:, 16:24], ph[:, 8:16]).then_inc(prj.inverse, 1)
                dve.wait_ge(prj.rstd, u + 1)
                if u >= 2:
                    dve.wait_ge(prj.turned, u - 1)
                st = STAGE[:, u % 2, :]
                last = v.tensor_tensor(st.rearrange("p (h d) -> p h d", d=HD), ps.rearrange("p (h d) -> p h d", d=HD),
                                       ph[:, 0:8].unsqueeze(2).to_broadcast([P, 8, HD]), ALU.mult)
                last.then_inc(prj.scaled, 1)
                dve.wait_ge(prj.scaled, u + 1)
                if c < 2:
                    nh = 8 if c == 0 else 2
                    a = st[:, 0:nh * HD]
                    dve_after(v.tensor_tensor(a.rearrange("p (h d) -> p h d", d=HD), a.rearrange("p (h d) -> p h d", d=HD),
                                              GA[:, c, :].unsqueeze(1).to_broadcast([P, nh, HD]), ALU.mult))
                    if c == 0:
                        dst = STAGE2[:, u % 2, :].rearrange("p (j a d) -> p a j d", j=4, a=2)
                    else:
                        dst = STAGE2[:, u % 2, 0:nh * HD].rearrange("p (j a d) -> p a j d", j=1, a=2)
                    if t < LT:
                        cos = CONST[:, C_ROPE + t * P:C_ROPE + t * P + HD]
                        sin = CONST[:, C_ROPE + t * P + HD:C_ROPE + (t + 1) * P].rearrange("p (g s i) -> p g s i", g=2, s=2)
                        src4 = a.rearrange("p (h g s i) -> p (h g) s i", g=2, s=2, i=16)
                        rot4 = ROT[:, 0:nh * HD].rearrange("p (h g s i) -> p (h g) s i", g=2, s=2, i=16)
                        for g in range(2):
                            for sd in range(2):
                                dve_after(v.tensor_tensor(
                                    rot4[:, g::2, sd, :], src4[:, g::2, 1 - sd, :],
                                    sin[:, g, sd, :].unsqueeze(1).to_broadcast([P, nh, 16]), ALU.mult))
                        dve_after(v.tensor_tensor(a.rearrange("p (h d) -> p h d", d=HD), a.rearrange("p (h d) -> p h d", d=HD),
                                                  cos.unsqueeze(1).to_broadcast([P, nh, HD]), ALU.mult))
                        for aa in range(2):
                            hh = nh // 2
                            dve_after(v.tensor_tensor(
                                dst[:, aa], a[:, aa * hh * HD:(aa + 1) * hh * HD].rearrange("p (j d) -> p j d", d=HD),
                                ROT[:, aa * hh * HD:(aa + 1) * hh * HD].rearrange("p (j d) -> p j d", d=HD), ALU.add))
                    else:
                        for aa in range(2):
                            hh = nh // 2
                            dve_after(v.tensor_copy(dst[:, aa], a[:, aa * hh * HD:(aa + 1) * hh * HD].rearrange("p (j d) -> p j d", d=HD)))
                    if c == 1:
                        dve_after(v.tensor_copy(STAGE2[:, u % 2, 256:512], st[:, 256:512]))
                v.engine_nop().then_inc(prj.stage, 1)
                ada((2, u))
            end(dve, "dve")
            begin(dve, "dve", 3)
            def softmax(first, N):
                nbias = 0
                for i in range(first, N + 3):
                    if i < N:
                        u = heads[i]
                        b0 = 2 * (i % 2)
                        dve.wait_ge(att.scores, i + 1)
                        sc = bank(b0, 2)[:, (0 if u.t < LT else LAT):TOK]
                        if u.biased:
                            nbias += 1
                            lo = (u.head * NSH + (ROWS - 2 - 2 * u.t)) * GRID_W
                            v.tensor_tensor(bank(b0), bank(b0), BIAS[:, lo:lo + LAT], ALU.add).then_inc(att.biased, 1)
                            dve.wait_ge(att.biased, nbias)
                        dve_after(v.tensor_reduce(SM[:, i % 3:i % 3 + 1], sc, X_AXIS, ALU.max))
                        if i >= 3:
                            dve.wait_ge(att.probs, i - 2)
                        v.tensor_scalar(SM[:, 3 + i % 3:4 + i % 3], SM[:, i % 3:i % 3 + 1], -1.0, None, ALU.mult
                                        ).then_inc(att.negmax, 1)
                    j = i - 1
                    if first <= j < N:
                        u = heads[j]
                        dve.wait_ge(att.probs, j + 1)
                        dve_after(v.reciprocal(SM[:, 9:10], SM[:, 6 + j % 3:7 + j % 3]))
                        pr = PROB[:, j % 3, (0 if u.t < LT else LAT):TOK]
                        v.tensor_scalar(pr, pr, SM[:, 9:10], None, ALU.mult).then_inc(att.normal, 1)
                        dve.wait_ge(att.normal, j + 1)
                    if i < N:
                        ada((3, i))
                    j = i - 2
                    if first <= j < N:
                        dve.wait_ge(att.turned, j + 1)
                        if j >= 2:
                            dve.wait_ge(att.mixed, j - 1)
                        v.tensor_copy(PROBT[:, j % 2, LAT:TOK], bank(5)[:, 0:CTX]).then_inc(att.evac_dve, 1)

            softmax(0, N_A)
            for i in range(0, BIAS_N, 2):
                dve.wait_ge(bias_flipped, i + 1)
                v.tensor_copy(BIAS[:, i * BW:(i + 1) * BW], bank(i % 4)).then_inc(bias_evac_dve, 1)
            dve.wait_ge(bias_evac_act, BIAS_N // 2)
            dve.wait_ge(bias_evac_dve, BIAS_N // 2)
            softmax(N_A, len(heads))
            end(dve, "dve")
            begin(dve, "dve", 4)
            residual(0, TT)
            end(dve, "dve")
            begin(dve, "dve", 5)
            norm(0, 1, TT)
            route(0, TT)
            end(dve, "dve")
            begin(dve, "dve", 6)
            experts(0)
            end(dve, "dve")
            begin(dve, "dve", 7)
            end(dve, "dve")
            begin(dve, "dve", 8)
            norm(1, 0, TT)
            end(dve, "dve")
            begin(dve, "dve", 9)
            GTMP = xr(9216, TOK)
            for i, (d, j) in enumerate(gates):
                dve.wait_ge(gp.gate_abs, i + 1)
                bcol = VCOL[:, 1, 80 + 4 * d + j:81 + 4 * d + j]
                v.tensor_scalar(GTMP, bank(4 + 2 * (i % 2), 2)[:, 0:TOK], bcol, 0.0, ALU.add, ALU.min).then_inc(gp.gate_x, 1)
                dve.wait_ge(gp.gate_ln, i + 1)
                dve.wait_ge(gp.gate_x, i + 1)
                dve_after(v.tensor_tensor(GTMP, GTMP, GLN, ALU.subtract))
                cum = CUM[d][:, j, :]
                for lo, hi, m in ((0, LAT, CONST[:, C_RESET:C_RESET + LAT]), (LAT, TOK, CONST[:, C_RESET + 1:C_RESET + 2].to_broadcast([P, CTX]))):
                    o, g = cum[:, lo:hi], GTMP[:, lo:hi]
                    if d:
                        o, g = o[:, ::-1], g[:, ::-1]
                    last = v.tensor_tensor_scan(o, m, g, 0.0, ALU.mult, ALU.add)
                dve_after(last)
                v.engine_nop().then_inc(gp.cum, 1)
            end(dve, "dve")
            begin(dve, "dve", 10)
            for d in range(2):
                dve_after(v.memset(lanes[d].QZ, 0.0))
                dve_after(v.memset(lanes[d].AT, 0.0))
            for h in range(G_H):
                for d in range(2):
                    L = lanes[d]
                    n = 2 * h + d
                    cum = CUM[d][:, h, :]
                    edge = CHUNK - 1 if d == 0 else 0
                    dve.wait_ge(gs.e_pos, n + 1)
                    if h:
                        dve.wait_ge(gs.o_done, lane_o(h - 1, d, LT - 1))
                    e4 = L.TMP[:, 0:LAT].rearrange("p (t x) -> p t x", x=P)
                    q4 = GQ[:, h, :].rearrange("p (t x) -> p t x", x=P)
                    qz4 = L.QZ.rearrange("p (t e x) -> p t e x", e=2, x=P)
                    dve_after(v.tensor_copy(L.DEC, L.TMP[:, edge:LAT:CHUNK]))
                    for eo in range(2):
                        sl = slice(eo * CHUNK, (eo + 1) * CHUNK)
                        last = v.tensor_tensor(qz4[:, :, eo, sl], q4[:, :, sl], e4[:, :, sl], ALU.mult)
                        dve_after(last)
                    v.engine_nop().then_inc(gs.qdec, 1)
                    c3 = cum[:, 0:LAT].rearrange("p (c x) -> p c x", x=CHUNK)
                    dve_after(v.tensor_tensor(L.TMP[:, 0:LAT].rearrange("p (c x) -> p c x", x=CHUNK),
                                              c3[:, :, edge:edge + 1].to_broadcast([P, LAT // CHUNK, CHUNK]), c3, ALU.subtract))
                    cx = LAT + (CTX - 1 if d == 0 else 0)
                    v.tensor_tensor(L.TMP[:, LAT:TOK], cum[:, cx:cx + 1].to_broadcast([P, CTX]), cum[:, LAT:TOK],
                                    ALU.subtract).then_inc(gs.diff, 1)
                    dve.wait_ge(gs.e_neg, n + 1)
                    v.tensor_tensor(L.KI, L.KI, GK[:, h, 0:LAT], ALU.mult).then_inc(gs.kinv, 1)
                    dve.wait_ge(gs.e_diff, n + 1)
                    v.tensor_tensor(L.KS, L.TMP, GK[:, h, :], ALU.mult).then_inc(gs.kst, 1)
                for d in range(2):
                    L = lanes[d]
                    n = 2 * h + d
                    dve.wait_ge(gs.s0, n + 1)
                    v.tensor_copy(L.S[:, 0, :], bank(4 * d + 2)[:, 0:G_DV]).then_inc(gs.s0_out, 1)
                    dve.wait_ge(gs.a_done, n + 1)
                    m = CONST[:, (C_MASKF, C_MASKB)[d]:(C_MASKF, C_MASKB)[d] + P].bitcast(U32)
                    for t in range(LT):
                        last = v.copy_predicated(L.AT[:, t * P:(t + 1) * P], m, bank(4 * d)[:, t * P:(t + 1) * P])
                        dve_after(last)
                    v.engine_nop().then_inc(gs.a_out, 1)
                for i in range(2 * LT):
                    for d in range(2):
                        L = lanes[d]
                        if i < 2 * LT - 1:
                            c = i if d == 0 else 2 * LT - 1 - i
                            dve.wait_ge(gs.upd, lane_state(h, d, i))
                            if i == 0:
                                dve.wait_ge(gs.s0_out, 2 * h + d + 1)
                            else:
                                dve.wait_ge(gs.state, lane_state(h, d, i - 1))
                            v.scalar_tensor_tensor(out=L.S[:, (i + 1) % 2, :], in0=L.S[:, i % 2, :],
                                                   scalar=L.DEC[:, c:c + 1], in1=bank(4 * d + 2)[:, 256:512],
                                                   op0=ALU.mult, op1=ALU.add).then_inc(gs.state, 1)
                        if i % 2:
                            t = (i // 2) if d == 0 else LT - 1 - i // 2
                            ob = bank(4 * d + 1 + 2 * ((i // 2) % 2))[:, 0:G_DV]
                            o = GO[:, t, h * G_DV:(h + 1) * G_DV]
                            k = lane_o(h, d, i // 2)
                            dve.wait_ge(gs.o_done, k)
                            first = (i < LT)
                            if first:
                                v.tensor_copy(o, ob).then_inc(gs.o_out, 1)
                            else:
                                dve.wait_ge(gs.o_out, k - 1)
                                v.tensor_tensor(o, o, ob, ALU.add).then_inc(gs.o_out, 1)
            end(dve, "dve")
            begin(dve, "dve", 11)
            st = STAT[:, 0:48]
            dve.wait_ge(mg.squares, LT * G_H)
            dve_after(v.tensor_scalar(st[:, 16:32], st[:, 0:16], 1.0 / G_DV, EPS, ALU.mult, ALU.add))
            v.reciprocal(st[:, 32:48], st[:, 16:32]).then_inc(mg.inverse, 1)
            dve.wait_ge(mg.rstd, 1)
            for t in range(LT):
                for h in range(G_H):
                    o = GO[:, t, h * G_DV:(h + 1) * G_DV]
                    last = v.scalar_tensor_tensor(out=o, in0=o, scalar=st[:, 4 * t + h:4 * t + h + 1],
                                                  in1=OG[:, t, h * G_DV:(h + 1) * G_DV], op0=ALU.mult, op1=ALU.mult)
                last.then_inc(mg.scaled, 1)
            end(dve, "dve")
            begin(dve, "dve", 12)
            residual(1, LT)
            end(dve, "dve")
            begin(dve, "dve", 13)
            norm(1, 1, LT)
            route(1, LT)
            end(dve, "dve")
            begin(dve, "dve", 14)
            experts(1)
            end(dve, "dve")

        @block.scalar
        def _(act):
            a = nc.scalar.activation

            def ada(where):
                for what, l, i in ada_at.get(where, ()):
                    if what == "chunk":
                        act.wait_ge(ada_s.product, 12 * l + i + 1)
                        if i % 2 == 0 and (l, i) != (0, 0):
                            act.wait_ge(ada_s.turned, 6 * l + i // 2)
                        a(ADA_ROWS[:, (i % 2) * BW:(i % 2 + 1) * BW], bank(7)[0:2, :], ACT.Copy).then_inc(ada_s.rows, 1)

            def squares(l, w, tiles, updated):
                for t in range(tiles):
                    if w == 0:
                        act.wait_ge((updated.readback0, updated.readback1)[t // (TT // 2)], 16)
                    else:
                        act.wait_ge(updated.added, updated.n.added + t + 1)
                    act_after(a(sq_junk, H[:, t, :], ACT.Square, accum_out=STAT[:, 304 + t:305 + t]))
                    act.drain().then_inc(norm_s[(l, w)].sumsq, 1)

            def norm(l, w, tiles):
                s = norm_s[(l, w)]
                act.wait_ge(s.inverse, s.n.inverse + 1)
                a(MSR[:, 0:tiles], STAT[:, 8:8 + tiles], ACT.Sqrt).then_inc(s.rstd, 1)
                for u in range(tiles):
                    act.wait_ge(s.turned, s.n.turned + u + 1)
                    st = 0 if u < LT else 1
                    for k in range(4):
                        last = a(UT[:, k, u * P:(u + 1) * P], bank(2 * (u % 2))[:, k * P:(k + 1) * P], ACT.Identity,
                                 bias=MCOL[:, l, 3 * w * KD + k, st:st + 1], scale=ACOL[:, l, w, k, st:st + 1])
                    last.then_inc(s.evac_act, 1)

            def experts(l):
                s, n = moe[l], NSLOT[l]
                XT, SIL = xr(3072, KD, NPAD), xr(4864, D)

                def modulate(e):
                    act.wait_ge(s.x_turned, s.n.x_turned + e + 1)
                    for k in range(4):
                        b = bank(6)[:, k * P:k * P + n]
                        for st, lo, hi in ((0, 0, CAP_L), (1, CAP_L, n))[:1 if n == CAP_L else 2]:
                            last = a(XT[:, k, lo:hi], b[:, lo:hi], ACT.Identity, bias=MCOL[:, l, 3 * KD + k, st:st + 1],
                                     scale=ACOL[:, l, 1, k, st:st + 1])
                    last.then_inc(s.xt_act, 1)

                def higher_rows(e):
                    act.wait_ge(s.xt_act, s.n.xt_act + e + 1)
                    act.wait_ge(s.xt_dve, s.n.xt_dve + e + 1)
                    a(XSPLIT[:, 0], XT, ACT.Copy).then_inc(s.xt_high, 1)

                def higher_hidden(e):
                    act.wait_ge(s.h_turned, s.n.h_turned + e + 1)
                    a(HSPLIT[:, 0, :, 0:n], bank(6, 2).rearrange("p (k t) -> p k t", t=P)[:, :, 0:n], ACT.Copy
                      ).then_inc(s.ht_high, 1)

                def step(e):
                    first, final = isinstance(e, int) and e == 0, isinstance(e, int) and e == E
                    if final:
                        higher_hidden(e - 1)
                    for i, sl, k, owner in slices(e):
                        if k == 0:
                            act.wait_ge(slot_full[sl], (owner + place[("moe", l, 0, sl)][1] + 1) * 16)
                        if not first or i >= WBUF:
                            act.wait_ge(s.used, s.n.used + first_slice(e) + i + 1 - WBUF)
                        a(WSPLIT[:, buffer_of(e, i), 0], RING[:, sl, k * D:(k + 1) * D], ACT.Copy).then_inc(s.high, 1)
                        if first and i == WBUF - 1:
                            modulate(0)
                            if n < NPAD:
                                act.wait_ge(s.padded, s.n.padded + 1)
                            higher_rows(0)
                        if i == 3 and not first and not final:
                            higher_hidden(e - 1)
                        if i == 10:
                            act.wait_ge(s.used, s.n.used + first_slice(e) + GU // 2)
                            if not first:
                                act.wait_ge(s.hidden, s.n.hidden + e)
                            a(SIL[0:n], bank(0, 2)[0:n], ACT.Silu).then_inc(s.silu, 1)
                        if i == 11:
                            modulate(e + 1)
                        if i == (GU - 1 if first else GU + 2):
                            act.wait_ge(s.used, s.n.used + first_slice(e) + GU)
                            higher_rows(e + 1)

                step(0)
                step(1)
                with act.Fori(2, E) as e:
                    step(e)
                step(E)

            def vectors(eng, l, what):
                for at, src in what:
                    n = int(np.prod(src.shape)) // D
                    eng.dma_start(VCOL[:, l, at:at + KD * n].rearrange("p (v k) -> p v k", k=KD),
                                  src.rearrange("(v p k) -> p v k", p=P, k=KD)).then_inc(
                                      vec_loaded if at >= 64 else consts_loaded, 16)

            vectors(act, 0, ((64, A["c"][0]), (72, A["c_ctx"])))
            act.dma_start(CONST[:, :], A["shape_constants"]).then_inc(consts_loaded, 16)
            vectors(act, 0, ((48, A["norm1_g"][0]), (0, A["ada_b"][0]), (56, A["norm2_g"][0])))
            act.wait_ge(vec_loaded, 32)
            a(SCT[:, 0], VCOL[:, 0, 64:80].rearrange("p (w k) -> p k w", w=2), ACT.Exp, scale=-1.0).then_inc(cond_exp, 1)
            for i in range(6):
                ada((0, i))
                if i == 3:
                    act.wait_ge(h_loaded, 32)
                    for t in range(TT):
                        act_after(a(sq_junk, H[:, t, :], ACT.Square, accum_out=STAT[:, 304 + t:305 + t]))
                        act.drain().then_inc(norm_s[(0, 0)].sumsq, 1)
            end(act, "act")
            begin(act, "act", 1)
            norm(0, 0, TT)
            end(act, "act")
            begin(act, "act", 2)
            act_units = [(c, t) for c in range(5) for t in range(TT)]

            def evac_heads(u):
                c, t = act_units[u]
                if c == 4:
                    return
                act.wait_ge(prj.turned, u + 1)
                b = bank(4 + u % 2)
                tok = slice(t * P, (t + 1) * P)
                for i, (col, num, dst, gain) in enumerate((
                        ((0, 4, 0, None),), ((0, 1, 4, None), (2, 2, 5, 0)), ((0, 2, 7, 0), (2, 2, 9, 1)), ((0, 2, 11, 1),))[c]):
                    src = b[:, col * P:(col + num) * P].rearrange("p (j x) -> p j x", x=P)
                    if gain is None:
                        last = a(qk(dst, num)[:, :, tok], src, ACT.Copy)
                    else:
                        last = a(qk(dst, num)[:, :, tok], src, ACT.Copy, scale=GB[:, gain:gain + 1])
                last.then_inc(prj.evac, 1)

            for u, (c, t) in enumerate(act_units):
                b = bank(u % 4)
                act.wait_ge(prj.product, u + 1)
                if c < 4:
                    if u >= 2:
                        act.wait_ge(prj.scaled, u - 1)
                    a(SQ[:, u % 2, :], b, ACT.Square).then_inc(prj.squares, 1)
                if c == 1:
                    a(V[:, t, 0:P], b[:, P:2 * P], ACT.Copy).then_inc(prj.v_out, 1)
                elif c == 3:
                    a(V[:, t, P:P + 256], b[:, 256:512], ACT.Copy).then_inc(prj.v_out, 1)
                elif c == 4:
                    a(V[:, t, P + 256:P + 512], b[:, 0:256], ACT.Copy).then_inc(prj.v_out, 1)
                else:
                    act.drain().then_inc(prj.v_out, 1)
                if c < 4:
                    act.wait_ge(prj.inverse, u + 1)
                    ph = PH[:, 24 * (u % 2):24 * (u % 2) + 24]
                    a(ph[:, 0:8], ph[:, 16:24], ACT.Sqrt).then_inc(prj.rstd, 1)
                if u:
                    evac_heads(u - 1)
                ada((2, u))
            end(act, "act")
            begin(act, "act", 3)
            def exponentials(first, N):
                for i in range(first, N + 3):
                    if i < N:
                        u = heads[i]
                        lo = 0 if u.t < LT else LAT
                        act.wait_ge(att.negmax, i + 1)
                        if i >= 3:
                            act.wait_ge(att.turned, i - 2)
                        a(PROB[:, i % 3, lo:TOK], bank(2 * (i % 2), 2)[:, lo:TOK], ACT.Exp, bias=SM[:, 3 + i % 3:4 + i % 3],
                          accum_out=SM[:, 6 + i % 3:7 + i % 3]).then_inc(att.probs, 1)
                        ada((3, i))
                    j = i - 2
                    if first <= j < N:
                        act.wait_ge(att.turned, j + 1)
                        if j >= 2:
                            act.wait_ge(att.mixed, j - 1)
                        if heads[j].t < LT:
                            a(PROBT[:, j % 2, 0:LAT], bank(4), ACT.Copy).then_inc(att.evac_act, 1)
                        else:
                            act.drain().then_inc(att.evac_act, 1)
                    j = i - 3
                    if first <= j < N:
                        u = heads[j]
                        act.wait_ge(att.mixed, j + 1)
                        a(UT[u.base:u.base + HD, u.mix, u.t * P:(u.t + 1) * P], bank(6)[u.base:u.base + HD, 0:P],
                          ACT.Copy).then_inc(att.evac_mix, 1)

            exponentials(0, N_A)
            for i in range(1, BIAS_N, 2):
                act.wait_ge(bias_flipped, i + 1)
                a(BIAS[:, i * BW:(i + 1) * BW], bank(i % 4), ACT.Copy).then_inc(bias_evac_act, 1)
            exponentials(N_A, len(heads))
            end(act, "act")
            begin(act, "act", 4)
            act.wait_ge(outp[0].gate_turned, 1)
            a(by_slice(MROW[:, 0, :]), bank(4, 2).rearrange("p (k x) -> p k x", k=KD), ACT.Copy).then_inc(outp[0].gate_act, 1)
            squares(0, 1, TT, outp[0])
            end(act, "act")

            def route(l, tiles):
                s = rt[l]
                lg = xr(7200, TT, E)[:, 0:tiles]
                act.wait_ge(s.shifted, s.n.shifted + 1)
                a(lg, lg, ACT.Exp).then_inc(s.exps, 1)
                if l == 1:
                    for i in range(2):
                        ada(("route", l, i))
                act.wait_ge(s.gate_turned, s.n.gate_turned + 1)
                for w, lo, hi in ((0, 0, CAP_L), (1, CAP_L, NPAD)):
                    act_after(a(by_slice(MROW[lo:hi, 0, :]), bank(2 * w, 2)[lo:hi].rearrange("p (k x) -> p k x", k=KD), ACT.Copy))
                act.drain().then_inc(s.gate_act, 1)
                if l == 0:
                    for i in range(2):
                        ada(("route", l, i))

            begin(act, "act", 5)
            norm(0, 1, TT)
            route(0, TT)
            end(act, "act")
            begin(act, "act", 6)
            experts(0)
            squares(1, 0, TT, moe[0])
            end(act, "act")
            begin(act, "act", 7)
            end(act, "act")
            begin(act, "act", 8)
            norm(1, 0, TT)
            end(act, "act")
            begin(act, "act", 9)
            n_out = 0

            def out_bank():
                act.wait_ge(gp.product, n_out + 1)
                return bank(n_out % 4)

            for c in range(2):
                for j in range(G_H):
                    if c == 0:
                        a(GQ[:, j, :], out_bank(), ACT.Copy, scale=G_DK ** -0.5).then_inc(gp.evac_act, 1)
                        n_out += 1
                    else:
                        for lo, hi in ((0, LAT), (LAT, TOK)):
                            a(GK[:, j, lo:hi], out_bank()[:, 0:hi - lo], ACT.Copy).then_inc(gp.evac_act, 1)
                            n_out += 1
            for lo, hi in ((0, LAT), (LAT, TOK)):
                a(ZT[:, lo:hi], out_bank()[0:48, 0:hi - lo], ACT.Copy).then_inc(gp.evac_act, 1)
                n_out += 1

            def gate_smooth(i):
                d, j = gates[i]
                act.wait_ge(gp.raw, i + 1)
                bcol = VCOL[:, 1, 80 + 4 * d + j:81 + 4 * d + j]
                if i:
                    act.wait_ge(gp.cum, i)
                a(GLN, bank(4 + 2 * (i % 2), 2)[:, 0:TOK], ACT.Abs, bias=bcol).then_inc(gp.gate_abs, 1)
                act.wait_ge(gp.gate_abs, i + 1)
                a(GLN, GLN, ACT.Exp, scale=-1.0).then_inc(gp.gate_exp, 1)
                act.wait_ge(gp.gate_exp, i + 1)
                a(GLN, GLN, ACT.Ln, bias=1.0).then_inc(gp.gate_ln, 1)

            for c in range(2, 4):
                for t in range(TT):
                    a(GV[:, t, (c - 2) * BW:(c - 1) * BW], out_bank(), ACT.Copy).then_inc(gp.evac_act, 1)
                    n_out += 1
                    if (c - 2) * TT + t < len(gates):
                        gate_smooth((c - 2) * TT + t)
            for c in range(4, 6):
                for t in range(LT):
                    a(OG[:, t, (c - 4) * BW:(c - 3) * BW], out_bank(), ACT.Silu).then_inc(gp.evac_act, 1)
                    n_out += 1
            end(act, "act")
            begin(act, "act", 10)

            def head_squares(h):
                for t in range(LT):
                    a(xr(9216, G_DV), GO[:, t, h * G_DV:(h + 1) * G_DV], ACT.Square,
                      accum_out=STAT[:, 4 * t + h:4 * t + h + 1]).then_inc(mg.squares, 1)
                    act.wait_ge(mg.squares, LT * h + t + 1)

            for h in range(G_H):
                for d in range(2):
                    L = lanes[d]
                    n = 2 * h + d
                    cum = CUM[d][:, h, :]
                    if h:
                        act.wait_ge(gs.kst, 2 * (h - 1) + d + 1)
                        act.wait_ge(gs.a_done, 2 * (h - 1) + d + 1)
                    a(L.TMP[:, 0:LAT], cum[:, 0:LAT], ACT.Exp, scale=1.0 / 16).then_inc(gs.e_pos, 1)
                    a(L.KI, cum[:, 0:LAT], ACT.Exp, scale=-1.0 / 16).then_inc(gs.e_neg, 1)
                    act.wait_ge(gs.diff, n + 1)
                    a(L.TMP, L.TMP, ACT.Exp, scale=1.0 / 16).then_inc(gs.e_diff, 1)
                for d in range(2):
                    L = lanes[d]
                    act.wait_ge(gs.kturned, 2 * h + d + 1)
                    a(L.KS, bank(4 * d, 2)[:, 0:TOK], ACT.Copy).then_inc(gs.kst_out, 1)
                if h:
                    act.wait_ge(gs.o_out, lane_o(h - 1, 1, LT - 1))
                    head_squares(h - 1)
            end(act, "act")
            begin(act, "act", 11)
            head_squares(G_H - 1)
            act.wait_ge(mg.inverse, 1)
            a(STAT[:, 0:16], STAT[:, 32:48], ACT.Sqrt).then_inc(mg.rstd, 1)
            for t in range(LT):
                act.wait_ge(mg.turned, t + 1)
                for n in range(2):
                    last = a(OT[:, 4 * n:4 * n + 4, t * P:(t + 1) * P],
                             bank(2 * (t % 2) + n).rearrange("p (k x) -> p k x", x=P), ACT.Copy)
                last.then_inc(mg.evac, 1)
            end(act, "act")
            begin(act, "act", 12)
            act.wait_ge(outp[1].gate_turned, 2)
            a(by_slice(MROW[:, 0, :]), bank(4, 2).rearrange("p (k x) -> p k x", k=KD), ACT.Copy).then_inc(outp[1].gate_act, 1)
            squares(1, 1, LT, outp[1])
            end(act, "act")
            begin(act, "act", 13)
            norm(1, 1, LT)
            route(1, LT)
            end(act, "act")
            begin(act, "act", 14)
            experts(1)
            end(act, "act")

        @block.gpsimd
        def _(pool):
            g = nc.gpsimd

            for i, g_ in enumerate(("a_q_norm", "a_k_norm")):
                pool.dma_start(GA[:, i, :], A[g_][0:1, :].to_broadcast([P, HD])).then_inc(small_loaded, 16)
            for i, g_ in enumerate(("b_q_norm", "b_k_norm")):
                for half in range(2):
                    pool.dma_start(GB[half * HD:(half + 1) * HD, i:i + 1],
                                   A[g_].rearrange("a d -> d a")).then_inc(small_loaded, 16)
            for l in range(2):
                pool.dma_start(RW[:, l], A["moe_router"][l].rearrange("(p k) e -> p k e", p=P)).then_inc(small_loaded, 16)
            for at, src in ((48, A["norm1_g"][1]), (0, A["ada_b"][1]), (56, A["norm2_g"][1])):
                n = int(np.prod(src.shape)) // D
                pool.dma_start(VCOL[:, 1, at:at + KD * n].rearrange("p (v k) -> p v k", k=KD),
                               src.rearrange("(v p k) -> p v k", p=P, k=KD)).then_inc(small_loaded, 16)
            for at, src in ((80, A["gla_gk_b_f"]), (84, A["gla_gk_b_b"])):
                pool.dma_start(VCOL[:, 1, at:at + 4], src[0].rearrange("(j p) -> p j", p=P), allow_slow_non_contiguous=True).then_inc(small_loaded, 16)
            pool.dma_start(ONORM[:, :], A["gla_o_norm"][0:1, :].to_broadcast([P, G_DV])).then_inc(small_loaded, 16)
            pool.dma_start(GKW[0:16, :], A["gla_gk_w_f"][0]).then_inc(small_loaded, 16)
            pool.dma_start(GKW[32:48, :], A["gla_gk_w_b"][0]).then_inc(small_loaded, 16)
            n = B_H * DR * DC
            flat = A["na_rpb"][0].rearrange("h a b -> (h a b)")
            pool.dma_start(RPB[96:96 + n], flat).then_inc(bias_copied, 16)
            pool.dma_start(RPB[0:96], flat[0:96]).then_inc(bias_copied, 16)
            pool.dma_start(RPB[96 + n:192 + n], flat[0:96]).then_inc(bias_copied, 16)

            def store_rows(l, tiles):
                s = norm_s[(l, 1)]
                pool.dma_start(ACC[l].rearrange("(t p) d -> p t d", p=P), H[:, 0:tiles, :]).then_inc(moe[l].scattered, 16)
                for t in range(tiles):
                    pool.wait_ge(s.xhat, s.n.xhat + t + 1)
                    pool.dma_start(XH[l][t * P:(t + 1) * P, :], xhat[:, t, :]).then_inc((s.stored0, s.stored1)[t % 2], 16)
                pool.wait_ge(s.stored0, s.n.stored0 + 16 * ((tiles + 1) // 2))
                pool.wait_ge(s.stored1, s.n.stored1 + 16 * (tiles // 2))

            def experts(l):
                s, n = moe[l], NSLOT[l]
                XG, Y = xr(2048, D), xr(5888, D)

                def gather(e):
                    pool.wait_ge(s.x_turned, s.n.x_turned + e)
                    pool.wait_ge(s.gathered, s.n.gathered + e * 16)
                    g.tensor_copy(IDXG[0:n, :], IDXT[0:n, bass.ds(e, 1)]).then_inc(s.idx_next, 1)
                    pool.wait_ge(s.idx_next, s.n.idx_next + e)
                    apart(pool)
                    pool.indirect_dma_start(XG[0:n, :], None, XH[l], bass.IndirectOffsetOnAxis(IDXG[0:n, 0:1], 0)
                                            ).then_inc(s.gathered, 16)

                def scatter(e):
                    pool.wait_ge(s.scattered, s.n.scattered + e * 16 + 16)
                    g.tensor_copy(IDXS[0:n, :], IDXT[0:n, bass.ds(e, 1)])
                    g.tensor_copy(GCUR[0:n, :], GATET[0:n, bass.ds(e, 1)]).then_inc(s.routes, 1)
                    pool.wait_ge(s.routes, s.n.routes + e + 1)
                    pool.wait_ge(s.weighed, s.n.weighed + e + 1)
                    apart(pool)
                    pool.indirect_dma_start(ACC[l], bass.IndirectOffsetOnAxis(IDXS[0:n, 0:1], 0), Y[0:n, :], None,
                                            compute_op=ALU.add).then_inc(s.scattered, 16)

                pool_after(g.tensor_copy(IDXG[0:n, :], IDXT[0:n, 0:1]))
                pool.indirect_dma_start(XG[0:n, :], None, XH[l], bass.IndirectOffsetOnAxis(IDXG[0:n, 0:1], 0)
                                        ).then_inc(s.gathered, 16)
                gather(1)
                pool.wait_ge(s.scattered, s.n.scattered + 16)
                gather(2)
                with pool.Fori(2, E) as e:
                    gather(e + 1)
                    scatter(e - 2)
                for e in (E - 2, E - 1):
                    scatter(e)
                pool.wait_ge(s.scattered, s.n.scattered + 16 * (E + 1))
                pool.wait_ge(s.gathered, s.n.gathered + 16 * (E + 1))
                pool.wait_ge(s.h_turned, s.n.h_turned + E)
                if l == 0:
                    rows, half = ACC[l].rearrange("(t p) d -> p t d", p=P), TT // 2
                    pool.dma_start(H[:, 0:half, :], rows[:, 0:half]).then_inc(s.readback0, 16)
                    pool.dma_start(H[:, half:TT, :], rows[:, half:TT]).then_inc(s.readback1, 16)
                    pool.wait_ge(s.readback0, 16)
                    pool.wait_ge(s.readback1, 16)

            pool_after(g.memset(WZ[:, :, :], 0.0))
            wv = A["gla_w_in"][0].rearrange("(p k) n -> p k n", p=P)
            pool.dma_start(WZ[:, :, 0:16], wv[:, :, 3072:3088]).then_inc(wz_loaded, 16)
            pool.dma_start(WZ[:, :, 32:48], wv[:, :, 3088:3104]).then_inc(wz_loaded, 16)
            pool.wait_ge(wz_loaded, 32)
            end(pool, "pool")
            for n in (1, 2):
                begin(pool, "pool", n)
                end(pool, "pool")
            begin(pool, "pool", 3)
            pool.wait_ge(bias_loaded, 16 * 2 * B_H)
            for half in range(2):
                b = BIAS[half * GRID_W:(half + 1) * GRID_W, :].rearrange("p (s c) -> p s c", c=GRID_W)
                w = GRID_W - NA_COLS
                pool_after(g.affine_select(out=b[:, :, 0:w], in_=b[:, :, 0:w], compare_op=ALU.is_ge, fill=MASKED,
                                           base=NA_COLS // 2 - (GRID_W - 1), pattern=[[0, B_H * NSH], [1, w]], channel_multiplier=1))
                pool_after(g.affine_select(out=b[:, :, NA_COLS:], in_=b[:, :, NA_COLS:], compare_op=ALU.is_ge, fill=MASKED,
                                           base=(GRID_W - 1) + NA_COLS // 2 - 1 - NA_COLS, pattern=[[0, B_H * NSH], [-1, w]],
                                           channel_multiplier=-1))
            pool.drain().then_inc(bias_masked, 1)
            end(pool, "pool")
            begin(pool, "pool", 4)
            end(pool, "pool")
            begin(pool, "pool", 5)
            store_rows(0, TT)
            end(pool, "pool")
            begin(pool, "pool", 6)
            experts(0)
            end(pool, "pool")
            for n in range(7, 13):
                begin(pool, "pool", n)
                if n == 10:
                    for t in range(LT):
                        og = OG[:, t, :].rearrange("p (h e) -> p h e", h=G_H)
                        g.tensor_tensor(og, og, ONORM[:, :].unsqueeze(1).to_broadcast([P, G_H, G_DV]), ALU.mult)
                end(pool, "pool")
            begin(pool, "pool", 13)
            store_rows(1, LT)
            end(pool, "pool")
            begin(pool, "pool", 14)
            experts(1)
            end(pool, "pool")


_INS = ["x", "c", "ctx", "c_ctx", "ada_w", "ada_b", "norm1_g", "norm2_g", "attn_w_in", "attn_w_out",
        "a_q_norm", "a_k_norm", "b_q_norm", "b_k_norm", "na_rpb", "gla_w_in", "gla_gk_w_f", "gla_gk_b_f",
        "gla_gk_w_b", "gla_gk_b_b", "gla_o_norm", "gla_w_out", "moe_router", "moe_w_gate", "moe_w_up", "moe_w_down"]


def kernel(**inputs):
    import numpy as _np
    import concourse.bacc as _bacc
    from concourse import mybir as _mybir
    from concourse.bass_utils import run_bass_kernel_spmd as _run

    nc = _bacc.Bacc("TRN2", target_bir_lowering=False, num_devices=1)
    arrays, args = {}, {}
    for name in _INS:
        a = _np.ascontiguousarray(inputs[name])
        arrays[f"in_{name}"] = a
        args[name] = nc.dram_tensor(f"in_{name}", a.shape, _mybir.dt.from_np(a.dtype), kind="ExternalInput").ap()
    a = shape_constants()
    arrays["in_shape_constants"] = a
    args["shape_constants"] = nc.dram_tensor("in_shape_constants", a.shape, _mybir.dt.from_np(a.dtype),
                                             kind="ExternalInput").ap()
    out = nc.dram_tensor("out_0", (LAT, D), _mybir.dt.float32, kind="ExternalOutput").ap()
    build(nc, args, out)
    r = _run(nc, [arrays], core_ids=[0])
    return r.results[0]["out_0"].reshape(1, LAT, D)
```
